# Optimizing a Trainium2 kernel written in Bass

```python
import jax
import jax.numpy as jnp
from jax import lax
import numpy as np

D_MODEL = 1024
BATCH = 1
SEQ = 256
DEPTH = 2

GRID_W = 64
CTX_LEN = 256
EPS = 1e-6
NEG_INF = -1e30
HEAD_DIM = 64

POOL_WIDTH = D_MODEL // 4
POOL_WINDOWS = (2, 4, 8, 16)
POOL_GROUP = POOL_WIDTH // len(POOL_WINDOWS)

GDN_WIDTH = (3 * D_MODEL) // 8
GDN_HEADS = GDN_WIDTH // HEAD_DIM
GDN_CHUNK = 64
CONV_K = 5

ATTN_WIDTH = D_MODEL - POOL_WIDTH - GDN_WIDTH
ATTN_HEADS = ATTN_WIDTH // HEAD_DIM
KV_HEADS = 2
ATTN_GROUP = ATTN_HEADS // KV_HEADS
KV_WIDTH = KV_HEADS * HEAD_DIM
WINDOW = 128
ATTN_BLOCK = 128
ROPE_BASE = 10000.0
ROPE_PAIRS = HEAD_DIM // 4

IN_SPLITS = (POOL_WIDTH, 3 * GDN_WIDTH, GDN_WIDTH, 4 * GDN_HEADS, ATTN_WIDTH, KV_WIDTH, KV_WIDTH)
IN_WIDTH = POOL_WIDTH + 4 * GDN_WIDTH + 4 * GDN_HEADS + ATTN_WIDTH + 2 * KV_WIDTH

PEER_HEADS = 8
N_KEYS = 128
N_EXPERTS = N_KEYS * N_KEYS
PEER_TOPK = 16
PEER_QDIM = 256
PEER_HALF = PEER_QDIM // 2
PEER_BLOCK = 128

kernel_name = "hybrid_pool_gdn_swa_peer_dit"

def rmsnorm(x, gain):
    xf = x.astype(jnp.float32)
    y = xf * lax.rsqrt(jnp.mean(jnp.square(xf), axis=-1, keepdims=True) + EPS)
    return (y * gain.astype(jnp.float32)).astype(x.dtype)

def l2norm(x):
    return x * lax.rsqrt(jnp.sum(jnp.square(x), axis=-1, keepdims=True) + EPS)

def split_cols(p):
    idx, acc = [], 0
    for w in IN_SPLITS[:-1]:
        acc += w
        idx.append(acc)
    return jnp.split(p, idx, axis=-1)

def axial_rope_tables(seq_len):
    rows = seq_len // GRID_W
    r, col = jnp.meshgrid(jnp.arange(rows), jnp.arange(GRID_W), indexing='ij')
    pos = jnp.stack([r.reshape(-1), col.reshape(-1)], axis=-1).astype(jnp.float32)
    inv = jnp.power(ROPE_BASE, -jnp.arange(ROPE_PAIRS, dtype=jnp.float32) / ROPE_PAIRS)
    ang = pos[:, :, None] * inv
    return jnp.cos(ang), jnp.sin(ang)

def apply_rope(x, tables):
    cos, sin = tables
    xf = x.astype(jnp.float32).reshape(x.shape[:-1] + (2, 2, ROPE_PAIRS))
    x1, x2 = xf[..., 0, :], xf[..., 1, :]
    c, s = cos[:, None], sin[:, None]
    out = jnp.stack([x1 * c - x2 * s, x2 * c + x1 * s], axis=-2)
    return out.reshape(x.shape).astype(x.dtype)

def multiscale_pool(a, w_pool, pool_scale):
    L = a.shape[1]
    af = a.astype(jnp.float32)
    cs = jnp.pad(jnp.cumsum(af, axis=1), ((0, 0), (1, 0), (0, 0)))
    t = jnp.arange(L)
    outs = []
    for gi, w in enumerate(POOL_WINDOWS):
        ch = slice(gi * POOL_GROUP, (gi + 1) * POOL_GROUP)
        lo = jnp.clip(t - w // 2, 0, L)
        hi = jnp.clip(t + w - w // 2, 0, L)
        csg = cs[..., ch]
        win_sum = jnp.take(csg, hi, axis=1) - jnp.take(csg, lo, axis=1)
        cnt = (hi - lo).astype(jnp.float32)[None, :, None]
        pooled = win_sum / cnt - af[..., ch]
        outs.append(jnp.einsum('blc,ce->ble', pooled, w_pool[gi].astype(jnp.float32)))
    return (jnp.concatenate(outs, axis=-1) * pool_scale.astype(jnp.float32)).astype(a.dtype)

def short_conv(u, w):
    ch = u.shape[-1]
    y = lax.conv_general_dilated(u, w[:, None, :].astype(u.dtype), window_strides=(1,),
                                 padding=[(CONV_K // 2, CONV_K // 2)],
                                 dimension_numbers=('NWC', 'WIO', 'NWC'), feature_group_count=ch)
    return jax.nn.silu(y)

def gated_delta_chunked(q, k, v, g, beta, state0):
    bn, nh, L, dk = k.shape
    dv = v.shape[-1]
    n = L // GDN_CHUNK
    q = q * (dk ** -0.5)
    rs = lambda t: t.reshape(bn, nh, n, GDN_CHUNK, t.shape[-1])
    qc, kc, vc = rs(q), rs(k), rs(v)
    bc = beta.reshape(bn, nh, n, GDN_CHUNK)
    gc = jnp.cumsum(g.reshape(bn, nh, n, GDN_CHUNK), axis=-1)
    tri = jnp.tril(jnp.ones((GDN_CHUNK, GDN_CHUNK), dtype=bool))
    strict = jnp.tril(jnp.ones((GDN_CHUNK, GDN_CHUNK), dtype=bool), -1)
    diff = gc[..., :, None] - gc[..., None, :]
    decay = jnp.where(tri, jnp.exp(jnp.where(tri, diff, 0.0)), 0.0)
    kb = kc * bc[..., None]
    lower = jnp.where(strict, jnp.einsum('bhnid,bhnjd->bhnij', kb, kc) * decay, 0.0)
    a_mat = lower + jnp.eye(GDN_CHUNK, dtype=jnp.float32)
    rhs = jnp.concatenate([vc * bc[..., None], kb * jnp.exp(gc)[..., None]], axis=-1)
    sol = lax.linalg.triangular_solve(a_mat, rhs, left_side=True, lower=True, unit_diagonal=True)
    u_c, w_c = sol[..., :dv], sol[..., dv:]
    attn_local = jnp.einsum('bhnid,bhnjd->bhnij', qc, kc) * decay
    q_dec = qc * jnp.exp(gc)[..., None]
    k_dec = kc * jnp.exp(gc[..., -1:] - gc)[..., None]
    g_last = jnp.exp(gc[..., -1])

    def step(state, xs):
        u, w, qd, kd, al, gl = xs
        v_new = u - jnp.einsum('bhcd,bhde->bhce', w, state)
        o = jnp.einsum('bhcd,bhde->bhce', qd, state) + jnp.einsum('bhij,bhje->bhie', al, v_new)
        state = state * gl[..., None, None] + jnp.einsum('bhcd,bhce->bhde', kd, v_new)
        return state, o

    xs = tuple(jnp.moveaxis(t, 2, 0) for t in (u_c, w_c, q_dec, k_dec, attn_local, g_last))
    state, o = lax.scan(step, state0, xs)
    o = jnp.moveaxis(o, 0, 2).reshape(bn, nh, L, dv)
    return o, state

def gated_deltanet(qkv_x, z_x, ba_x, qkv_c, z_c, ba_c, conv_w, a_log, dt_bias, out_gain, need_ctx):
    def prep(qkv, ba):
        bn, L, _ = qkv.shape
        y = short_conv(qkv, conv_w).astype(jnp.float32)
        heads = lambda t: t.reshape(bn, L, GDN_HEADS, HEAD_DIM).transpose(0, 2, 1, 3)
        q, k, v = [heads(t) for t in jnp.split(y, 3, axis=-1)]
        ba = ba.astype(jnp.float32).reshape(bn, L, 4, GDN_HEADS).transpose(2, 0, 3, 1)
        beta = jax.nn.sigmoid(ba[:2])
        g = -jnp.exp(a_log.astype(jnp.float32))[:, None, :, None] * jax.nn.softplus(
            ba[2:] + dt_bias.astype(jnp.float32)[:, None, :, None])
        return l2norm(q), l2norm(k), v, beta, g

    def finish(o, z):
        bn, nh, L, d = o.shape
        o = o.transpose(0, 2, 1, 3)
        o = o * lax.rsqrt(jnp.mean(jnp.square(o), axis=-1, keepdims=True) + EPS) * out_gain.astype(jnp.float32)
        return (o.reshape(bn, L, GDN_WIDTH) * jax.nn.silu(z.astype(jnp.float32))).astype(z.dtype)

    qx, kx, vx, beta_x, g_x = prep(qkv_x, ba_x)
    qc, kc, vc, beta_c, g_c = prep(qkv_c, ba_c)
    bn = qx.shape[0]
    outs_x, outs_c = [], []
    for d in range(2):
        fl = (lambda t: jnp.flip(t, axis=2)) if d == 1 else (lambda t: t)
        s0 = jnp.zeros((bn, GDN_HEADS, HEAD_DIM, HEAD_DIM), jnp.float32)
        oc_d, s_ctx = gated_delta_chunked(fl(qc), fl(kc), fl(vc), fl(g_c[d]), fl(beta_c[d]), s0)
        ox_d, _ = gated_delta_chunked(fl(qx), fl(kx), fl(vx), fl(g_x[d]), fl(beta_x[d]), s_ctx)
        outs_x.append(fl(ox_d))
        outs_c.append(fl(oc_d))
    y_x = finish(outs_x[0] + outs_x[1], z_x)
    y_c = finish(outs_c[0] + outs_c[1], z_c) if need_ctx else None
    return y_x, y_c

def window_attention(q_x, k_x, v_x, q_c, k_c, v_c, sink, rope, need_ctx):
    bn, S, _ = q_x.shape
    lc = q_c.shape[1]
    nb = S // ATTN_BLOCK
    nk = 3 * ATTN_BLOCK
    scale = HEAD_DIM ** -0.5
    qx = apply_rope(q_x.reshape(bn, S, ATTN_HEADS, HEAD_DIM), rope)
    kx = apply_rope(k_x.reshape(bn, S, KV_HEADS, HEAD_DIM), rope)
    vx = v_x.reshape(bn, S, KV_HEADS, HEAD_DIM)
    kc = k_c.reshape(bn, lc, KV_HEADS, HEAD_DIM)
    vc = v_c.reshape(bn, lc, KV_HEADS, HEAD_DIM)
    qb = qx.reshape(bn, nb, ATTN_BLOCK, KV_HEADS, ATTN_GROUP, HEAD_DIM)

    def band(t):
        tp = jnp.pad(t, ((0, 0), (ATTN_BLOCK, ATTN_BLOCK), (0, 0), (0, 0)))
        tp = tp.reshape(bn, nb + 2, ATTN_BLOCK, KV_HEADS, HEAD_DIM)
        return jnp.concatenate([tp[:, :-2], tp[:, 1:-1], tp[:, 2:]], axis=2)

    kb, vb = band(kx), band(vx)
    qo = jnp.arange(ATTN_BLOCK)[:, None]
    ko = jnp.arange(nk)[None, :]
    kpos = jnp.arange(nb)[:, None, None] * ATTN_BLOCK - ATTN_BLOCK + ko[None]
    mask = (jnp.abs(ko - ATTN_BLOCK - qo) <= WINDOW)[None] & (kpos >= 0) & (kpos < S)
    s_loc = jnp.einsum('bnqhgd,bnkhd->bnhgqk', qb, kb).astype(jnp.float32) * scale
    s_loc = jnp.where(mask[None, :, None, None], s_loc, NEG_INF)
    s_ctx = jnp.einsum('bnqhgd,bkhd->bnhgqk', qb, kc).astype(jnp.float32) * scale
    sink_h = sink.astype(jnp.float32).reshape(KV_HEADS, ATTN_GROUP, 1, 1)
    sink_l = jnp.broadcast_to(sink_h, s_loc.shape[:-1] + (1,))
    p = jax.nn.softmax(jnp.concatenate([s_loc, s_ctx, sink_l], axis=-1), axis=-1).astype(vx.dtype)
    o = (jnp.einsum('bnhgqk,bnkhd->bnqhgd', p[..., :nk], vb)
         + jnp.einsum('bnhgqk,bkhd->bnqhgd', p[..., nk:nk + lc], vc))
    y_x = o.reshape(bn, S, ATTN_WIDTH)
    if need_ctx:
        qcc = q_c.reshape(bn, lc, KV_HEADS, ATTN_GROUP, HEAD_DIM)
        s = jnp.einsum('bqhgd,bkhd->bhgqk', qcc, kc).astype(jnp.float32) * scale
        sink_c = jnp.broadcast_to(sink_h, s.shape[:-1] + (1,))
        pc = jax.nn.softmax(jnp.concatenate([s, sink_c], axis=-1), axis=-1).astype(vc.dtype)
        y_c = jnp.einsum('bhgqk,bkhd->bqhgd', pc[..., :lc], vc).reshape(bn, lc, ATTN_WIDTH)
    else:
        y_c = None
    return y_x, y_c

def token_mixing(hx, hc, w_in, conv_w, a_log, dt_bias, gdn_norm, w_pool, pool_scale, sink, w_out, rope, need_ctx):
    ax, qkvx, zx, bax, qx, kx, vx = split_cols(hx @ w_in)
    ac, qkvc, zc, bac, qc, kc, vc = split_cols(hc @ w_in)
    ya_x = multiscale_pool(ax, w_pool, pool_scale)
    yb_x, yb_c = gated_deltanet(qkvx, zx, bax, qkvc, zc, bac, conv_w, a_log, dt_bias, gdn_norm, need_ctx)
    yc_x, yc_c = window_attention(qx, kx, vx, qc, kc, vc, sink, rope, need_ctx)
    out_x = jnp.concatenate([ya_x, yb_x, yc_x], axis=-1) @ w_out
    if need_ctx:
        ya_c = multiscale_pool(ac, w_pool, pool_scale)
        out_c = jnp.concatenate([ya_c, yb_c, yc_c], axis=-1) @ w_out
    else:
        out_c = None
    return out_x, out_c

def peer_ffn(h, w_query, sub_keys, u_tab, v_tab):
    bn, L, D = h.shape
    h_blocks = h.reshape(bn * L // PEER_BLOCK, PEER_BLOCK, D)

    def one_block(hb):
        q = (hb @ w_query).reshape(PEER_BLOCK, PEER_HEADS, 2, PEER_HALF)
        s = jnp.einsum('thpd,hpkd->thpk', q, sub_keys).astype(jnp.float32)
        sv, si = lax.top_k(s, PEER_TOPK)
        cand = (sv[:, :, 0, :, None] + sv[:, :, 1, None, :]).reshape(PEER_BLOCK, PEER_HEADS, PEER_TOPK * PEER_TOPK)
        cv, ci = lax.top_k(cand, PEER_TOPK)
        i1 = jnp.take_along_axis(si[:, :, 0], ci // PEER_TOPK, axis=-1)
        i2 = jnp.take_along_axis(si[:, :, 1], ci % PEER_TOPK, axis=-1)
        expert = i1 * N_KEYS + i2
        gate = jax.nn.softmax(cv, axis=-1)
        u = jnp.take(u_tab, expert, axis=0)
        v = jnp.take(v_tab, expert, axis=0)
        act = jax.nn.gelu(jnp.einsum('td,thkd->thk', hb, u).astype(jnp.float32), approximate=False)
        return jnp.einsum('thk,thkd->td', (gate * act).astype(v.dtype), v).astype(h.dtype)

    return lax.map(one_block, h_blocks).reshape(bn, L, D)

def setup_inputs(seed: int = 0) -> dict:
    key = jax.random.key(seed)
    ks = jax.random.split(key, 24)
    f32 = jnp.float32
    nrm = lambda k, shape, s: jax.random.normal(k, shape, f32) * s
    D = D_MODEL
    dt = jnp.exp(jax.random.uniform(ks[11], (DEPTH, 2, GDN_HEADS), f32, np.log(1e-3), np.log(1e-1)))
    return {
        "x": nrm(ks[0], (BATCH, SEQ, D), 1.0),
        "c": nrm(ks[1], (BATCH, D), 1.0),
        "ctx": nrm(ks[2], (BATCH, CTX_LEN, D), 1.0),
        "c_ctx": nrm(ks[3], (D,), 1.0),
        "w_ada": nrm(ks[4], (DEPTH, D, 6 * D), 0.5 * D ** -0.5),
        "b_ada": nrm(ks[5], (DEPTH, 6 * D), 0.02),
        "norm1": 1.0 + nrm(ks[6], (DEPTH, D), 0.02),
        "norm2": 1.0 + nrm(ks[7], (DEPTH, D), 0.02),
        "w_in": nrm(ks[8], (DEPTH, D, IN_WIDTH), D ** -0.5),
        "conv_w": nrm(ks[9], (DEPTH, CONV_K, 3 * GDN_WIDTH), CONV_K ** -0.5),
        "a_log": jnp.log(jax.random.uniform(ks[10], (DEPTH, 2, GDN_HEADS), f32, 1.0, 16.0)),
        "dt_bias": jnp.log(jnp.expm1(dt)),
        "gdn_norm": 1.0 + nrm(ks[12], (DEPTH, HEAD_DIM), 0.02),
        "w_pool": nrm(ks[13], (DEPTH, len(POOL_WINDOWS), POOL_GROUP, POOL_GROUP), POOL_GROUP ** -0.5),
        "pool_scale": 1.0 + nrm(ks[14], (DEPTH, POOL_WIDTH), 0.1),
        "sink": nrm(ks[15], (DEPTH, ATTN_HEADS), 1.0),
        "w_out": nrm(ks[16], (DEPTH, D, D), D ** -0.5),
        "peer_wq": nrm(ks[17], (DEPTH, D, PEER_HEADS * PEER_QDIM), D ** -0.5),
        "peer_keys": nrm(ks[18], (DEPTH, PEER_HEADS, 2, N_KEYS, PEER_HALF), PEER_HALF ** -0.5),
        "peer_u": nrm(ks[19], (DEPTH, N_EXPERTS, D), D ** -0.5),
        "peer_v": nrm(ks[20], (DEPTH, N_EXPERTS, D), 1.0),
        "norm_f": 1.0 + nrm(ks[21], (D,), 0.02),
    }

def reference(x, c, ctx, c_ctx, w_ada, b_ada, norm1, norm2, w_in, conv_w, a_log, dt_bias, gdn_norm,
              w_pool, pool_scale, sink, w_out, peer_wq, peer_keys, peer_u, peer_v, norm_f):
    rope = axial_rope_tables(x.shape[1])
    silu_c = jax.nn.silu(c)
    silu_cc = jax.nn.silu(c_ctx)
    h_ctx = ctx
    for l in range(DEPTH):
        need_ctx = l < DEPTH - 1
        mod_x = (silu_c @ w_ada[l] + b_ada[l])[:, None, :]
        mod_c = silu_cc @ w_ada[l] + b_ada[l]
        sh1, sc1, g1, sh2, sc2, g2 = jnp.split(mod_x, 6, axis=-1)
        csh1, csc1, cg1, csh2, csc2, cg2 = jnp.split(mod_c, 6, axis=-1)
        hx = rmsnorm(x, norm1[l]) * (1.0 + sc1) + sh1
        hc = rmsnorm(h_ctx, norm1[l]) * (1.0 + csc1) + csh1
        out_x, out_c = token_mixing(hx, hc, w_in[l], conv_w[l], a_log[l], dt_bias[l], gdn_norm[l],
                                    w_pool[l], pool_scale[l], sink[l], w_out[l], rope, need_ctx)
        x = x + g1 * out_x
        hx = rmsnorm(x, norm2[l]) * (1.0 + sc2) + sh2
        x = x + g2 * peer_ffn(hx, peer_wq[l], peer_keys[l], peer_u[l], peer_v[l])
        if need_ctx:
            h_ctx = h_ctx + cg1 * out_c
            hc = rmsnorm(h_ctx, norm2[l]) * (1.0 + csc2) + csh2
            h_ctx = h_ctx + cg2 * peer_ffn(hc, peer_wq[l], peer_keys[l], peer_u[l], peer_v[l])
    return rmsnorm(x, norm_f)


_drawn_inputs = setup_inputs


def setup_inputs(seed=0):
    import zlib

    import numpy as np

    out = dict(_drawn_inputs(seed))
    spreads = {}
    factors = {'gdn_norm': 3.797, 'sink': 8.0, 'norm_f': 2.75}
    for name, (base, spread) in spreads.items():
        noise = np.random.default_rng([zlib.crc32(name.encode()), seed]).standard_normal(out[name].shape)
        drawn = base * np.exp(spread * noise) if base else spread * noise
        out[name] = jnp.asarray(drawn.astype(out[name].dtype))
    for name, factor in factors.items():
        out[name] = (out[name] * factor).astype(out[name].dtype)
    return out
```

```python
from contextlib import ExitStack

import numpy as np

import concourse.bass as bass
from concourse import mybir

F32, F32R, U32 = mybir.dt.float32, mybir.dt.float32r, mybir.dt.uint32
ALU, ACT, AX = mybir.AluOpType, mybir.ActivationFunctionType, mybir.AxisListType

P = 128
D = 1024
DC = D // P
T = 256
TT = T // P
EPS = 1e-6
HEADS, N_KEYS, TOPK = 8, 128, 16
GROUPS = 2 * HEADS
SLOTS = HEADS * TOPK
ROUND = 8
WQ_RING = 3
LOWEST = -3.0e38
MASKED = -1.0e30

UU = 2 * TT
HD = 64
POOL_W, GDN_W, ATT_W = 256, 384, 384
POOL_WINDOWS = (2, 4, 8, 16)
GH, AH, KV = GDN_W // HD, ATT_W // HD, 2
QKV_C = 3 * GDN_W // P
CONV_K = 5
PAD = CONV_K // 2
Z_AT = POOL_W
BA_AT = Z_AT + GDN_W
Q_AT = BA_AT + 4 * GH
V_AT = Q_AT + ATT_W + KV * HD
TOK_W = V_AT + KV * HD
MIXED_AT = [P * c for c in range(5)] + [Q_AT + P * c for c in range(3)]
MIX_CONSTS = (("chunk_ones", (P,)), ("tri", (2, P)), ("neg", (2, P)), ("lvl", (2, 6, P)))
CONSTS = sum(int(np.prod(s)) for _, s in MIX_CONSTS)
WINDOW = 128
GRID_W, ROPE_BASE, ROPE_PAIRS = 64, 10000.0, 16


def due(count):
    return not isinstance(count, int) or count > 0


class Core:

    def __init__(self, nc):
        self.nc, self.semaphores, self.stage = nc, {}, 0

    def semaphore(self, name):
        assert name not in self.semaphores, name
        self.semaphores[name] = self.nc.alloc_semaphore(name=f"{name}_{self.stage}")
        return self.semaphores[name]

    def end_stage(self):
        self.nc.clear_and_free_semaphores(list(self.semaphores.values()))
        self.nc.all_engine_barrier()
        self.semaphores, self.stage = {}, self.stage + 1

    def sbuf(self, scope, tag):
        return lambda name, shape, dt=F32: scope.enter_context(self.nc.sbuf_tensor(f"{tag}_{name}", shape, dt))

    def psum(self, scope, tag):
        return lambda name, shape, dt=F32: scope.enter_context(self.nc.psum_tensor(f"{tag}_{name}", shape, dt))


def normalize(core, tag, cols, parts):
    nc = core.nc
    n = cols.stop - cols.start
    with ExitStack() as scope:
        sb = core.sbuf(scope, tag)
        ps = core.psum(scope, tag)
        sq = sb("sq", [P, DC, n])
        rstd = sb("rstd", [P, n])
        s_ps = ps("s_ps", [P, n])
        squared, sums = core.semaphore("squared"), core.semaphore("square_sums")
        mean, root, scaled = core.semaphore("mean_square"), core.semaphore("rms"), core.semaphore("h_scaled")
        inverse = core.semaphore("rstd_ready")
        with nc.Block() as block:

            @block.scalar
            def _(act):
                for c in range(DC):
                    act.activation(sq[:, c], core.x[:, c, cols], ACT.Square).then_inc(squared, 1)
                act.wait_ge(mean, 1)
                act.activation(rstd[:, :], rstd[:, :], ACT.Sqrt).then_inc(root, 1)
                for c in range(DC):
                    for i, (to, shift, _) in enumerate(parts):
                        if shift is not None:
                            act.wait_ge(scaled, c * len(parts) + i + 1)
                            act.activation(core.h[:, c, to], core.h[:, c, to], ACT.Identity, bias=shift[c])

            @block.tensor
            def _(pe):
                for c in range(DC):
                    pe.wait_ge(squared, c + 1)
                    mm = pe.matmul(s_ps[:, :], core.ones, sq[:, c], start=(c == 0), stop=(c == DC - 1))
                mm.then_inc(sums, 1)

            @block.vector
            def _(dve):
                dve.wait_ge(sums, 1)
                dve.tensor_scalar(rstd[:, :], s_ps[:, :], 1.0 / D, EPS, ALU.mult, ALU.add).then_inc(mean, 1)
                dve.wait_ge(root, 1)
                dve.reciprocal(rstd[:, :], rstd[:, :]).then_inc(inverse, 1)
                dve.wait_ge(inverse, 1)
                for c in range(DC):
                    for to, _, g in parts:
                        src = slice(cols.start + to.start, cols.start + to.stop)
                        dve.scalar_tensor_tensor(core.h[:, c, to], core.x[:, c, src], g[c], rstd[:, to],
                                                 ALU.mult, ALU.mult).then_inc(scaled, 1)


def modulation(core, layer, dram):
    nc = core.nc
    tag = f"mod{layer}"
    parts = 6
    with ExitStack() as scope:
        sb = core.sbuf(scope, tag)
        ps = core.psum(scope, tag)
        w = sb("w", [P, 2, DC, D])
        cc = sb("cc", [P, DC, 2])
        bias = sb("bias", [P, parts * DC])
        norms = sb("norms", [P, 2, DC])
        m_ps = ps("m_ps", [P, parts * DC, 2])
        w_in = [core.semaphore(f"wada_in{r}") for r in range(2)]
        cols_in, activated = core.semaphore("mod_cols_in"), core.semaphore("c_activated")
        used, step = core.semaphore("wada_used"), core.semaphore("mod_step")
        with nc.Block() as block:

            @block.sync
            def _(sp):
                sp.dma_start(cc[:, :, :], dram["c2"]).then_inc(cols_in, 16)
                sp.dma_start(bias[:, :], dram["b_ada"][layer]).then_inc(cols_in, 16)
                sp.dma_start(norms[:, :, :], dram["norms"][layer]).then_inc(cols_in, 16)
                for k in range(parts):
                    if due(k - 1):
                        sp.wait_ge(used, k - 1)
                    sp.dma_start(w[:, k % 2], dram["w_ada"][layer, k]).then_inc(w_in[k % 2], 16)

            @block.scalar
            def _(act):
                act.wait_ge(cols_in, 48)
                act.activation(cc[:, :, :], cc[:, :, :], ACT.Silu).then_inc(activated, 1)

            @block.tensor
            def _(pe):
                pe.wait_ge(activated, 1)
                for k in range(parts):
                    pe.wait_ge(w_in[k % 2], 16 * (k // 2 + 1))
                    for j in range(DC):
                        for c in range(DC):
                            mm = pe.matmul(m_ps[:, k * DC + j], w[:, k % 2, c, j * P:(j + 1) * P], cc[:, c],
                                           start=(c == 0), stop=(c == DC - 1))
                    mm.then_inc(used, 1)

            @block.vector
            def _(dve):
                dve.wait_ge(used, parts)
                dve.tensor_tensor(core.mod[:, :, :], m_ps[:, :, :],
                                  bias[:, :].unsqueeze(2).broadcast_to([P, parts * DC, 2]), ALU.add).then_inc(step, 1)
                dve.wait_ge(step, 1)
                for n in range(2):
                    scale = core.mod[:, (3 * n + 1) * DC:(3 * n + 2) * DC]
                    dve.tensor_scalar(core.gain[:, n], scale, 1.0, None, ALU.add).then_inc(step, 1)
                dve.wait_ge(step, 3)
                for n in range(2):
                    dve.tensor_tensor(core.gain[:, n], core.gain[:, n],
                                      norms[:, n].unsqueeze(2).broadcast_to([P, DC, 2]), ALU.mult)


def project_in(core, layer, dram, conv_in, tok):
    nc = core.nc
    tag = f"pi{layer}"
    with ExitStack() as scope:
        sb = core.sbuf(scope, tag)
        ps = core.psum(scope, tag)
        ring = 3
        wf = sb("wf", [P, ring, DC, P])
        wt = sb("wt", [P, DC, TOK_W])
        o_ps = ps("o_ps", [P, 4, 512])
        wf_in = [core.semaphore(f"wf_in{r}") for r in range(ring)]
        wt_in, made = core.semaphore("wt_in"), core.semaphore("proj_made")
        copied = [core.semaphore("proj_copied_act"), core.semaphore("proj_copied_dve")]
        padded = core.semaphore("conv_padded")
        width = TOK_W // 4
        products = QKV_C + 4 * UU

        def place(n):
            if n < QKV_C:
                return conv_in[:, n, :, PAD:PAD + T], o_ps[:, n % 4].rearrange("p (s t) -> p s t", s=2)
            u, k = divmod(n - QKV_C, 4)
            return tok[:, u, k * width:(k + 1) * width], o_ps[:, n % 4, 0:width]

        with nc.Block() as block:

            @block.gpsimd
            def _(pool):
                pool.memset(conv_in[:, :, :, 0:PAD], 0.0)
                pool.memset(conv_in[:, :, :, PAD + T:2 * PAD + T], 0.0).then_inc(padded, 1)

            @block.sync
            def _(sp):
                for j in range(QKV_C):
                    if j == ring:
                        sp.dma_start(wt[:, :, :], dram["w_tok"][layer]).then_inc(wt_in, 16)
                    if due(j - ring + 1):
                        sp.wait_ge(made, j - ring + 1)
                    sp.dma_start(wf[:, j % ring], dram["w_qkv"][layer, j]).then_inc(wf_in[j % ring], 16)

            @block.tensor
            def _(pe):
                for n in range(products):
                    b = n % 4
                    if due((n - 4) // 2 + 1):
                        pe.wait_ge(copied[n % 2], (n - 4) // 2 + 1)
                    if n < QKV_C:
                        pe.wait_ge(wf_in[n % ring], 16 * (n // ring + 1))
                        for c in range(DC):
                            mm = pe.matmul(o_ps[:, b], wf[:, n % ring, c], core.h[:, c, :], start=(c == 0), stop=(c == DC - 1))
                    else:
                        if n == QKV_C:
                            pe.wait_ge(wt_in, 16)
                        u, k = divmod(n - QKV_C, 4)
                        for c in range(DC):
                            mm = pe.matmul(o_ps[:, b, 0:width], core.h[:, c, u * P:(u + 1) * P],
                                           wt[:, c, k * width:(k + 1) * width], start=(c == 0), stop=(c == DC - 1))
                    mm.then_inc(made, 1)

            @block.scalar
            def _(act):
                for n in range(0, products, 2):
                    act.wait_ge(made, n + 1)
                    act.activation(*place(n), ACT.Copy).then_inc(copied[0], 1)

            @block.vector
            def _(dve):
                for n in range(1, products, 2):
                    dve.wait_ge(made, n + 1)
                    dve.tensor_copy(*place(n)).then_inc(copied[1], 1)


def short_conv(core, layer, dram, conv_in, qkv, heads_t):
    nc = core.nc
    tag = f"sc{layer}"
    with ExitStack() as scope:
        sb = core.sbuf(scope, tag)
        ps = core.psum(scope, tag)
        conv = sb("conv", [P, QKV_C, 2, T])
        taps = sb("taps", [P, QKV_C, CONV_K])
        sq = sb("sq", [P, 2, 2 * GDN_W])
        norm = sb("norm", [P, UU, 2 * GH])
        t_ps = ps("t_ps", [P, 2, UU, P])
        h_ps = ps("h_ps", [HD, 3, 4, P])
        taps_in, step, convolved = core.semaphore("taps_in"), core.semaphore("conv_step"), core.semaphore("convolved")
        silud, turned, back = core.semaphore("conv_silu"), core.semaphore("conv_turned"), core.semaphore("conv_token_major")
        squares, roots, unit = core.semaphore("norm_squares"), core.semaphore("norm_roots"), core.semaphore("unit_qk")
        turned_h, kept_h = core.semaphore("heads_turned"), core.semaphore("heads_kept")
        n_steps = [0]
        with nc.Block() as block:

            @block.sync
            def _(sp):
                sp.dma_start(taps[:, :, :], dram["conv_w"][layer]).then_inc(taps_in, 16)

            @block.vector
            def _(dve):
                def link(ins):
                    n_steps[0] += 1
                    ins.then_inc(step, 1)
                    dve.wait_ge(step, n_steps[0])

                dve.wait_ge(taps_in, 16)
                for j0 in range(0, QKV_C, 3):
                    for k in range(CONV_K):
                        for j in range(j0, j0 + 3):
                            src = conv_in[:, j, :, k:k + T]
                            if k == 0:
                                ins = dve.tensor_scalar(conv[:, j], src, taps[:, j, 0:1], None, ALU.mult)
                            else:
                                ins = dve.scalar_tensor_tensor(conv[:, j], src, taps[:, j, k:k + 1], conv[:, j], ALU.mult, ALU.add)
                            if k == CONV_K - 1:
                                ins.then_inc(convolved, 1)
                        if k < CONV_K - 1:
                            link(ins)
                dve.wait_ge(back, QKV_C)
                for u in range(UU):
                    link(dve.tensor_tensor(sq[:, u % 2], qkv[:, u, 0:2 * GDN_W], qkv[:, u, 0:2 * GDN_W], ALU.mult))
                    link(dve.tensor_reduce(norm[:, u], sq[:, u % 2].rearrange("p (h d) -> p h d", d=HD), AX.X, ALU.add))
                dve.tensor_scalar(norm[:, :, :], norm[:, :, :], EPS, None, ALU.add).then_inc(squares, 1)
                dve.wait_ge(roots, 1)
                link(dve.reciprocal(norm[:, :, :], norm[:, :, :]))
                link(dve.tensor_scalar(norm[:, :, 0:GH], norm[:, :, 0:GH], HD ** -0.5, None, ALU.mult))
                for u in range(UU):
                    rows = qkv[:, u, 0:2 * GDN_W].rearrange("p (h d) -> p h d", d=HD)
                    dve.tensor_tensor(rows, rows, norm[:, u].unsqueeze(2).broadcast_to([P, 2 * GH, HD]),
                                      ALU.mult).then_inc(unit, 1)

            @block.scalar
            def _(act):
                for j in range(QKV_C):
                    act.wait_ge(convolved, j + 1)
                    act.activation(conv[:, j], conv[:, j], ACT.Silu).then_inc(silud, 1)
                    if j:
                        act.wait_ge(turned, j)
                        act.activation(qkv[:, :, (j - 1) * P:j * P], t_ps[:, (j - 1) % 2], ACT.Copy).then_inc(back, 1)
                act.wait_ge(turned, QKV_C)
                act.activation(qkv[:, :, (QKV_C - 1) * P:QKV_C * P], t_ps[:, (QKV_C - 1) % 2], ACT.Copy).then_inc(back, 1)
                act.wait_ge(squares, 1)
                act.activation(norm[:, :, :], norm[:, :, :], ACT.Sqrt).then_inc(roots, 1)
                for n in range(3 * UU):
                    u, g = divmod(n, 3)
                    act.wait_ge(turned_h, n + 1)
                    act.activation(heads_t[:, u, 4 * g:4 * g + 4], h_ps[:, g], ACT.Copy).then_inc(kept_h, 1)

            @block.tensor
            def _(pe):
                for j in range(QKV_C):
                    pe.wait_ge(silud, j + 1)
                    if due(j - 1):
                        pe.wait_ge(back, j - 1)
                    for u in range(UU):
                        mm = pe.transpose(t_ps[:, j % 2, u], conv[:, j, u // TT, (u % TT) * P:(u % TT + 1) * P], core.ident)
                    mm.then_inc(turned, 1)
                for n in range(3 * UU):
                    u, g = divmod(n, 3)
                    pe.wait_ge(unit, u + 1)
                    if due(n - 2):
                        pe.wait_ge(kept_h, n - 2)
                    for x in range(4):
                        hd = 4 * g + x
                        mm = pe.transpose(h_ps[:, g, x], qkv[:, u, hd * HD:(hd + 1) * HD], core.ident)
                    mm.then_inc(turned_h, 1)


def gdn_gates(core, layer, dram, tok, beta, decay_g):
    nc = core.nc
    tag = f"gg{layer}"
    with ExitStack() as scope:
        sb = core.sbuf(scope, tag)
        rate, bias = sb("rate", [P, 2 * GH]), sb("bias", [P, 2 * GH])
        a, neg = sb("a", [P, UU, 2 * GH]), sb("neg", [P, UU, 2 * GH])
        rows_in, step = core.semaphore("gate_rows_in"), core.semaphore("gate_step")
        biased, logged, done = core.semaphore("gate_biased"), core.semaphore("gate_logged"), core.semaphore("gate_act")
        full = [P, UU, 2 * GH]
        b0 = BA_AT
        with nc.Block() as block:

            @block.sync
            def _(sp):
                sp.dma_start(rate[:, :], dram["a_log"][layer].unsqueeze(0).broadcast_to([P, 2 * GH])).then_inc(rows_in, 16)
                sp.dma_start(bias[:, :], dram["dt_bias"][layer].unsqueeze(0).broadcast_to([P, 2 * GH])).then_inc(rows_in, 16)

            @block.vector
            def _(dve):
                dve.wait_ge(rows_in, 32)
                dve.tensor_tensor(a[:, :, :], tok[:, :, b0 + 2 * GH:b0 + 4 * GH], bias[:, :].unsqueeze(1).broadcast_to(full),
                                  ALU.add).then_inc(step, 1)
                dve.wait_ge(step, 1)
                dve.scalar_tensor_tensor(neg[:, :, :], a[:, :, :], -1.0, a[:, :, :], ALU.mult, ALU.min).then_inc(biased, 1)
                dve.wait_ge(logged, 1)
                dve.scalar_tensor_tensor(a[:, :, :], a[:, :, :], 0.0, neg[:, :, :], ALU.max, ALU.add).then_inc(step, 1)
                dve.wait_ge(step, 2)
                dve.scalar_tensor_tensor(decay_g[:, :, :], a[:, :, :], -1.0, rate[:, :].unsqueeze(1).broadcast_to(full),
                                         ALU.mult, ALU.mult)

            @block.scalar
            def _(act):
                act.wait_ge(rows_in, 32)
                act.activation(beta[:, :, :], tok[:, :, b0:b0 + 2 * GH], ACT.Sigmoid)
                act.activation(rate[:, :], rate[:, :], ACT.Exp)
                act.wait_ge(biased, 1)
                act.activation(neg[:, :, :], neg[:, :, :], ACT.Exp).then_inc(done, 1)
                act.wait_ge(done, 1)
                act.activation(neg[:, :, :], neg[:, :, :], ACT.Ln, bias=1.0).then_inc(logged, 1)


def gdn_chunks(core, layer, cst, qkv, heads_t, beta, decay_g, made):
    nc = core.nc
    tag = f"gc{layer}"
    groups = [(u, d) for u in range(UU) for d in range(2)]
    levels = 5
    with ExitStack() as scope:
        sb = core.sbuf(scope, tag)
        ps = core.psum(scope, tag)
        three = [P, 3, P]
        gcol, gtot = sb("gcol", [P, UU, 2 * GH]), sb("gtot", [P, UU, 2 * GH])
        bexp, kexp = sb("bexp", [P, UU, 2 * GH]), sb("kexp", [P, UU, 2 * GH])
        kbe, vb = sb("kbe", [P, 2, 2, 3, HD]), sb("vb", [P, 2, 2, 3, HD])
        work = [{k: sb(f"{k}{f}", three) for k in ("dif", "lt", "x", "xt", "y")} for f in range(2)]
        cut = [sb(f"cut{f}", [P, levels + 1, 3, P]) for f in range(2)]
        bank = [ps(f"bank{f}", [P, 4, 512]) for f in range(2)]
        S = core.semaphore
        sums, sums_out, decays, scaled = S("g_sums"), S("g_sums_out"), S("g_decays"), S("g_scaled")
        two = lambda name: [S(f"{name}{f}") for f in range(2)]
        products, lower, cuts = two("products"), two("lower"), two("cuts")
        dstep, decayed = two("dif_step"), two("decayed")
        start_t, start_turned, start_x = two("start_t"), two("start_turned"), two("start_x")
        y_made, y_kept, xy_made, xyt_made = two("y_made"), two("y_kept"), two("xy_made"), two("xyt_made")
        x_new, xt_new, solved, kept = two("x_new"), two("xt_new"), two("solved"), two("kept")
        rhs, rhs_step = S("rhs"), S("rhs_step")
        tri, neg, lvl, chunk_ones = cst["tri"], cst["neg"], cst["lvl"], cst["chunk_ones"]

        def b3(f, k, n=P, rows=P):
            return bank[f][0:rows, k, 0:3 * n].rearrange("p (h n) -> p h n", h=3)

        with nc.Block() as block:

            @block.tensor
            def _(pe):
                g_ps, w_ps = bank[0][:, 0], bank[1][0:HD, 0]
                for u in range(UU):
                    for d in range(2):
                        a = u * 24 + d * GH
                        pe.matmul(g_ps[:, a:a + GH], tri[d], decay_g[:, u, d * GH:(d + 1) * GH], start=True, stop=True)
                    pe.matmul(g_ps[:, u * 24 + 12:u * 24 + 24], chunk_ones, decay_g[:, u], start=True, stop=True)
                    for x in range(2):
                        a = (2 * u + x) * 12
                        mm = pe.matmul(w_ps[:, a:a + 12], chunk_ones[:, x * HD:(x + 1) * HD], decay_g[:, u], start=True, stop=True)
                mm.then_inc(sums, 1)
                pe.wait_ge(sums_out, 2)

                def setup(n, f):
                    u, d = groups[n]
                    if due(2 * n):
                        pe.wait_ge(kept[f], 2 * n)
                    if due((levels - 1) * n):
                        pe.wait_ge(x_new[f], (levels - 1) * n)
                    if due(levels * n):
                        pe.wait_ge(xt_new[f], levels * n)
                    for k, h in enumerate(range(3 * f, 3 * f + 3)):
                        pe.matmul(b3(f, 0)[:, k], heads_t[:, u, GH + h], heads_t[:, u, GH + h], start=True, stop=True)
                        pe.matmul(b3(f, 1)[:, k], heads_t[:, u, GH + h], heads_t[:, u, h], start=True, stop=True)
                        c = d * GH + h
                        pe.matmul(b3(f, 2)[:, k], decay_g[:, u, c:c + 1].broadcast_to([P, P]), tri[d], start=True, stop=True)
                        mm = pe.matmul(b3(f, 3)[:, k], beta[:, u, c:c + 1].broadcast_to([P, P]), core.ident, start=True, stop=True)
                    mm.then_inc(products[f], 1)

                def turn(n, f):
                    pe.wait_ge(start_t[f], n + 1)
                    for k in range(3):
                        mm = pe.transpose(b3(f, 1)[:, k], work[f]["xt"][:, k], core.ident)
                    mm.then_inc(start_turned[f], 1)

                def times_x(n, v, f):
                    pe.wait_ge(cuts[f], (levels + 1) * n + v + 2)
                    if v == 0:
                        pe.wait_ge(start_x[f], n + 1)
                    else:
                        if due((levels - 1) * n + v):
                            pe.wait_ge(x_new[f], (levels - 1) * n + v)
                    if due(levels * n + v):
                        pe.wait_ge(y_kept[f], levels * n + v)
                    for k in range(3):
                        mm = pe.matmul(b3(f, 0)[:, k], cut[f][:, v + 1, k], work[f]["x"][:, k], start=True, stop=True)
                    mm.then_inc(y_made[f], 1)

                def x_times(n, v, f):
                    pe.wait_ge(y_kept[f], levels * n + v + 1)
                    if v:
                        if due(levels * n + v):
                            pe.wait_ge(xt_new[f], levels * n + v)
                    if v < levels - 1:
                        for k in range(3):
                            mm = pe.matmul(b3(f, 1)[:, k], work[f]["xt"][:, k], work[f]["y"][:, k], start=True, stop=True)
                        mm.then_inc(xy_made[f], 1)
                    for k in range(3):
                        mm = pe.matmul(b3(f, 2)[:, k], work[f]["y"][:, k], work[f]["xt"][:, k], start=True, stop=True)
                    mm.then_inc(xyt_made[f], 1)

                def solve(n, f):
                    pe.wait_ge(xt_new[f], levels * (n + 1))
                    pe.wait_ge(rhs, n + 1)
                    for k in range(3):
                        pe.matmul(b3(f, 3, HD)[:, k], work[f]["xt"][:, k], vb[:, n % 2, f, k], start=True, stop=True)
                        mm = pe.matmul(b3(f, 0, P, HD)[:, k], kbe[:, n % 2, f, k], work[f]["xt"][:, k], start=True, stop=True)
                    mm.then_inc(solved[f], 1)

                for n in range(len(groups)):
                    for f in range(2):
                        setup(n, f)
                    for f in range(2):
                        turn(n, f)
                    for v in range(levels):
                        for f in range(2):
                            times_x(n, v, f)
                        for f in range(2):
                            x_times(n, v, f)
                    for f in range(2):
                        solve(n, f)

            @block.vector
            def _(dve):
                dve.wait_ge(sums, 1)
                g_ps = bank[0][:, 0, 0:UU * 24].rearrange("p (u n) -> p u n", u=UU)
                dve.tensor_copy(gcol[:, :, :], g_ps[:, :, 0:12])
                dve.tensor_copy(gtot[:, :, :], g_ps[:, :, 12:24]).then_inc(sums_out, 1)
                dve.wait_ge(sums_out, 2)
                dve.tensor_tensor(kexp[:, :, :], gtot[:, :, :], gcol[:, :, :], ALU.subtract).then_inc(decays, 1)
                dve.wait_ge(scaled, 1)
                dve.tensor_tensor(bexp[:, :, :], beta[:, :, :], made["grow"][:, :, :], ALU.mult).then_inc(rhs_step, 1)

                def decay(n, f):
                    u, d = groups[n]
                    w = work[f]
                    dve.wait_ge(products[f], n + 1)
                    c = d * GH + 3 * f
                    dve.tensor_tensor(w["dif"][:, :, :], b3(f, 2), gcol[:, u, c:c + 3].unsqueeze(2).broadcast_to(three),
                                      ALU.subtract).then_inc(dstep[f], 1)

                def mask(n, f):
                    d = groups[n][1]
                    w = work[f]
                    dve.wait_ge(dstep[f], 4 * n + 1)
                    dve.scalar_tensor_tensor(w["dif"][:, :, :], w["dif"][:, :, :], 0.0, neg[d].unsqueeze(1).broadcast_to(three),
                                             ALU.min, ALU.add).then_inc(dstep[f], 1)

                def weigh(n, f):
                    u, d = groups[n]
                    w = work[f]
                    dve.wait_ge(decayed[f], n + 1)
                    dve.tensor_tensor(w["lt"][:, :, :], b3(f, 0), w["dif"][:, :, :], ALU.mult).then_inc(dstep[f], 1)
                    dve.tensor_tensor(made["attn"][:, u, d, 3 * f:3 * f + 3], b3(f, 1), w["dif"][:, :, :], ALU.mult).then_inc(dstep[f], 1)
                    dve.wait_ge(dstep[f], 4 * n + 3)
                    dve.tensor_tensor(w["lt"][:, :, :], w["lt"][:, :, :], b3(f, 3), ALU.mult).then_inc(lower[f], 1)

                def begin(n, f):
                    dve.wait_ge(cuts[f], (levels + 1) * n + 1)
                    dve.tensor_tensor(work[f]["xt"][:, :, :], core.ident.unsqueeze(1).broadcast_to(three), cut[f][:, 0],
                                      ALU.subtract).then_inc(start_t[f], 1)

                def update(n, v, f):
                    w = work[f]
                    if v < levels - 1:
                        dve.wait_ge(xy_made[f], (levels - 1) * n + v + 1)
                        if v == 0:
                            dve.wait_ge(start_x[f], n + 1)
                        else:
                            if due((levels - 1) * n + v):
                                dve.wait_ge(x_new[f], (levels - 1) * n + v)
                        dve.tensor_tensor(w["x"][:, :, :], w["x"][:, :, :], b3(f, 1), ALU.subtract).then_inc(x_new[f], 1)
                    dve.wait_ge(xyt_made[f], levels * n + v + 1)
                    if v == 0:
                        dve.wait_ge(start_t[f], n + 1)
                    else:
                        if due(levels * n + v):
                            dve.wait_ge(xt_new[f], levels * n + v)
                    dve.tensor_tensor(w["xt"][:, :, :], w["xt"][:, :, :], b3(f, 2), ALU.subtract).then_inc(xt_new[f], 1)

                for n in range(len(groups)):
                    for f in range(2):
                        if n:
                            if due((levels + 1) * n):
                                dve.wait_ge(cuts[f], (levels + 1) * n)
                            if due(n):
                                dve.wait_ge(solved[f], n)
                        decay(n, f)
                    for f in range(2):
                        mask(n, f)
                    for f in range(2):
                        weigh(n, f)
                    for f in range(2):
                        begin(n, f)
                    for v in range(levels):
                        for f in range(2):
                            update(n, v, f)

            @block.scalar
            def _(act):
                act.wait_ge(sums, 1)
                act.activation(made["whole"][:, :, :], bank[1][0:HD, 0, 0:2 * UU * 12].rearrange("p (c n) -> p c n", c=2 * UU),
                               ACT.Exp).then_inc(sums_out, 1)
                act.wait_ge(decays, 1)
                act.activation(kexp[:, :, :], kexp[:, :, :], ACT.Exp)
                act.activation(made["grow"][:, :, :], gcol[:, :, :], ACT.Exp).then_inc(scaled, 1)
                for n, (u, d) in enumerate(groups):
                    for f in range(2):
                        act.wait_ge(dstep[f], 4 * n + 2)
                        act.activation(work[f]["dif"][:, :, :], work[f]["dif"][:, :, :], ACT.Exp).then_inc(decayed[f], 1)
                    for f in range(2):
                        act.wait_ge(start_turned[f], n + 1)
                        act.activation(work[f]["x"][:, :, :], b3(f, 1), ACT.Copy).then_inc(start_x[f], 1)
                    for v in range(levels):
                        for f in range(2):
                            act.wait_ge(y_made[f], levels * n + v + 1)
                            if due(levels * n + v):
                                act.wait_ge(xyt_made[f], levels * n + v)
                            act.activation(work[f]["y"][:, :, :], b3(f, 0), ACT.Copy).then_inc(y_kept[f], 1)
                    for f in range(2):
                        act.wait_ge(solved[f], n + 1)
                        act.activation(made["value"][:, u, d, 3 * f:3 * f + 3], b3(f, 3, HD), ACT.Copy).then_inc(kept[f], 1)
                        act.activation(made["key_t"][:, u, d, 3 * f:3 * f + 3], b3(f, 0, P, HD), ACT.Copy).then_inc(kept[f], 1)

            @block.gpsimd
            def _(pool):
                def sides(n):
                    u, d = groups[n]
                    six = [P, GH, HD]
                    for f in range(2):
                        if due(n - 1):
                            pool.wait_ge(solved[f], n - 1)
                    k = qkv[:, u, GDN_W:2 * GDN_W].rearrange("p (h e) -> p h e", e=HD)
                    v = qkv[:, u, 2 * GDN_W:3 * GDN_W].rearrange("p (h e) -> p h e", e=HD)
                    c = slice(d * GH, (d + 1) * GH)
                    pool.tensor_tensor(kbe[:, n % 2].rearrange("p f h e -> p (f h) e"), k, bexp[:, u, c].unsqueeze(2).broadcast_to(six), ALU.mult)
                    pool.tensor_tensor(made["key_dec"][:, u, d], k, kexp[:, u, c].unsqueeze(2).broadcast_to(six), ALU.mult)
                    pool.tensor_tensor(vb[:, n % 2].rearrange("p f h e -> p (f h) e"), v, beta[:, u, c].unsqueeze(2).broadcast_to(six),
                                       ALU.mult).then_inc(rhs, 1)

                pool.wait_ge(rhs_step, 1)
                for n, (u, d) in enumerate(groups):
                    sides(n)
                    for v in range(levels + 1):
                        for f in range(2):
                            if v == 0:
                                pool.wait_ge(lower[f], n + 1)
                                if due(n):
                                    pool.wait_ge(start_t[f], n)
                                if due(levels * n):
                                    pool.wait_ge(y_made[f], levels * n)
                            pool.tensor_tensor(cut[f][:, v], work[f]["lt"][:, :, :], lvl[d][:, v].unsqueeze(1).broadcast_to(three),
                                               ALU.mult).then_inc(cuts[f], 1)
        n = len(groups)


def gdn_states(core, layer, need_ctx, heads_t, made):
    nc = core.nc
    tag = f"gs{layer}"
    with ExitStack() as scope:
        sb = core.sbuf(scope, tag)
        ps = core.psum(scope, tag)
        state = [sb(f"state{d}", [HD, GH, HD]) for d in range(2)]
        new = [sb(f"new{d}", [P, GH, HD]) for d in range(2)]
        part = [sb(f"part{d}", [P, GH, HD]) for d in range(2)]
        bank = [ps(f"bank{d}", [P, 4, 512]) for d in range(2)]
        S = core.semaphore
        two = lambda name: [S(f"{name}{d}") for d in range(2)]
        zeroed, read, corrected = two("state_zeroed"), two("state_read"), two("value_corrected")
        added, decayed, stated, outed = two("chunk_added"), two("state_decayed"), two("state_new"), two("out_part")
        out_done = two("out_done")
        steps = 2 * T // HD

        def place(n, d):
            ch = n % 4 if d == 0 else 3 - n % 4
            u = (TT if n < 4 else 0) + ch // 2
            return u, HD * (ch % 2), n >= 4 or need_ctx, 2 * u + ch % 2

        def b6(d, k, a, rows=HD):
            return bank[d][a:a + rows, k, 0:GH * HD].rearrange("p (h e) -> p h e", h=GH)

        with nc.Block() as block:

            @block.tensor
            def _(pe):
                for n in range(steps):
                    for d in range(2):
                        u, a, out, _ = place(n, d)
                        pe.wait_ge(zeroed[d], 1)
                        if due(n):
                            pe.wait_ge(stated[d], n)
                        if n:
                            if due(n):
                                pe.wait_ge(out_done[d], n)
                        for h in range(GH):
                            mm = pe.matmul(b6(d, 0, a)[:, h], made["key_t"][:, u, d, h, a:a + HD], state[d][:, h], start=True, stop=True)
                        if out:
                            for h in range(GH):
                                mm = pe.matmul(b6(d, 1, a)[:, h], heads_t[:, u, h, a:a + HD], state[d][:, h], start=True, stop=True)
                        mm.then_inc(read[d], 1)
                    for d in range(2):
                        u, a, out, _ = place(n, d)
                        pe.wait_ge(corrected[d], n + 1)
                        for h in range(GH):
                            mm = pe.matmul(b6(d, 2, 0)[:, h], made["key_dec"][a:a + HD, u, d, h], new[d][a:a + HD, h], start=True, stop=True)
                        if out:
                            for h in range(GH):
                                mm = pe.matmul(b6(d, 3, a)[:, h], made["attn"][a:a + HD, u, d, h, a:a + HD], new[d][a:a + HD, h],
                                               start=True, stop=True)
                        mm.then_inc(added[d], 1)

            @block.vector
            def _(dve):
                for d in range(2):
                    dve.memset(state[d][:, :, :], 0.0).then_inc(zeroed[d], 1)
                six = [HD, GH, HD]
                for n in range(steps):
                    for d in range(2):
                        u, a, out, c = place(n, d)
                        dve.wait_ge(read[d], n + 1)
                        dve.tensor_tensor(new[d][a:a + HD], made["value"][a:a + HD, u, d], b6(d, 0, a), ALU.subtract).then_inc(corrected[d], 1)
                    for d in range(2):
                        u, a, out, c = place(n, d)
                        dve.wait_ge(zeroed[d], 1)
                        if due(n):
                            dve.wait_ge(stated[d], n)
                        dve.tensor_tensor(state[d][:, :, :], state[d][:, :, :],
                                          made["whole"][:, c, d * GH:(d + 1) * GH].unsqueeze(2).broadcast_to(six),
                                          ALU.mult).then_inc(decayed[d], 1)
                        if out:
                            if due(n):
                                dve.wait_ge(out_done[d], n)
                            dve.tensor_tensor(part[d][a:a + HD], b6(d, 1, a),
                                              made["grow"][a:a + HD, u, d * GH:(d + 1) * GH].unsqueeze(2).broadcast_to(six),
                                              ALU.mult).then_inc(outed[d], 1)
                        else:
                            dve.engine_nop().then_inc(outed[d], 1)
                    for d in range(2):
                        u, a, out, c = place(n, d)
                        dve.wait_ge(added[d], n + 1)
                        dve.wait_ge(decayed[d], n + 1)
                        dve.tensor_tensor(state[d][:, :, :], state[d][:, :, :], b6(d, 2, 0), ALU.add).then_inc(stated[d], 1)
                        dve.wait_ge(outed[d], n + 1)
                        if out:
                            dve.wait_ge(corrected[d], n + 1)
                            dve.tensor_tensor(made["value"][a:a + HD, u, d], part[d][a:a + HD], b6(d, 3, a), ALU.add).then_inc(out_done[d], 1)
                        else:
                            dve.engine_nop().then_inc(out_done[d], 1)


def gdn_finish(core, layer, tiles, dram, tok, made):
    nc = core.nc
    tag = f"gf{layer}"
    with ExitStack() as scope:
        sb = core.sbuf(scope, tag)
        gain = sb("gain", [P, HD])
        sq = sb("sq", [P, tiles, GH, HD])
        n2 = sb("n2", [P, tiles, GH])
        z = sb("z", [P, tiles, GDN_W])
        gain_in, step = core.semaphore("gdn_gain_in"), core.semaphore("finish_step")
        squares, roots, gated = core.semaphore("out_squares"), core.semaphore("out_roots"), core.semaphore("z_silu")
        n_steps = [0]
        full = [P, tiles * GH, HD]
        with nc.Block() as block:

            @block.sync
            def _(sp):
                sp.dma_start(gain[:, :], dram["gdn_norm"][layer].unsqueeze(0).broadcast_to([P, HD])).then_inc(gain_in, 16)

            @block.scalar
            def _(act):
                act.activation(z[:, :, :], tok[:, 0:tiles, Z_AT:Z_AT + GDN_W], ACT.Silu).then_inc(gated, 1)
                act.wait_ge(squares, 1)
                act.activation(n2[:, :, :], n2[:, :, :], ACT.Sqrt).then_inc(roots, 1)

            @block.vector
            def _(dve):
                def link(ins):
                    n_steps[0] += 1
                    ins.then_inc(step, 1)
                    dve.wait_ge(step, n_steps[0])

                o = made["value"][:, 0:tiles, 0]
                link(dve.tensor_tensor(o, o, made["value"][:, 0:tiles, 1], ALU.add))
                link(dve.tensor_tensor(sq[:, :, :, :], o, o, ALU.mult))
                link(dve.tensor_reduce(n2[:, :, :], sq[:, :, :, :], AX.X, ALU.add))
                dve.tensor_scalar(n2[:, :, :], n2[:, :, :], 1.0 / HD, EPS, ALU.mult, ALU.add).then_inc(squares, 1)
                dve.wait_ge(roots, 1)
                link(dve.reciprocal(n2[:, :, :], n2[:, :, :]))
                link(dve.tensor_tensor(o, o, n2[:, :, :].unsqueeze(3).broadcast_to([P, tiles, GH, HD]), ALU.mult))
                dve.wait_ge(gain_in, 16)
                g = gain[:, :].unsqueeze(1).unsqueeze(1).broadcast_to([P, tiles, GH, HD])
                link(dve.tensor_tensor(o, o, g, ALU.mult))
                dve.wait_ge(gated, 1)
                dve.tensor_tensor(tok[:, 0:tiles, Z_AT:Z_AT + GDN_W], o.rearrange("p u h e -> p u (h e)"),
                                  z[:, :, :], ALU.mult)


def pooling(core, layer, streams, dram, tok):
    nc = core.nc
    tag = f"pl{layer}"
    with ExitStack() as scope:
        sb = core.sbuf(scope, tag)
        ps = core.psum(scope, tag)
        w = sb("w", [HD, 4, HD])
        scale = sb("scale", [P, POOL_W])
        pooled = sb("pooled", [HD, streams, 4, T])
        a_ps = ps("a_ps", [HD, 2, 2, T])
        o_ps = ps("o_ps", [P, 2, 512])
        rows_in, summed = core.semaphore("pool_rows_in"), core.semaphore("pool_summed")
        kept, made, done = core.semaphore("pool_kept"), core.semaphore("pool_made"), core.semaphore("pool_scaled")
        band = sb("band", [P, 4, TT, T])
        with nc.Block() as block:

            @block.sync
            def _(sp):
                sp.dma_start(w[:, :, :], dram["w_pool"][layer]).then_inc(rows_in, 16)
                sp.dma_start(band[:, :, :, :], dram["band"]).then_inc(rows_in, 16)
                sp.dma_start(scale[:, :], dram["pool_scale"][layer].unsqueeze(0).broadcast_to([P, POOL_W])).then_inc(rows_in, 16)

            @block.tensor
            def _(pe):
                pe.wait_ge(rows_in, 48)
                for n in range(2 * streams):
                    s, b = divmod(n, 2)
                    if due(n - 1):
                        pe.wait_ge(kept, n - 1)
                    for x in range(2):
                        g = 2 * b + x
                        for k in range(TT):
                            mm = pe.matmul(a_ps[:, b, x], tok[:, s * TT + k, g * HD:(g + 1) * HD], band[:, g, k],
                                           start=(k == 0), stop=(k == TT - 1))
                    mm.then_inc(summed, 1)
                for u in range(streams * TT):
                    pe.wait_ge(kept, 2 * (u // TT) + 2)
                    if due(u - 1):
                        pe.wait_ge(done, u - 1)
                    for g in range(4):
                        mm = pe.matmul(o_ps[:, u % 2, g * HD:(g + 1) * HD], pooled[:, u // TT, g, (u % TT) * P:(u % TT + 1) * P],
                                       w[:, g], start=True, stop=True)
                    mm.then_inc(made, 1)

            @block.scalar
            def _(act):
                for n in range(2 * streams):
                    s, b = divmod(n, 2)
                    act.wait_ge(summed, n + 1)
                    act.activation(pooled[:, s, 2 * b:2 * b + 2], a_ps[:, b], ACT.Copy).then_inc(kept, 1)

            @block.vector
            def _(dve):
                dve.wait_ge(rows_in, 48)
                for u in range(streams * TT):
                    dve.wait_ge(made, u + 1)
                    dve.tensor_tensor(tok[:, u, 0:POOL_W], o_ps[:, u % 2, 0:POOL_W], scale[:, :], ALU.mult).then_inc(done, 1)


def attention(core, layer, need_ctx, dram, tok):
    nc = core.nc
    tag = f"at{layer}"
    with ExitStack() as scope:
        sb = core.sbuf(scope, tag)
        ps = core.psum(scope, tag)
        heads = AH + KV
        sink = sb("sink", [P, AH])
        roped = sb("roped", [P, TT, heads * HD])
        tmp = sb("tmp", [P, 2, TT, heads * 2 * 16])
        q_t, k_t = sb("q_t", [HD, UU, AH, P]), sb("k_t", [HD, KV, 2 * T])
        s_sb, p_sb, p_t = sb("s_sb", [P, 2, 2 * T]), sb("p_sb", [P, 2, 2 * T]), sb("p_t", [P, 2, UU, P])
        units = [(u, h) for u in range(UU if need_ctx else TT) for h in range(AH)]
        small = sb("small", [P, 6, len(units)])
        s_ps, t_ps = ps("s_ps", [P, 2, 512]), ps("t_ps", [P, 2, UU, P])
        o_ps, h_ps = ps("o_ps", [P, 2, 512]), ps("h_ps", [HD, 2, 4, P])
        S = core.semaphore
        sink_in, rope_step, roped_s = S("sink_in"), S("rope_step"), S("roped")
        turned, kept = S("att_turned"), S("att_kept")
        scored, masked, peaked, raised, totals = S("att_scored"), S("att_masked"), S("att_peaked"), S("att_raised"), S("att_totals")
        p_turned, p_kept, summed, done = S("p_turned"), S("p_kept"), S("att_summed"), S("att_done")
        peak_found, added_up, inverted = S("peak_found"), S("totals_added"), S("totals_inverted")
        rope, amask = sb("rope", [P, 2, TT, 2, 16]), sb("amask", [P, TT, 2 * T])
        cos, sin = rope[:, 0], rope[:, 1]
        n_rope = [0]
        turns = [(u, x) for u in range(UU) for x in range(2)]
        peak, minus, total, sunk, inv = (small[:, i] for i in range(5))

        def keys(u):
            return slice(0, 2 * T) if u < TT else slice(T, 2 * T)

        with nc.Block() as block:

            @block.sync
            def _(sp):
                sp.dma_start(rope[:, :, :, :, :], dram["rope"]).then_inc(sink_in, 16)
                sp.dma_start(amask[:, :, :], dram["amask"]).then_inc(sink_in, 16)
                sp.dma_start(sink[:, :], dram["sink"][layer].unsqueeze(0).broadcast_to([P, AH])).then_inc(sink_in, 16)

            @block.vector
            def _(dve):
                def link(ins):
                    n_rope[0] += 1
                    ins.then_inc(rope_step, 1)
                    dve.wait_ge(rope_step, n_rope[0])

                dve.wait_ge(sink_in, 48)
                half = [P, heads, 2, 16]
                for u in range(TT):
                    src = tok[:, u, Q_AT:Q_AT + heads * HD].rearrange("p (h a x i) -> p h a x i", h=heads, a=2, x=2)
                    dst = roped[:, u].rearrange("p (h a x i) -> p h a x i", h=heads, a=2, x=2)
                    ts = [tmp[:, k, u].rearrange("p (h a i) -> p h a i", h=heads, a=2) for k in range(2)]
                    c = cos[:, u].unsqueeze(1).broadcast_to(half)
                    s = sin[:, u].unsqueeze(1).broadcast_to(half)
                    dve.tensor_tensor(ts[0], src[:, :, :, 1], s, ALU.mult)
                    dve.tensor_tensor(ts[1], src[:, :, :, 0], s, ALU.mult)
                    dve.tensor_tensor(dst[:, :, :, 0], src[:, :, :, 0], c, ALU.mult)
                    link(dve.tensor_tensor(dst[:, :, :, 1], src[:, :, :, 1], c, ALU.mult))
                    dve.tensor_tensor(dst[:, :, :, 0], dst[:, :, :, 0], ts[0], ALU.subtract)
                    dve.tensor_tensor(dst[:, :, :, 1], dst[:, :, :, 1], ts[1], ALU.add).then_inc(roped_s, 1)

                def back(n):
                    u, h = units[n]
                    dve.wait_ge(totals, n + 1)
                    dve.tensor_tensor(total[:, n:n + 1], total[:, n:n + 1], sunk[:, n:n + 1], ALU.add).then_inc(added_up, 1)
                    dve.wait_ge(added_up, n + 1)
                    dve.reciprocal(inv[:, n:n + 1], total[:, n:n + 1]).then_inc(inverted, 1)
                    dve.wait_ge(summed, n + 1)
                    dve.wait_ge(inverted, n + 1)
                    dve.tensor_scalar(tok[:, u, Q_AT + h * HD:Q_AT + (h + 1) * HD], o_ps[:, n % 2, 0:HD],
                                      inv[:, n:n + 1], None, ALU.mult).then_inc(done, 1)

                def front(n):
                    u, h = units[n]
                    w = slice(0, 2 * T) if u < TT else slice(0, T)
                    dve.wait_ge(scored, n + 1)
                    if due(n - 1):
                        dve.wait_ge(raised, n - 1)
                    if u < TT:
                        ins = dve.scalar_tensor_tensor(s_sb[:, n % 2, w], s_ps[:, n % 2, w], HD ** -0.5, amask[:, u], ALU.mult, ALU.add)
                    else:
                        ins = dve.tensor_scalar(s_sb[:, n % 2, w], s_ps[:, n % 2, w], HD ** -0.5, None, ALU.mult)
                    ins.then_inc(masked, 1)
                    dve.wait_ge(masked, n + 1)
                    dve.tensor_reduce(peak[:, n:n + 1], s_sb[:, n % 2, w], AX.X, ALU.max).then_inc(peak_found, 1)
                    dve.wait_ge(peak_found, n + 1)
                    dve.tensor_scalar(minus[:, n:n + 1], peak[:, n:n + 1], sink[:, h:h + 1], -1.0, ALU.max, ALU.mult).then_inc(peaked, 1)

                for n in range(len(units) + 2):
                    if n >= 2:
                        back(n - 2)
                    if n < len(units):
                        front(n)

            @block.scalar
            def _(act):
                for n, (u, x) in enumerate(turns):
                    act.wait_ge(turned, n + 1)
                    if x == 0:
                        act.activation(q_t[:, u, 0:4], h_ps[:, x], ACT.Copy).then_inc(kept, 1)
                    else:
                        act.activation(q_t[:, u, 4:6], h_ps[:, x, 0:2], ACT.Copy)
                        act.activation(k_t[:, :, u * P:(u + 1) * P], h_ps[:, x, 2:4], ACT.Copy).then_inc(kept, 1)
                act.wait_ge(sink_in, 48)

                def raise_(n):
                    u, h = units[n]
                    w = slice(0, 2 * T) if u < TT else slice(0, T)
                    act.wait_ge(peaked, n + 1)
                    if due(n - 1):
                        act.wait_ge(p_turned, n - 1)
                    act.activation(p_sb[:, n % 2, w], s_sb[:, n % 2, w], ACT.Exp, bias=minus[:, n:n + 1],
                                   accum_out=total[:, n:n + 1]).then_inc(raised, 1)
                    act.activation(sunk[:, n:n + 1], sink[:, h:h + 1], ACT.Exp, bias=minus[:, n:n + 1]).then_inc(totals, 1)

                def keep(n):
                    u, _ = units[n]
                    w = slice(0, UU) if u < TT else slice(0, TT)
                    act.wait_ge(p_turned, n + 1)
                    if due(n - 1):
                        act.wait_ge(summed, n - 1)
                    act.activation(p_t[:, n % 2, w], t_ps[:, n % 2, w], ACT.Copy).then_inc(p_kept, 1)

                for n in range(len(units) + 1):
                    if n < len(units):
                        raise_(n)
                    if n >= 1:
                        keep(n - 1)

            @block.tensor
            def _(pe):
                for n, (u, x) in enumerate(turns):
                    if u < TT:
                        pe.wait_ge(roped_s, u + 1)
                    if due(n - 1):
                        pe.wait_ge(kept, n - 1)
                    for k in range(4):
                        a = (4 * x + k) * HD
                        src = roped[:, u, a:a + HD] if u < TT else tok[:, u, Q_AT + a:Q_AT + a + HD]
                        mm = pe.transpose(h_ps[:, x, k], src, core.ident)
                    mm.then_inc(turned, 1)
                pe.wait_ge(kept, len(turns))

                def score(n):
                    u, h = units[n]
                    if due(n - 1):
                        pe.wait_ge(masked, n - 1)
                    ks = keys(u)
                    pe.matmul(s_ps[:, n % 2, 0:ks.stop - ks.start], q_t[:, u, h], k_t[:, h // (AH // KV), ks],
                              start=True, stop=True).then_inc(scored, 1)

                def turn(n):
                    u, h = units[n]
                    pe.wait_ge(raised, n + 1)
                    if due(n - 1):
                        pe.wait_ge(p_kept, n - 1)
                    for k in range(UU if u < TT else TT):
                        mm = pe.transpose(t_ps[:, n % 2, k], p_sb[:, n % 2, k * P:(k + 1) * P], core.ident)
                    mm.then_inc(p_turned, 1)

                def weigh(n):
                    u, h = units[n]
                    pe.wait_ge(p_kept, n + 1)
                    if due(n - 1):
                        pe.wait_ge(done, n - 1)
                    tiles = range(UU) if u < TT else range(TT, UU)
                    for k, t in enumerate(tiles):
                        a = V_AT + (h // (AH // KV)) * HD
                        mm = pe.matmul(o_ps[:, n % 2, 0:HD], p_t[:, n % 2, k], tok[:, t, a:a + HD],
                                       start=(k == 0), stop=(k == len(tiles) - 1))
                    mm.then_inc(summed, 1)

                for n in range(len(units) + 2):
                    if n < len(units):
                        score(n)
                    if 1 <= n <= len(units):
                        turn(n - 1)
                    if n >= 2:
                        weigh(n - 2)


def project_out(core, layer, streams, dram, tok):
    nc = core.nc
    tag = f"po{layer}"
    n_tok = streams * T
    with ExitStack() as scope:
        sb = core.sbuf(scope, tag)
        ps = core.psum(scope, tag)
        ring = 3
        w = sb("w", [P, ring, DC, P])
        y_t = sb("y_t", [P, DC, n_tok])
        t_ps, o_ps = ps("t_ps", [P, 2, 512]), ps("o_ps", [P, 2, 512])
        w_in = [core.semaphore(f"wo_in{r}") for r in range(ring)]
        turned, kept, made, added = (core.semaphore(x) for x in ("y_turned_o", "y_kept_o", "out_made", "out_added"))
        with nc.Block() as block:

            @block.sync
            def _(sp):
                for j in range(DC):
                    if due(j - ring + 1):
                        sp.wait_ge(made, j - ring + 1)
                    sp.dma_start(w[:, j % ring], dram["w_out"][layer, j]).then_inc(w_in[j % ring], 16)

            @block.tensor
            def _(pe):
                for c in range(DC):
                    if due(c - 1):
                        pe.wait_ge(kept, c - 1)
                    for u in range(streams * TT):
                        mm = pe.transpose(t_ps[:, c % 2, u * P:(u + 1) * P], tok[:, u, MIXED_AT[c]:MIXED_AT[c] + P], core.ident)
                    mm.then_inc(turned, 1)
                pe.wait_ge(kept, DC)
                for j in range(DC):
                    pe.wait_ge(w_in[j % ring], 16 * (j // ring + 1))
                    if due(streams * (j - 1)):
                        pe.wait_ge(added, streams * (j - 1))
                    for c in range(DC):
                        mm = pe.matmul(o_ps[:, j % 2, 0:n_tok], w[:, j % ring, c], y_t[:, c], start=(c == 0), stop=(c == DC - 1))
                    mm.then_inc(made, 1)

            @block.scalar
            def _(act):
                for c in range(DC):
                    act.wait_ge(turned, c + 1)
                    act.activation(y_t[:, c], t_ps[:, c % 2, 0:n_tok], ACT.Copy).then_inc(kept, 1)

            @block.vector
            def _(dve):
                for j in range(DC):
                    dve.wait_ge(made, j + 1)
                    for s in range(streams):
                        cols = slice(s * T, (s + 1) * T)
                        dve.scalar_tensor_tensor(core.x[:, j, cols], o_ps[:, j % 2, cols], core.mod[:, 2 * DC + j, s:s + 1],
                                                 core.x[:, j, cols], ALU.mult, ALU.add).then_inc(added, 1)


def mixing(core, layer, need_ctx, dram):
    nc = core.nc
    tag = f"mx{layer}"
    streams = 2 if need_ctx else 1
    with ExitStack() as scope:
        sb = core.sbuf(scope, tag)
        tok = sb("tok", [P, UU, TOK_W])
        consts = sb("consts", [P, CONSTS])
        consts_in = core.semaphore("mix_consts_in")
        cst = {}
        at = 0
        for name, shape in MIX_CONSTS:
            n = int(np.prod(shape))
            cst[name] = consts[:, at:at + n]
            at += n
        cst["tri"] = [cst["tri"][:, d * P:(d + 1) * P] for d in range(2)]
        cst["neg"] = [cst["neg"][:, d * P:(d + 1) * P] for d in range(2)]
        cst["lvl"] = [cst["lvl"].rearrange("p (d s n) -> p d s n", d=2, s=6)[:, d] for d in range(2)]
        with ExitStack() as inner:
            heads_sb = core.sbuf(inner, tag)
            qkv = heads_sb("qkv", [P, UU, 3 * GDN_W])
            heads_t = heads_sb("heads_t", [HD, UU, 2 * GH, P])
            beta = heads_sb("beta", [P, UU, 2 * GH])
            decay_g = heads_sb("decay_g", [P, UU, 2 * GH])
            with ExitStack() as first:
                conv_in = core.sbuf(first, tag)("conv_in", [P, QKV_C, 2, T + 2 * PAD])
                with ExitStack() as hs:
                    core.h = core.sbuf(hs, tag)("h", [P, DC, 2 * T])
                    with nc.Block() as block:

                        @block.sync
                        def _(sp):
                            sp.dma_start(consts[:, :], dram["mix_consts"]).then_inc(consts_in, 16)
                            sp.wait_ge(consts_in, 16)

                    parts = [(slice(s * T, (s + 1) * T), [core.mod[:, c, s:s + 1] for c in range(DC)],
                              [core.gain[:, 0, c, s:s + 1] for c in range(DC)]) for s in range(2)]
                    normalize(core, tag + "n", slice(0, 2 * T), parts)
                    project_in(core, layer, dram, conv_in, tok)
                short_conv(core, layer, dram, conv_in, qkv, heads_t)
                core.end_stage()
            gdn_gates(core, layer, dram, tok, beta, decay_g)
            made = {
                "attn": heads_sb("attn", [P, UU, 2, GH, P]),
                "value": heads_sb("value", [P, UU, 2, GH, HD]),
                "key_t": heads_sb("key_t", [HD, UU, 2, GH, P]),
                "key_dec": heads_sb("key_dec", [P, UU, 2, GH, HD]),
                "grow": heads_sb("grow", [P, UU, 2 * GH]),
                "whole": heads_sb("whole", [HD, 2 * UU, 2 * GH]),
            }
            gdn_chunks(core, layer, cst, qkv, heads_t, beta, decay_g, made)
            core.end_stage()
            gdn_states(core, layer, need_ctx, heads_t, made)
            gdn_finish(core, layer, streams * TT, dram, tok, made)
        pooling(core, layer, streams, dram, tok)
        attention(core, layer, need_ctx, dram, tok)
        project_out(core, layer, streams, dram, tok)


def topk_and_gates(core, layer, stream, dram):
    nc = core.nc
    tag = f"pr{layer}{stream}"
    h = core.h
    with ExitStack() as scope:
        sb = core.sbuf(scope, tag)
        ps = core.psum(scope, tag)
        keys = sb("keys", [P, GROUPS, N_KEYS])
        top = sb("top", [P, TT, GROUPS, TOPK])
        top_i = sb("top_i", [P, TT, GROUPS, TOPK], U32)
        top_f = sb("top_f", [P, TT, GROUPS, TOPK])
        slot_gate = sb("slot_gate", [P, TT, SLOTS])
        slot_key = sb("slot_key", [P, 2, TT, SLOTS])
        slot_major = sb("slot_major", [P, 3, T])
        keys_in = core.semaphore("peer_keys_in")

        with ExitStack() as inner:
            sb1 = core.sbuf(inner, tag)
            ps1 = core.psum(inner, tag)
            wq = sb1("wq", [P, WQ_RING, DC, P])
            q_sb = sb1("q_sb", [P, 2, T])
            s_sb = sb1("s_sb", [P, 2, TT, N_KEYS])
            s_cut = sb1("s_cut", [P, TT, N_KEYS])
            q_ps = ps1("q_ps", [P, 2, 512])
            s_ps = ps1("s_ps", [P, 2, 512])
            wq_in = [core.semaphore(f"wq_in{r}") for r in range(WQ_RING)]
            q_made, q_copied = core.semaphore("q_made"), core.semaphore("q_copied")
            s_made, s_copied = core.semaphore("s_made"), core.semaphore("s_copied")
            picked, step = core.semaphore("picked"), core.semaphore("topk_step")
            with nc.Block() as block:

                @block.sync
                def _(sp):
                    sp.dma_start(keys[:, :, :], dram["keys"][layer]).then_inc(keys_in, 16)
                    for g in range(GROUPS):
                        if due(g - WQ_RING + 1):
                            sp.wait_ge(q_made, g - WQ_RING + 1)
                        sp.dma_start(wq[:, g % WQ_RING], dram["wq"][layer, g]).then_inc(wq_in[g % WQ_RING], 16)

                @block.tensor
                def _(pe):
                    def queries(g):
                        pe.wait_ge(wq_in[g % WQ_RING], 16 * (g // WQ_RING + 1))
                        if due(g - 1):
                            pe.wait_ge(q_copied, g - 1)
                        for c in range(DC):
                            mm = pe.matmul(q_ps[:, g % 2, 0:T], wq[:, g % WQ_RING, c], h[:, c, 0:T],
                                           start=(c == 0), stop=(c == DC - 1))
                        mm.then_inc(q_made, 1)

                    def scores(g):
                        if g == 0:
                            pe.wait_ge(keys_in, 16)
                        pe.wait_ge(q_copied, g + 1)
                        if due(g - 1):
                            pe.wait_ge(s_copied, g - 1)
                        for u in range(TT):
                            mm = pe.matmul(s_ps[:, g % 2, u * P:(u + 1) * P], q_sb[:, g % 2, u * P:(u + 1) * P],
                                           keys[:, g], start=True, stop=True)
                        mm.then_inc(s_made, 1)

                    queries(0)
                    for g in range(GROUPS):
                        if g + 1 < GROUPS:
                            queries(g + 1)
                        scores(g)

                @block.scalar
                def _(act):
                    for g in range(GROUPS):
                        act.wait_ge(q_made, g + 1)
                        if due(g - 1):
                            act.wait_ge(s_made, g - 1)
                        act.activation(q_sb[:, g % 2, :], q_ps[:, g % 2, 0:T], ACT.Copy).then_inc(q_copied, 1)
                        act.wait_ge(s_made, g + 1)
                        if due(g - 1):
                            act.wait_ge(picked, g - 1)
                        act.activation(s_sb[:, g % 2], s_ps[:, g % 2, 0:T], ACT.Copy).then_inc(s_copied, 1)

                @block.vector
                def _(dve):
                    for g in range(GROUPS):
                        dve.wait_ge(s_copied, g + 1)
                        k = 6 * g
                        for u in range(TT):
                            dve.max(top[:, u, g, 0:8], s_sb[:, g % 2, u]).then_inc(step, 1)
                        for u in range(TT):
                            dve.wait_ge(step, k + u + 1)
                            dve.match_replace(s_cut[:, u], top[:, u, g, 0:8], s_sb[:, g % 2, u], LOWEST).then_inc(step, 1)
                            dve.max_index(top_i[:, u, g, 0:8], top[:, u, g, 0:8], s_sb[:, g % 2, u])
                        for u in range(TT):
                            dve.wait_ge(step, k + u + 3)
                            dve.max(top[:, u, g, 8:16], s_cut[:, u]).then_inc(step, 1)
                        for u in range(TT):
                            dve.wait_ge(step, k + u + 5)
                            last = dve.max_index(top_i[:, u, g, 8:16], top[:, u, g, 8:16], s_cut[:, u])
                        last.then_inc(picked, 1)

        with ExitStack() as inner:
            sb1 = core.sbuf(inner, tag)
            ps1 = core.psum(inner, tag)
            cand = sb1("cand", [P, TT * HEADS, TOPK, TOPK])
            cut = sb1("cut", [P, TT * HEADS, TOPK * TOPK])
            best = sb1("best", [P, TT, HEADS, TOPK])
            best_i = sb1("best_i", [P, TT, HEADS, TOPK], U32)
            rank_u = sb1("rank_u", [P, 2, TT, HEADS, TOPK], U32)
            rank = sb1("rank", [P, 2, TT, HEADS, TOPK])
            hot = sb1("hot", [P, 2, TT, HEADS, TOPK, TOPK])
            sums = sb1("sums", [P, TT, HEADS])
            inv = sb1("inv", [P, TT, HEADS])
            t_ps = ps1("t_ps", [P, 3, 512])
            step, shifted = core.semaphore("best_step"), core.semaphore("gates_shifted")
            expd, ready = core.semaphore("gates_exp"), core.semaphore("slots_ready")
            turned = core.semaphore("slots_turned")
            n_steps = [0]
            halves = top[:, :, :, :].rearrange("p u (h s) k -> p u h s k", s=2)
            halves_i = top_f[:, :, :, :].rearrange("p u (h s) k -> p u h s k", s=2)
            with nc.Block() as block:

                @block.vector
                def _(dve):
                    def link(ins):
                        n_steps[0] += 1
                        ins.then_inc(step, 1)
                        dve.wait_ge(step, n_steps[0])

                    dve.tensor_copy(top_f[:, :, :, :], top_i[:, :, :, :])
                    pairs = [(u, hd) for u in range(TT) for hd in range(HEADS)]
                    for u, hd in pairs:
                        a = halves[:, u, hd, 0].unsqueeze(2).broadcast_to([P, TOPK, TOPK])
                        b = halves[:, u, hd, 1].unsqueeze(1).broadcast_to([P, TOPK, TOPK])
                        last = dve.tensor_tensor(cand[:, u * HEADS + hd], a, b, ALU.add)
                    link(last)
                    flat = cand[:, :, :, :].rearrange("p n a b -> p n (a b)")
                    for u, hd in pairs:
                        last = dve.max(best[:, u, hd, 0:8], flat[:, u * HEADS + hd])
                    link(last)
                    for u, hd in pairs:
                        n = u * HEADS + hd
                        dve.max_index(best_i[:, u, hd, 0:8], best[:, u, hd, 0:8], flat[:, n])
                        last = dve.match_replace(cut[:, n], best[:, u, hd, 0:8], flat[:, n], LOWEST)
                    link(last)
                    for u, hd in pairs:
                        last = dve.max(best[:, u, hd, 8:16], cut[:, u * HEADS + hd])
                    link(last)
                    dve.tensor_tensor(slot_gate[:, :, :].rearrange("p u (h k) -> p u h k", h=HEADS), best[:, :, :, :],
                                      best[:, :, :, 0:1].broadcast_to([P, TT, HEADS, TOPK]),
                                      ALU.subtract).then_inc(shifted, 1)
                    for u, hd in pairs:
                        last = dve.max_index(best_i[:, u, hd, 8:16], best[:, u, hd, 8:16], cut[:, u * HEADS + hd])
                    link(last)
                    dve.tensor_scalar(rank_u[:, 0], best_i[:, :, :, :], 4, None, ALU.logical_shift_right)
                    link(dve.tensor_scalar(rank_u[:, 1], best_i[:, :, :, :], TOPK - 1, None, ALU.bitwise_and))
                    link(dve.tensor_copy(rank[:, :, :, :, :], rank_u[:, :, :, :, :]))
                    iota16 = core.iota[:, 0:TOPK]
                    for s in range(2):
                        for u in range(TT):
                            r = rank[:, s, u].unsqueeze(3).broadcast_to([P, HEADS, TOPK, TOPK])
                            i = iota16.unsqueeze(1).unsqueeze(1).broadcast_to([P, HEADS, TOPK, TOPK])
                            last = dve.tensor_tensor(hot[:, s, u], r, i, ALU.is_equal)
                    link(last)
                    for s in range(2):
                        for u in range(TT):
                            k = halves_i[:, u, :, s].unsqueeze(2).broadcast_to([P, HEADS, TOPK, TOPK])
                            last = dve.tensor_tensor(hot[:, s, u], hot[:, s, u], k, ALU.mult)
                    link(last)
                    for s in range(2):
                        dve.tensor_reduce(slot_key[:, s], hot[:, s].rearrange("p u h k r -> p (u h k) r"), AX.X, ALU.add)
                    dve.wait_ge(expd, 1)
                    g4 = slot_gate[:, :, :].rearrange("p u (h k) -> p u h k", h=HEADS)
                    link(dve.tensor_reduce(sums[:, :, :], g4, AX.X, ALU.add))
                    link(dve.reciprocal(inv[:, :, :], sums[:, :, :]))
                    dve.tensor_tensor(g4, g4, inv[:, :, :].unsqueeze(3).broadcast_to([P, TT, HEADS, TOPK]),
                                      ALU.mult).then_inc(ready, 1)
                    dve.wait_ge(turned, 1)
                    link(dve.tensor_copy(slot_major[:, :, :], t_ps[:, :, 0:T]))

                @block.scalar
                def _(act):
                    act.wait_ge(shifted, 1)
                    act.activation(slot_gate[:, :, :], slot_gate[:, :, :], ACT.Exp).then_inc(expd, 1)

                @block.tensor
                def _(pe):
                    pe.wait_ge(ready, 1)
                    for u in range(TT):
                        pe.transpose(t_ps[:, 0, u * P:(u + 1) * P], slot_key[:, 0, u], core.ident)
                        pe.transpose(t_ps[:, 1, u * P:(u + 1) * P], slot_key[:, 1, u], core.ident)
                        mm = pe.transpose(t_ps[:, 2, u * P:(u + 1) * P], slot_gate[:, u], core.ident)
                    mm.then_inc(turned, 1)

        with ExitStack() as inner:
            sb1 = core.sbuf(inner, tag)
            ps1 = core.psum(inner, tag)
            first = sb1("first", [P, ROUND, N_KEYS])
            second = sb1("second", [P, ROUND, N_KEYS])
            stage = sb1("stage", [P, N_KEYS, P])
            w_ps = ps1("w_ps", [P, 2, 4, P])
            hots, outer = core.semaphore("hots_ready"), core.semaphore("outer_done")
            staged, stored = core.semaphore("w_staged"), core.semaphore("w_stored")
            rounds = P // ROUND
            with nc.Block() as block:

                @block.vector
                def _(dve):
                    for u in range(TT):
                        def round_(r):
                            for x in range(ROUND):
                                t = r * ROUND + (x + u * P)
                                if x % 4 == 0:
                                    if due((u * rounds + r) * 2 + (x // 4 - 1)):
                                        dve.wait_ge(outer, (u * rounds + r) * 2 + (x // 4 - 1))
                                dve.tensor_scalar(first[:, x], core.iota, slot_major[:, 0, bass.ds(t, 1)],
                                                  slot_major[:, 2, bass.ds(t, 1)], ALU.is_equal, ALU.mult)
                                last = dve.tensor_scalar(second[:, x], core.iota, slot_major[:, 1, bass.ds(t, 1)], None,
                                                         ALU.is_equal)
                                if x % 4 == 3:
                                    last.then_inc(hots, 1)

                        if u == 0:
                            round_(0)
                        with dve.Fori(1 if u == 0 else 0, rounds) as r:
                            round_(r)

                @block.tensor
                def _(pe):
                    for u in range(TT):
                        def round_(r):
                            for x in range(ROUND):
                                if x % 4 == 0:
                                    pe.wait_ge(hots, (u * rounds + r) * 2 + (x // 4 + 1))
                                    if due((u * rounds + r) * 2 + (x // 4 - 1)):
                                        pe.wait_ge(staged, (u * rounds + r) * 2 + (x // 4 - 1))
                                mm = pe.matmul(w_ps[:, x // 4, x % 4], first[:, x], second[:, x], start=True, stop=True)
                                if x % 4 == 3:
                                    mm.then_inc(outer, 1)

                        if u == 0:
                            round_(0)
                        with pe.Fori(1 if u == 0 else 0, rounds) as r:
                            round_(r)

                @block.scalar
                def _(act):
                    for u in range(TT):
                        def round_(r):
                            for q in range(2):
                                act.wait_ge(outer, (u * rounds + r) * 2 + (q + 1))
                                t = r * ROUND + 4 * q
                                act.activation(stage[:, :, bass.ds(t, 4)], w_ps[:, q].rearrange("p t i -> p i t"),
                                               ACT.Copy).then_inc(staged, 1)

                        if u > 0:
                            act.wait_ge(stored, 16 * u)
                        with act.Fori(0, rounds) as r:
                            round_(r)

                @block.sync
                def _(sp):
                    for u in range(TT):
                        sp.wait_ge(staged, 2 * rounds * (u + 1))
                        sp.dma_start(dram["gates"][:, :, u * P:(u + 1) * P].rearrange("j i t -> i j t"),
                                     stage[:, :, :]).then_inc(stored, 16)
                    sp.wait_ge(stored, 16 * TT)


def experts(core, layer, stream, dram):
    nc = core.nc
    tag = f"ex{layer}{stream}"
    with ExitStack() as scope:
        sb = core.sbuf(scope, tag)
        ps = core.psum(scope, tag)
        h_hi, h_lo = sb("h_hi", [P, DC, T], F32R), sb("h_lo", [P, DC, T], F32R)
        u_raw, v_raw = sb("u_raw", [P, 2, 2, D]), sb("v_raw", [P, 2, 2, D])
        w_raw = sb("w_raw", [P, 2, 2, T])
        u_hi, u_lo = sb("u_hi", [P, 2, D], F32R), sb("u_lo", [P, 2, D], F32R)
        v_hi, v_lo = sb("v_hi", [P, 2, D], F32R), sb("v_lo", [P, 2, D], F32R)
        gel, prod = sb("gel", [P, 2, T]), sb("prod", [P, 2, T])
        p_hi, p_lo = sb("p_hi", [P, 2, T], F32R), sb("p_lo", [P, 2, T], F32R)
        y_sb = sb("y_sb", [P, TT, D])
        a_ps = ps("a_ps", [P, 2, 512])
        y_ps = ps("y_ps", [P, TT, 2, 512])
        t_ps = ps("t_ps", [P, 2, 512])
        u_in = [core.semaphore(f"u_in{r}") for r in range(2)]
        v_in = [core.semaphore(f"v_in{r}") for r in range(2)]
        w_in = [core.semaphore(f"w_in{r}") for r in range(2)]
        h_hi_done, h_split = core.semaphore("h_hi_done"), core.semaphore("h_split")
        u_hi_done, v_hi_done = core.semaphore("u_hi_done"), core.semaphore("v_hi_done")
        u_split, v_split = core.semaphore("u_split"), core.semaphore("v_split")
        scored, gelud, gated = core.semaphore("scored"), core.semaphore("gelud"), core.semaphore("gated")
        p_hi_done, p_split, summed = core.semaphore("p_hi_done"), core.semaphore("p_split"), core.semaphore("summed")
        y_out, y_turned, added = core.semaphore("y_out"), core.semaphore("y_turned"), core.semaphore("added")
        pairs = N_KEYS // 2
        cols = slice(stream * T, (stream + 1) * T)

        def quads(eng, body):
            for n in range(4):
                body(0, n // 2, n % 2)
            with eng.Fori(1, pairs // 2) as q:
                for n in range(4):
                    body(q, n // 2, n % 2)

        with nc.Block() as block:

            @block.sync
            def _(sp):
                def load(q, r):
                    m = 2 * q + r
                    if due(2 * m - 2):
                        sp.wait_ge(u_split, 2 * m - 2)
                    sp.dma_start(u_raw[:, r], dram["u"][layer, bass.ds(m, 1)].rearrange("o p b n -> p (o b) n")).then_inc(u_in[r], 16)
                    if due(2 * m - 2):
                        sp.wait_ge(v_split, 2 * m - 2)
                    sp.dma_start(v_raw[:, r], dram["v"][layer, bass.ds(m, 1)].rearrange("o p b n -> p (o b) n")).then_inc(v_in[r], 16)
                    if due(2 * m - 2):
                        sp.wait_ge(gated, 2 * m - 2)
                    sp.dma_start(w_raw[:, r], dram["gates"][bass.ds(2 * m, 2)].rearrange("b i t -> i b t")).then_inc(w_in[r], 16)

                load(0, 0)
                load(0, 1)
                with sp.Fori(1, pairs // 2) as q:
                    load(q, 0)
                    load(q, 1)

            @block.scalar
            def _(act):
                act.activation(h_hi[:, :, :], core.h[:, :, 0:T], ACT.Copy).then_inc(h_hi_done, 1)

                def body(q, r, b):
                    i = 4 * q + (2 * r + b)
                    act.wait_ge(u_in[r], 16 * q + 16)
                    if due(i - 1):
                        act.wait_ge(scored, i - 1)
                    act.activation(u_hi[:, b], u_raw[:, r, b], ACT.Copy).then_inc(u_hi_done, 1)
                    if not (isinstance(i, int) and i < 1):
                        gelu_and_high(i - 1, 1 - b)
                    act.wait_ge(v_in[r], 16 * q + 16)
                    if due(i - 1):
                        act.wait_ge(summed, i - 1)
                    act.activation(v_hi[:, b], v_raw[:, r, b], ACT.Copy).then_inc(v_hi_done, 1)

                def gelu_and_high(i, b):
                    act.wait_ge(scored, i + 1)
                    if due(i - 1):
                        act.wait_ge(gated, i - 1)
                    act.activation(gel[:, b], a_ps[:, b, 0:T], ACT.Gelu).then_inc(gelud, 1)
                    act.wait_ge(gated, i + 1)
                    if due(i - 1):
                        act.wait_ge(summed, i - 1)
                    act.activation(p_hi[:, b], prod[:, b], ACT.Copy).then_inc(p_hi_done, 1)

                quads(act, body)
                gelu_and_high(N_KEYS - 1, 1)
                for u in range(TT):
                    for k in range(2):
                        act.wait_ge(summed, N_KEYS)
                        act.activation(y_sb[:, u, k * 512:(k + 1) * 512], y_ps[:, u, k], ACT.Copy).then_inc(y_out, 1)

            @block.vector
            def _(dve):
                dve.wait_ge(h_hi_done, 1)
                dve.tensor_tensor(h_lo[:, :, :], core.h[:, :, 0:T], h_hi[:, :, :].bitcast(F32), ALU.subtract).then_inc(h_split, 1)

                def body(q, r, b):
                    i = 4 * q + (2 * r + b)
                    dve.wait_ge(u_hi_done, i + 1)
                    if due(i - 1):
                        dve.wait_ge(scored, i - 1)
                    dve.tensor_tensor(u_lo[:, b], u_raw[:, r, b], u_hi[:, b].bitcast(F32), ALU.subtract).then_inc(u_split, 1)
                    if not (isinstance(i, int) and i < 1):
                        gate(i - 1, 1 - b, r if b else 1 - r, q if b or r else q - 1)
                    dve.wait_ge(v_hi_done, i + 1)
                    if due(i - 1):
                        dve.wait_ge(summed, i - 1)
                    dve.tensor_tensor(v_lo[:, b], v_raw[:, r, b], v_hi[:, b].bitcast(F32), ALU.subtract).then_inc(v_split, 1)

                def gate(i, b, r, q):
                    dve.wait_ge(gelud, i + 1)
                    dve.wait_ge(w_in[r], 16 * q + 16)
                    if due(i - 1):
                        dve.wait_ge(p_split, i - 1)
                    dve.tensor_tensor(prod[:, b], gel[:, b], w_raw[:, r, b], ALU.mult).then_inc(gated, 1)
                    dve.wait_ge(p_hi_done, i + 1)
                    if due(i - 1):
                        dve.wait_ge(summed, i - 1)
                    dve.tensor_tensor(p_lo[:, b], prod[:, b], p_hi[:, b].bitcast(F32), ALU.subtract).then_inc(p_split, 1)

                quads(dve, body)
                gate(N_KEYS - 1, 1, 1, pairs // 2 - 1)
                for c in range(DC):
                    dve.wait_ge(y_turned, c + 1)
                    dve.scalar_tensor_tensor(core.x[:, c, cols], t_ps[:, c % 2, 0:T], core.mod[:, 5 * DC + c, stream:stream + 1],
                                             core.x[:, c, cols], ALU.mult, ALU.add).then_inc(added, 1)

            @block.tensor
            def _(pe):
                pe.wait_ge(h_split, 1)

                def score(i, b):
                    pe.wait_ge(u_split, i + 1)
                    if due(i - 1):
                        pe.wait_ge(gelud, i - 1)
                    n = 0
                    for lhs, rhs in ((u_hi, h_hi), (u_hi, h_lo), (u_lo, h_hi)):
                        for c in range(DC):
                            mm = pe.matmul(a_ps[:, b, 0:T], lhs[:, b, c * P:(c + 1) * P], rhs[:, c, :],
                                           start=(n == 0), stop=(n == 3 * DC - 1))
                            n += 1
                    mm.then_inc(scored, 1)

                def project(i, b, first, last):
                    pe.wait_ge(p_split, i + 1)
                    pe.wait_ge(v_split, i + 1)
                    for u in range(TT):
                        for n, (lhs, rhs) in enumerate(((p_hi, v_hi), (p_hi, v_lo), (p_lo, v_hi))):
                            for k in range(2):
                                mm = pe.matmul(y_ps[:, u, k], lhs[:, b, u * P:(u + 1) * P], rhs[:, b, k * 512:(k + 1) * 512],
                                               start=(first and n == 0), stop=(last and n == 2), skip_group_check=True)
                    mm.then_inc(summed, 1)

                def body(q, r, b):
                    i = 4 * q + (2 * r + b)
                    score(i, b)
                    if not (isinstance(i, int) and i < 1):
                        project(i - 1, 1 - b, isinstance(i, int) and i == 1, False)

                quads(pe, body)
                project(N_KEYS - 1, 1, False, True)
                pe.wait_ge(y_out, 2 * TT)
                for c in range(DC):
                    if due(c - 1):
                        pe.wait_ge(added, c - 1)
                    for u in range(TT):
                        mm = pe.transpose(t_ps[:, c % 2, u * P:(u + 1) * P], y_sb[:, u, c * P:(c + 1) * P], core.ident)
                    mm.then_inc(y_turned, 1)
def constants():
    i, j = np.arange(P)[None, :], np.arange(P)[:, None]
    same = i // HD == j // HD
    tri = np.stack([same & (j <= i), same & (j >= i)], 1)
    neg = np.where(tri, 0.0, MASKED)
    lvl = np.zeros((P, 2, 6, P))
    for k in range(6):
        s = 2 ** k
        lvl[:, 0, k] = ((i // s) % 2 == 1) & (j // s == i // s - 1)
        lvl[:, 1, k] = ((i // s) % 2 == 0) & (j // s == i // s + 1)
    mix = np.concatenate([same, tri.reshape(P, -1), neg.reshape(P, -1), lvl.reshape(P, -1)], 1)
    base = np.concatenate([np.eye(P), np.ones((P, P)), np.broadcast_to(np.arange(P), (P, P))], 1)
    t = np.arange(T)
    band = np.zeros((T, 4, T))
    for g, w in enumerate(POOL_WINDOWS):
        lo, hi = np.clip(t - w // 2, 0, T), np.clip(t + w - w // 2, 0, T)
        inside = (t[:, None] >= lo[None]) & (t[:, None] < hi[None])
        band[:, g] = inside / (hi - lo)[None] - np.eye(T)
    band = band.reshape(TT, P, 4, T).transpose(1, 2, 0, 3)
    amask = np.zeros((T, 2 * T))
    amask[:, :T] = np.where(np.abs(t[:, None] - t[None]) <= WINDOW, 0.0, MASKED)
    amask = amask.reshape(TT, P, 2 * T).transpose(1, 0, 2)
    f32 = np.float32
    pos = np.stack([t // GRID_W, t % GRID_W], -1).astype(f32)
    inv = np.power(f32(ROPE_BASE), -np.arange(ROPE_PAIRS, dtype=f32) / f32(ROPE_PAIRS))
    ang = pos[:, :, None] * inv
    rope = np.stack([np.cos(ang), np.sin(ang)]).reshape(2, TT, P, 2, ROPE_PAIRS).transpose(2, 0, 1, 3, 4)
    found = {"base_consts": base, "mix_consts": mix, "band": band, "amask": amask, "rope": rope}
    return {k: np.ascontiguousarray(v, dtype=f32) for k, v in found.items()}


def layout(a):
    n = a["w_in"].shape[0]
    cols = lambda v: v.reshape(*v.shape[:-1], DC, P)
    r = {}
    r["x_t"] = np.concatenate([a["x"][0], a["ctx"][0]], 0).T.reshape(DC, P, 2 * T).transpose(1, 0, 2)
    r["c2"] = np.stack([a["c"][0], a["c_ctx"]], -1).reshape(DC, P, 2).transpose(1, 0, 2)
    r["w_ada"] = a["w_ada"].reshape(n, DC, P, 6, D).transpose(0, 3, 2, 1, 4)
    r["b_ada"] = a["b_ada"].reshape(n, 6 * DC, P).transpose(0, 2, 1)
    r["norms"] = np.stack([cols(a["norm1"]), cols(a["norm2"])], 1).transpose(0, 3, 1, 2)
    r["norm_f"] = cols(a["norm_f"]).T
    q0, q1 = POOL_W, POOL_W + 3 * GDN_W
    r["w_qkv"] = a["w_in"][:, :, q0:q1].reshape(n, DC, P, QKV_C, P).transpose(0, 3, 2, 1, 4)
    r["w_tok"] = np.concatenate([a["w_in"][:, :, :q0], a["w_in"][:, :, q1:]], 2).reshape(n, DC, P, TOK_W).transpose(0, 2, 1, 3)
    r["conv_w"] = a["conv_w"].reshape(n, CONV_K, QKV_C, P).transpose(0, 3, 2, 1)
    r["a_log"] = a["a_log"].reshape(n, 2 * GH)
    r["dt_bias"] = a["dt_bias"].reshape(n, 2 * GH)
    r["gdn_norm"], r["pool_scale"], r["sink"] = a["gdn_norm"], a["pool_scale"], a["sink"]
    r["w_pool"] = a["w_pool"].transpose(0, 2, 1, 3)
    r["w_out"] = a["w_out"].reshape(n, DC, P, DC, P).transpose(0, 3, 2, 1, 4)
    r["wq"] = a["peer_wq"].reshape(n, DC, P, GROUPS, P).transpose(0, 3, 2, 1, 4)
    r["keys"] = a["peer_keys"].reshape(n, GROUPS, N_KEYS, P).transpose(0, 3, 1, 2)
    u = a["peer_u"].reshape(n, N_KEYS, N_KEYS // 2, 2, DC, P)
    r["u"] = u.transpose(0, 2, 5, 3, 4, 1).reshape(n, N_KEYS // 2, P, 2, D)
    r["v"] = a["peer_v"].reshape(n, N_KEYS, N_KEYS // 2, 2, D).transpose(0, 2, 1, 3, 4)
    return {k: np.ascontiguousarray(v) for k, v in r.items()}


def hybrid_backbone(nc, depth, dram, out):
    dram = dict(dram)
    dram["gates"] = nc.dram_tensor("peer_gates", [N_KEYS, N_KEYS, T], F32, kind="Internal").ap()
    with ExitStack() as scope:
        core = Core(nc)
        sb = core.sbuf(scope, "core")
        core.x = sb("x", [P, DC, 2 * T])
        core.mod = sb("mod", [P, 6 * DC, 2])
        core.gain = sb("gain", [P, 2, DC, 2])
        base = sb("base", [P, 3 * P])
        last_gain = sb("norm_f", [P, DC])
        core.ident, core.ones, core.iota = base[:, 0:P], base[:, P:2 * P], base[:, 2 * P:3 * P]
        loaded = core.semaphore("loaded")
        with nc.Block() as block:

            @block.sync
            def _(sp):
                sp.dma_start(base[:, :], dram["base_consts"]).then_inc(loaded, 16)
                sp.dma_start(last_gain[:, :], dram["norm_f"]).then_inc(loaded, 16)
                sp.dma_start(core.x[:, :, :], dram["x_t"]).then_inc(loaded, 16)
                sp.wait_ge(loaded, 48)

        core.end_stage()
        for layer in range(depth):
            need_ctx = layer < depth - 1
            modulation(core, layer, dram)
            core.end_stage()
            mixing(core, layer, need_ctx, dram)
            core.end_stage()
            for stream in range(2 if need_ctx else 1):
                cols = slice(stream * T, (stream + 1) * T)
                with ExitStack() as hs:
                    core.h = core.sbuf(hs, f"pe{layer}{stream}")("h", [P, DC, T])
                    parts = [(slice(0, T), [core.mod[:, 3 * DC + c, stream:stream + 1] for c in range(DC)],
                              [core.gain[:, 1, c, stream:stream + 1] for c in range(DC)])]
                    normalize(core, f"pn{layer}{stream}", cols, parts)
                    topk_and_gates(core, layer, stream, dram)
                    core.end_stage()
                    experts(core, layer, stream, dram)
                    core.end_stage()
        with ExitStack() as hs:
            core.h = core.sbuf(hs, "final")("h", [P, DC, T])
            normalize(core, "fn", slice(0, T), [(slice(0, T), None, [last_gain[:, c:c + 1] for c in range(DC)])])
            stored = core.semaphore("stored")
            with nc.Block() as block:

                @block.sync
                def _(sp):
                    sp.dma_start(out, core.h[:, :, :]).then_inc(stored, 16)
                    sp.wait_ge(stored, 16)


def kernel(**inputs):
    import concourse.bacc as bacc
    from concourse.bass_utils import run_bass_kernel_spmd

    arrays = layout({k: np.asarray(v) for k, v in inputs.items()})
    arrays.update(constants())
    nc = bacc.Bacc("TRN2", target_bir_lowering=False, num_devices=1)
    dram = {k: nc.dram_tensor(f"in_{k}", v.shape, mybir.dt.from_np(v.dtype), kind="ExternalInput").ap()
            for k, v in arrays.items()}
    out = nc.dram_tensor("out_t", [P, DC, T], F32, kind="ExternalOutput").ap()
    hybrid_backbone(nc, inputs["w_in"].shape[0], dram, out)
    r = run_bass_kernel_spmd(nc, [{f"in_{k}": v for k, v in arrays.items()}], core_ids=[0])
    y = np.asarray(r.results[0]["out_t"])
    return np.ascontiguousarray(y.transpose(2, 1, 0).reshape(1, T, D))
```

```python
from contextlib import ExitStack

import numpy as np

import concourse.bass as bass
from concourse import mybir

F32, F32R, U32 = mybir.dt.float32, mybir.dt.float32r, mybir.dt.uint32
ALU, ACT, AX = mybir.AluOpType, mybir.ActivationFunctionType, mybir.AxisListType

P = 128
D = 1024
DC = D // P
T = 256
TT = T // P
EPS = 1e-6
HEADS, N_KEYS, TOPK = 8, 128, 16
GROUPS = 2 * HEADS
SLOTS = HEADS * TOPK
ROUND = 16
QUADS = ROUND // 4
WQ_RING = 3
WADA_RING = 5
LOWEST = -3.0e38
MASKED = -1.0e30

UU = 2 * TT
HD = 64
POOL_W, GDN_W, ATT_W = 256, 384, 384
POOL_WINDOWS = (2, 4, 8, 16)
GH, AH, KV = GDN_W // HD, ATT_W // HD, 2
QKV_C = 3 * GDN_W // P
CONV_K = 5
PAD = CONV_K // 2
Z_AT = POOL_W
BA_AT = Z_AT + GDN_W
Q_AT = BA_AT + 4 * GH
V_AT = Q_AT + ATT_W + KV * HD
TOK_W = V_AT + KV * HD
MIXED_AT = [P * c for c in range(5)] + [Q_AT + P * c for c in range(3)]
MIX_CONSTS = (("chunk_ones", (P,)), ("tri", (2, P)), ("neg", (2, P)), ("lvl", (2, 6, P)))
CONSTS = sum(int(np.prod(s)) for _, s in MIX_CONSTS)
WINDOW = 128
GRID_W, ROPE_BASE, ROPE_PAIRS = 64, 10000.0, 16


def due(count):
    return not isinstance(count, int) or count > 0


class Core:

    def __init__(self, nc):
        self.nc, self.semaphores, self.stage = nc, {}, 0

    def semaphore(self, name):
        assert name not in self.semaphores, name
        self.semaphores[name] = self.nc.alloc_semaphore(name=f"{name}_{self.stage}")
        return self.semaphores[name]

    def end_stage(self):
        self.nc.clear_and_free_semaphores(list(self.semaphores.values()))
        self.nc.all_engine_barrier()
        self.semaphores, self.stage = {}, self.stage + 1

    def sbuf(self, scope, tag):
        return lambda name, shape, dt=F32: scope.enter_context(self.nc.sbuf_tensor(f"{tag}_{name}", shape, dt))

    def psum(self, scope, tag):
        return lambda name, shape, dt=F32: scope.enter_context(self.nc.psum_tensor(f"{tag}_{name}", shape, dt))


def normalize(core, tag, cols, parts):
    nc = core.nc
    n = cols.stop - cols.start
    with ExitStack() as scope:
        sb = core.sbuf(scope, tag)
        ps = core.psum(scope, tag)
        sq = sb("sq", [P, DC, n])
        rstd = sb("rstd", [P, n])
        s_ps = ps("s_ps", [P, n])
        squared, sums = core.semaphore("squared"), core.semaphore("square_sums")
        mean, root, scaled = core.semaphore("mean_square"), core.semaphore("rms"), core.semaphore("h_scaled")
        inverse = core.semaphore("rstd_ready")
        with nc.Block() as block:

            @block.scalar
            def _(act):
                for c in range(DC):
                    act.activation(sq[:, c], core.x[:, c, cols], ACT.Square).then_inc(squared, 1)
                act.wait_ge(mean, 1)
                act.activation(rstd[:, :], rstd[:, :], ACT.Sqrt).then_inc(root, 1)
                for c in range(DC):
                    for i, (to, shift, _) in enumerate(parts):
                        if shift is not None:
                            act.wait_ge(scaled, c * len(parts) + i + 1)
                            act.activation(core.h[:, c, to], core.h[:, c, to], ACT.Identity, bias=shift[c])

            @block.tensor
            def _(pe):
                for c in range(DC):
                    pe.wait_ge(squared, c + 1)
                    mm = pe.matmul(s_ps[:, :], core.ones, sq[:, c], start=(c == 0), stop=(c == DC - 1))
                mm.then_inc(sums, 1)

            @block.vector
            def _(dve):
                dve.wait_ge(sums, 1)
                dve.tensor_scalar(rstd[:, :], s_ps[:, :], 1.0 / D, EPS, ALU.mult, ALU.add).then_inc(mean, 1)
                dve.wait_ge(root, 1)
                dve.reciprocal(rstd[:, :], rstd[:, :]).then_inc(inverse, 1)
                dve.wait_ge(inverse, 1)
                for c in range(DC):
                    for to, _, g in parts:
                        src = slice(cols.start + to.start, cols.start + to.stop)
                        dve.scalar_tensor_tensor(core.h[:, c, to], core.x[:, c, src], g[c], rstd[:, to],
                                                 ALU.mult, ALU.mult).then_inc(scaled, 1)


def modulation(core, layer, dram):
    nc = core.nc
    tag = f"mod{layer}"
    parts = 6
    with ExitStack() as scope:
        sb = core.sbuf(scope, tag)
        ps = core.psum(scope, tag)
        halves = 2 * parts
        w = sb("w", [P, WADA_RING, DC, 512])
        cc = sb("cc", [P, DC, 2])
        bias = sb("bias", [P, parts * DC])
        norms = sb("norms", [P, 2, DC])
        rows = sb("rows", [2, halves, 512])
        row_ps = ps("row_ps", [2, 2, 512])
        m_ps = ps("m_ps", [P, parts * DC, 2])
        w_in = [core.semaphore(f"wada_in{r}") for r in range(WADA_RING)]
        cols_in, activated = core.semaphore("mod_cols_in"), core.semaphore("c_activated")
        used, copied = core.semaphore("wada_used"), core.semaphore("mod_row_copied")
        turned, step = core.semaphore("mod_turned"), core.semaphore("mod_step")
        with nc.Block() as block:

            @block.sync
            def _(sp):
                sp.dma_start(cc[:, :, :], dram["c2"]).then_inc(cols_in, 16)
                sp.dma_start(bias[:, :], dram["b_ada"][layer]).then_inc(cols_in, 16)
                sp.dma_start(norms[:, :, :], dram["norms"][layer]).then_inc(cols_in, 16)
                for n in range(halves):
                    if due(n - WADA_RING + 1):
                        sp.wait_ge(used, n - WADA_RING + 1)
                    sp.dma_start(w[:, n % WADA_RING], dram["w_ada"][layer, n]).then_inc(w_in[n % WADA_RING], 16)

            @block.scalar
            def _(act):
                act.wait_ge(cols_in, 48)
                act.activation(cc[:, :, :], cc[:, :, :], ACT.Silu).then_inc(activated, 1)
                for n in range(halves):
                    act.wait_ge(used, n + 1)
                    act.activation(rows[:, n], row_ps[:, n % 2], ACT.Copy).then_inc(copied, 1)

            @block.tensor
            def _(pe):
                def turn(n):
                    pe.wait_ge(copied, n + 1)
                    for j in range(4):
                        mm = pe.transpose(m_ps[:, 4 * n + j], rows[:, n, j * P:(j + 1) * P], core.ident[0:2, 0:2])
                    mm.then_inc(turned, 1)

                pe.wait_ge(activated, 1)
                for n in range(halves):
                    pe.wait_ge(w_in[n % WADA_RING], 16 * (n // WADA_RING + 1))
                    if due(n - 1):
                        pe.wait_ge(copied, n - 1)
                    for c in range(DC):
                        mm = pe.matmul(row_ps[:, n % 2], cc[:, c], w[:, n % WADA_RING, c], start=(c == 0), stop=(c == DC - 1))
                    mm.then_inc(used, 1)
                    if n:
                        turn(n - 1)
                turn(halves - 1)

            @block.vector
            def _(dve):
                dve.wait_ge(turned, halves)
                dve.tensor_tensor(core.mod[:, :, :], m_ps[:, :, :],
                                  bias[:, :].unsqueeze(2).broadcast_to([P, parts * DC, 2]), ALU.add).then_inc(step, 1)
                dve.wait_ge(step, 1)
                for n in range(2):
                    scale = core.mod[:, (3 * n + 1) * DC:(3 * n + 2) * DC]
                    dve.tensor_scalar(core.gain[:, n], scale, 1.0, None, ALU.add).then_inc(step, 1)
                dve.wait_ge(step, 3)
                for n in range(2):
                    dve.tensor_tensor(core.gain[:, n], core.gain[:, n],
                                      norms[:, n].unsqueeze(2).broadcast_to([P, DC, 2]), ALU.mult)


def project_in(core, layer, dram, conv_in, tok):
    nc = core.nc
    tag = f"pi{layer}"
    with ExitStack() as scope:
        sb = core.sbuf(scope, tag)
        ps = core.psum(scope, tag)
        ring = 3
        wf = sb("wf", [P, ring, DC, P])
        wt = sb("wt", [P, DC, TOK_W])
        o_ps = ps("o_ps", [P, 4, 512])
        wf_in = [core.semaphore(f"wf_in{r}") for r in range(ring)]
        wt_in, made = core.semaphore("wt_in"), core.semaphore("proj_made")
        copied = [core.semaphore("proj_copied_act"), core.semaphore("proj_copied_dve")]
        padded = core.semaphore("conv_padded")
        width = TOK_W // 4
        products = QKV_C + 4 * UU

        def place(n):
            if n < QKV_C:
                return conv_in[:, n, :, PAD:PAD + T], o_ps[:, n % 4].rearrange("p (s t) -> p s t", s=2)
            u, k = divmod(n - QKV_C, 4)
            return tok[:, u, k * width:(k + 1) * width], o_ps[:, n % 4, 0:width]

        with nc.Block() as block:

            @block.gpsimd
            def _(pool):
                pool.memset(conv_in[:, :, :, 0:PAD], 0.0)
                pool.memset(conv_in[:, :, :, PAD + T:2 * PAD + T], 0.0).then_inc(padded, 1)

            @block.sync
            def _(sp):
                for j in range(QKV_C):
                    if j == ring:
                        sp.dma_start(wt[:, :, :], dram["w_tok"][layer]).then_inc(wt_in, 16)
                    if due(j - ring + 1):
                        sp.wait_ge(made, j - ring + 1)
                    sp.dma_start(wf[:, j % ring], dram["w_qkv"][layer, j]).then_inc(wf_in[j % ring], 16)

            @block.tensor
            def _(pe):
                for n in range(products):
                    b = n % 4
                    if due((n - 4) // 2 + 1):
                        pe.wait_ge(copied[n % 2], (n - 4) // 2 + 1)
                    if n < QKV_C:
                        pe.wait_ge(wf_in[n % ring], 16 * (n // ring + 1))
                        for c in range(DC):
                            mm = pe.matmul(o_ps[:, b], wf[:, n % ring, c], core.h[:, c, :], start=(c == 0), stop=(c == DC - 1))
                    else:
                        if n == QKV_C:
                            pe.wait_ge(wt_in, 16)
                        u, k = divmod(n - QKV_C, 4)
                        for c in range(DC):
                            mm = pe.matmul(o_ps[:, b, 0:width], core.h[:, c, u * P:(u + 1) * P],
                                           wt[:, c, k * width:(k + 1) * width], start=(c == 0), stop=(c == DC - 1))
                    mm.then_inc(made, 1)

            @block.scalar
            def _(act):
                for n in range(0, products, 2):
                    act.wait_ge(made, n + 1)
                    act.activation(*place(n), ACT.Copy).then_inc(copied[0], 1)

            @block.vector
            def _(dve):
                for n in range(1, products, 2):
                    dve.wait_ge(made, n + 1)
                    dve.tensor_copy(*place(n)).then_inc(copied[1], 1)


def short_conv(core, layer, dram, conv_in, qkv, heads_t):
    nc = core.nc
    tag = f"sc{layer}"
    with ExitStack() as scope:
        sb = core.sbuf(scope, tag)
        ps = core.psum(scope, tag)
        conv = sb("conv", [P, QKV_C, 2, T])
        taps = sb("taps", [P, QKV_C, CONV_K])
        sq = sb("sq", [P, 2, 2 * GDN_W])
        norm = sb("norm", [P, UU, 2 * GH])
        t_ps = ps("t_ps", [P, 2, UU, P])
        h_ps = ps("h_ps", [HD, 3, 4, P])
        taps_in, step, convolved = core.semaphore("taps_in"), core.semaphore("conv_step"), core.semaphore("convolved")
        silud, turned, back = core.semaphore("conv_silu"), core.semaphore("conv_turned"), core.semaphore("conv_token_major")
        squares, roots, unit = core.semaphore("norm_squares"), core.semaphore("norm_roots"), core.semaphore("unit_qk")
        turned_h, kept_h = core.semaphore("heads_turned"), core.semaphore("heads_kept")
        n_steps = [0]
        with nc.Block() as block:

            @block.sync
            def _(sp):
                sp.dma_start(taps[:, :, :], dram["conv_w"][layer]).then_inc(taps_in, 16)

            @block.vector
            def _(dve):
                def link(ins):
                    n_steps[0] += 1
                    ins.then_inc(step, 1)
                    dve.wait_ge(step, n_steps[0])

                dve.wait_ge(taps_in, 16)
                for j0 in range(0, QKV_C, 3):
                    for k in range(CONV_K):
                        for j in range(j0, j0 + 3):
                            src = conv_in[:, j, :, k:k + T]
                            if k == 0:
                                ins = dve.tensor_scalar(conv[:, j], src, taps[:, j, 0:1], None, ALU.mult)
                            else:
                                ins = dve.scalar_tensor_tensor(conv[:, j], src, taps[:, j, k:k + 1], conv[:, j], ALU.mult, ALU.add)
                            if k == CONV_K - 1:
                                ins.then_inc(convolved, 1)
                        if k < CONV_K - 1:
                            link(ins)
                dve.wait_ge(back, QKV_C)
                for u in range(UU):
                    link(dve.tensor_tensor(sq[:, u % 2], qkv[:, u, 0:2 * GDN_W], qkv[:, u, 0:2 * GDN_W], ALU.mult))
                    link(dve.tensor_reduce(norm[:, u], sq[:, u % 2].rearrange("p (h d) -> p h d", d=HD), AX.X, ALU.add))
                dve.tensor_scalar(norm[:, :, :], norm[:, :, :], EPS, None, ALU.add).then_inc(squares, 1)
                dve.wait_ge(roots, 1)
                link(dve.reciprocal(norm[:, :, :], norm[:, :, :]))
                link(dve.tensor_scalar(norm[:, :, 0:GH], norm[:, :, 0:GH], HD ** -0.5, None, ALU.mult))
                for u in range(UU):
                    rows = qkv[:, u, 0:2 * GDN_W].rearrange("p (h d) -> p h d", d=HD)
                    dve.tensor_tensor(rows, rows, norm[:, u].unsqueeze(2).broadcast_to([P, 2 * GH, HD]),
                                      ALU.mult).then_inc(unit, 1)

            @block.scalar
            def _(act):
                for j in range(QKV_C):
                    act.wait_ge(convolved, j + 1)
                    act.activation(conv[:, j], conv[:, j], ACT.Silu).then_inc(silud, 1)
                    if j:
                        act.wait_ge(turned, j)
                        act.activation(qkv[:, :, (j - 1) * P:j * P], t_ps[:, (j - 1) % 2], ACT.Copy).then_inc(back, 1)
                act.wait_ge(turned, QKV_C)
                act.activation(qkv[:, :, (QKV_C - 1) * P:QKV_C * P], t_ps[:, (QKV_C - 1) % 2], ACT.Copy).then_inc(back, 1)
                act.wait_ge(squares, 1)
                act.activation(norm[:, :, :], norm[:, :, :], ACT.Sqrt).then_inc(roots, 1)
                for n in range(3 * UU):
                    u, g = divmod(n, 3)
                    act.wait_ge(turned_h, n + 1)
                    act.activation(heads_t[:, u, 4 * g:4 * g + 4], h_ps[:, g], ACT.Copy).then_inc(kept_h, 1)

            @block.tensor
            def _(pe):
                for j in range(QKV_C):
                    pe.wait_ge(silud, j + 1)
                    if due(j - 1):
                        pe.wait_ge(back, j - 1)
                    for u in range(UU):
                        mm = pe.transpose(t_ps[:, j % 2, u], conv[:, j, u // TT, (u % TT) * P:(u % TT + 1) * P], core.ident)
                    mm.then_inc(turned, 1)
                for n in range(3 * UU):
                    u, g = divmod(n, 3)
                    pe.wait_ge(unit, u + 1)
                    if due(n - 2):
                        pe.wait_ge(kept_h, n - 2)
                    for x in range(4):
                        hd = 4 * g + x
                        mm = pe.transpose(h_ps[:, g, x], qkv[:, u, hd * HD:(hd + 1) * HD], core.ident)
                    mm.then_inc(turned_h, 1)


def gdn_gates(core, layer, dram, tok, beta, decay_g):
    nc = core.nc
    tag = f"gg{layer}"
    with ExitStack() as scope:
        sb = core.sbuf(scope, tag)
        rate, bias = sb("rate", [P, 2 * GH]), sb("bias", [P, 2 * GH])
        a, neg = sb("a", [P, UU, 2 * GH]), sb("neg", [P, UU, 2 * GH])
        rows_in, step = core.semaphore("gate_rows_in"), core.semaphore("gate_step")
        biased, logged, done = core.semaphore("gate_biased"), core.semaphore("gate_logged"), core.semaphore("gate_act")
        full = [P, UU, 2 * GH]
        b0 = BA_AT
        with nc.Block() as block:

            @block.sync
            def _(sp):
                sp.dma_start(rate[:, :], dram["a_log"][layer].unsqueeze(0).broadcast_to([P, 2 * GH])).then_inc(rows_in, 16)
                sp.dma_start(bias[:, :], dram["dt_bias"][layer].unsqueeze(0).broadcast_to([P, 2 * GH])).then_inc(rows_in, 16)

            @block.vector
            def _(dve):
                dve.wait_ge(rows_in, 32)
                dve.tensor_tensor(a[:, :, :], tok[:, :, b0 + 2 * GH:b0 + 4 * GH], bias[:, :].unsqueeze(1).broadcast_to(full),
                                  ALU.add).then_inc(step, 1)
                dve.wait_ge(step, 1)
                dve.scalar_tensor_tensor(neg[:, :, :], a[:, :, :], -1.0, a[:, :, :], ALU.mult, ALU.min).then_inc(biased, 1)
                dve.wait_ge(logged, 1)
                dve.scalar_tensor_tensor(a[:, :, :], a[:, :, :], 0.0, neg[:, :, :], ALU.max, ALU.add).then_inc(step, 1)
                dve.wait_ge(step, 2)
                dve.scalar_tensor_tensor(decay_g[:, :, :], a[:, :, :], -1.0, rate[:, :].unsqueeze(1).broadcast_to(full),
                                         ALU.mult, ALU.mult)

            @block.scalar
            def _(act):
                act.wait_ge(rows_in, 32)
                act.activation(beta[:, :, :], tok[:, :, b0:b0 + 2 * GH], ACT.Sigmoid)
                act.activation(rate[:, :], rate[:, :], ACT.Exp)
                act.wait_ge(biased, 1)
                act.activation(neg[:, :, :], neg[:, :, :], ACT.Exp).then_inc(done, 1)
                act.wait_ge(done, 1)
                act.activation(neg[:, :, :], neg[:, :, :], ACT.Ln, bias=1.0).then_inc(logged, 1)


def gdn_chunks(core, layer, cst, qkv, heads_t, beta, decay_g, made):
    nc = core.nc
    tag = f"gc{layer}"
    groups = [(u, d) for u in range(UU) for d in range(2)]
    levels = 5
    with ExitStack() as scope:
        sb = core.sbuf(scope, tag)
        ps = core.psum(scope, tag)
        three = [P, 3, P]
        gcol, gtot = sb("gcol", [P, UU, 2 * GH]), sb("gtot", [P, UU, 2 * GH])
        bexp, kexp = sb("bexp", [P, UU, 2 * GH]), sb("kexp", [P, UU, 2 * GH])
        kbe, vb = sb("kbe", [P, 2, 2, 3, HD]), sb("vb", [P, 2, 2, 3, HD])
        work = [{k: sb(f"{k}{f}", three) for k in ("dif", "lt", "x", "xt", "y")} for f in range(2)]
        cut = [sb(f"cut{f}", [P, levels + 1, 3, P]) for f in range(2)]
        bank = [ps(f"bank{f}", [P, 4, 512]) for f in range(2)]
        S = core.semaphore
        sums, sums_out, decays, scaled = S("g_sums"), S("g_sums_out"), S("g_decays"), S("g_scaled")
        two = lambda name: [S(f"{name}{f}") for f in range(2)]
        products, lower, cuts = two("products"), two("lower"), two("cuts")
        dstep, decayed = two("dif_step"), two("decayed")
        start_t, start_turned, start_x = two("start_t"), two("start_turned"), two("start_x")
        y_made, y_kept, xy_made, xyt_made = two("y_made"), two("y_kept"), two("xy_made"), two("xyt_made")
        x_new, xt_new, solved, kept = two("x_new"), two("xt_new"), two("solved"), two("kept")
        rhs, rhs_step = S("rhs"), S("rhs_step")
        tri, neg, lvl, chunk_ones = cst["tri"], cst["neg"], cst["lvl"], cst["chunk_ones"]

        def b3(f, k, n=P, rows=P):
            return bank[f][0:rows, k, 0:3 * n].rearrange("p (h n) -> p h n", h=3)

        with nc.Block() as block:

            @block.tensor
            def _(pe):
                g_ps, w_ps = bank[0][:, 0], bank[1][0:HD, 0]
                for u in range(UU):
                    for d in range(2):
                        a = u * 24 + d * GH
                        pe.matmul(g_ps[:, a:a + GH], tri[d], decay_g[:, u, d * GH:(d + 1) * GH], start=True, stop=True)
                    pe.matmul(g_ps[:, u * 24 + 12:u * 24 + 24], chunk_ones, decay_g[:, u], start=True, stop=True)
                    for x in range(2):
                        a = (2 * u + x) * 12
                        mm = pe.matmul(w_ps[:, a:a + 12], chunk_ones[:, x * HD:(x + 1) * HD], decay_g[:, u], start=True, stop=True)
                mm.then_inc(sums, 1)
                pe.wait_ge(sums_out, 2)

                def setup(n, f):
                    u, d = groups[n]
                    if due(2 * n):
                        pe.wait_ge(kept[f], 2 * n)
                    if due((levels - 1) * n):
                        pe.wait_ge(x_new[f], (levels - 1) * n)
                    if due(levels * n):
                        pe.wait_ge(xt_new[f], levels * n)
                    for k, h in enumerate(range(3 * f, 3 * f + 3)):
                        pe.matmul(b3(f, 0)[:, k], heads_t[:, u, GH + h], heads_t[:, u, GH + h], start=True, stop=True)
                        pe.matmul(b3(f, 1)[:, k], heads_t[:, u, GH + h], heads_t[:, u, h], start=True, stop=True)
                        c = d * GH + h
                        pe.matmul(b3(f, 2)[:, k], decay_g[:, u, c:c + 1].broadcast_to([P, P]), tri[d], start=True, stop=True)
                        mm = pe.matmul(b3(f, 3)[:, k], beta[:, u, c:c + 1].broadcast_to([P, P]), core.ident, start=True, stop=True)
                    mm.then_inc(products[f], 1)

                def turn(n, f):
                    pe.wait_ge(start_t[f], n + 1)
                    for k in range(3):
                        mm = pe.transpose(b3(f, 1)[:, k], work[f]["xt"][:, k], core.ident)
                    mm.then_inc(start_turned[f], 1)

                def times_x(n, v, f):
                    pe.wait_ge(cuts[f], (levels + 1) * n + v + 2)
                    if v == 0:
                        pe.wait_ge(start_x[f], n + 1)
                    else:
                        if due((levels - 1) * n + v):
                            pe.wait_ge(x_new[f], (levels - 1) * n + v)
                    if due(levels * n + v):
                        pe.wait_ge(y_kept[f], levels * n + v)
                    for k in range(3):
                        mm = pe.matmul(b3(f, 0)[:, k], cut[f][:, v + 1, k], work[f]["x"][:, k], start=True, stop=True)
                    mm.then_inc(y_made[f], 1)

                def x_times(n, v, f):
                    pe.wait_ge(y_kept[f], levels * n + v + 1)
                    if v:
                        if due(levels * n + v):
                            pe.wait_ge(xt_new[f], levels * n + v)
                    if v < levels - 1:
                        for k in range(3):
                            mm = pe.matmul(b3(f, 1)[:, k], work[f]["xt"][:, k], work[f]["y"][:, k], start=True, stop=True)
                        mm.then_inc(xy_made[f], 1)
                    for k in range(3):
                        mm = pe.matmul(b3(f, 2)[:, k], work[f]["y"][:, k], work[f]["xt"][:, k], start=True, stop=True)
                    mm.then_inc(xyt_made[f], 1)

                def solve(n, f):
                    pe.wait_ge(xt_new[f], levels * (n + 1))
                    pe.wait_ge(rhs, n + 1)
                    for k in range(3):
                        pe.matmul(b3(f, 3, HD)[:, k], work[f]["xt"][:, k], vb[:, n % 2, f, k], start=True, stop=True)
                        mm = pe.matmul(b3(f, 0, P, HD)[:, k], kbe[:, n % 2, f, k], work[f]["xt"][:, k], start=True, stop=True)
                    mm.then_inc(solved[f], 1)

                for n in range(len(groups)):
                    for f in range(2):
                        setup(n, f)
                    for f in range(2):
                        turn(n, f)
                    for v in range(levels):
                        for f in range(2):
                            times_x(n, v, f)
                        for f in range(2):
                            x_times(n, v, f)
                    for f in range(2):
                        solve(n, f)

            @block.vector
            def _(dve):
                dve.wait_ge(sums, 1)
                g_ps = bank[0][:, 0, 0:UU * 24].rearrange("p (u n) -> p u n", u=UU)
                dve.tensor_copy(gcol[:, :, :], g_ps[:, :, 0:12])
                dve.tensor_copy(gtot[:, :, :], g_ps[:, :, 12:24]).then_inc(sums_out, 1)
                dve.wait_ge(sums_out, 2)
                dve.tensor_tensor(kexp[:, :, :], gtot[:, :, :], gcol[:, :, :], ALU.subtract).then_inc(decays, 1)
                dve.wait_ge(scaled, 1)
                dve.tensor_tensor(bexp[:, :, :], beta[:, :, :], made["grow"][:, :, :], ALU.mult).then_inc(rhs_step, 1)

                def decay(n, f):
                    u, d = groups[n]
                    w = work[f]
                    dve.wait_ge(products[f], n + 1)
                    c = d * GH + 3 * f
                    dve.tensor_tensor(w["dif"][:, :, :], b3(f, 2), gcol[:, u, c:c + 3].unsqueeze(2).broadcast_to(three),
                                      ALU.subtract).then_inc(dstep[f], 1)

                def mask(n, f):
                    d = groups[n][1]
                    w = work[f]
                    dve.wait_ge(dstep[f], 4 * n + 1)
                    dve.scalar_tensor_tensor(w["dif"][:, :, :], w["dif"][:, :, :], 0.0, neg[d].unsqueeze(1).broadcast_to(three),
                                             ALU.min, ALU.add).then_inc(dstep[f], 1)

                def weigh(n, f):
                    u, d = groups[n]
                    w = work[f]
                    dve.wait_ge(decayed[f], n + 1)
                    dve.tensor_tensor(w["lt"][:, :, :], b3(f, 0), w["dif"][:, :, :], ALU.mult).then_inc(dstep[f], 1)
                    dve.tensor_tensor(made["attn"][:, u, d, 3 * f:3 * f + 3], b3(f, 1), w["dif"][:, :, :], ALU.mult).then_inc(dstep[f], 1)
                    dve.wait_ge(dstep[f], 4 * n + 3)
                    dve.tensor_tensor(w["lt"][:, :, :], w["lt"][:, :, :], b3(f, 3), ALU.mult).then_inc(lower[f], 1)

                def begin(n, f):
                    dve.wait_ge(cuts[f], (levels + 1) * n + 1)
                    dve.tensor_tensor(work[f]["xt"][:, :, :], core.ident.unsqueeze(1).broadcast_to(three), cut[f][:, 0],
                                      ALU.subtract).then_inc(start_t[f], 1)

                def update(n, v, f):
                    w = work[f]
                    if v < levels - 1:
                        dve.wait_ge(xy_made[f], (levels - 1) * n + v + 1)
                        if v == 0:
                            dve.wait_ge(start_x[f], n + 1)
                        else:
                            if due((levels - 1) * n + v):
                                dve.wait_ge(x_new[f], (levels - 1) * n + v)
                        dve.tensor_tensor(w["x"][:, :, :], w["x"][:, :, :], b3(f, 1), ALU.subtract).then_inc(x_new[f], 1)
                    dve.wait_ge(xyt_made[f], levels * n + v + 1)
                    if v == 0:
                        dve.wait_ge(start_t[f], n + 1)
                    else:
                        if due(levels * n + v):
                            dve.wait_ge(xt_new[f], levels * n + v)
                    dve.tensor_tensor(w["xt"][:, :, :], w["xt"][:, :, :], b3(f, 2), ALU.subtract).then_inc(xt_new[f], 1)

                for n in range(len(groups)):
                    for f in range(2):
                        if n:
                            if due((levels + 1) * n):
                                dve.wait_ge(cuts[f], (levels + 1) * n)
                            if due(n):
                                dve.wait_ge(solved[f], n)
                        decay(n, f)
                    for f in range(2):
                        mask(n, f)
                    for f in range(2):
                        weigh(n, f)
                    for f in range(2):
                        begin(n, f)
                    for v in range(levels):
                        for f in range(2):
                            update(n, v, f)

            @block.scalar
            def _(act):
                act.wait_ge(sums, 1)
                act.activation(made["whole"][:, :, :], bank[1][0:HD, 0, 0:2 * UU * 12].rearrange("p (c n) -> p c n", c=2 * UU),
                               ACT.Exp).then_inc(sums_out, 1)
                act.wait_ge(decays, 1)
                act.activation(kexp[:, :, :], kexp[:, :, :], ACT.Exp)
                act.activation(made["grow"][:, :, :], gcol[:, :, :], ACT.Exp).then_inc(scaled, 1)
                for n, (u, d) in enumerate(groups):
                    for f in range(2):
                        act.wait_ge(dstep[f], 4 * n + 2)
                        act.activation(work[f]["dif"][:, :, :], work[f]["dif"][:, :, :], ACT.Exp).then_inc(decayed[f], 1)
                    for f in range(2):
                        act.wait_ge(start_turned[f], n + 1)
                        act.activation(work[f]["x"][:, :, :], b3(f, 1), ACT.Copy).then_inc(start_x[f], 1)
                    for v in range(levels):
                        for f in range(2):
                            act.wait_ge(y_made[f], levels * n + v + 1)
                            if due(levels * n + v):
                                act.wait_ge(xyt_made[f], levels * n + v)
                            act.activation(work[f]["y"][:, :, :], b3(f, 0), ACT.Copy).then_inc(y_kept[f], 1)
                    for f in range(2):
                        act.wait_ge(solved[f], n + 1)
                        act.activation(made["value"][:, u, d, 3 * f:3 * f + 3], b3(f, 3, HD), ACT.Copy).then_inc(kept[f], 1)
                        act.activation(made["key_t"][:, u, d, 3 * f:3 * f + 3], b3(f, 0, P, HD), ACT.Copy).then_inc(kept[f], 1)

            @block.gpsimd
            def _(pool):
                def sides(n):
                    u, d = groups[n]
                    six = [P, GH, HD]
                    for f in range(2):
                        if due(n - 1):
                            pool.wait_ge(solved[f], n - 1)
                    k = qkv[:, u, GDN_W:2 * GDN_W].rearrange("p (h e) -> p h e", e=HD)
                    v = qkv[:, u, 2 * GDN_W:3 * GDN_W].rearrange("p (h e) -> p h e", e=HD)
                    c = slice(d * GH, (d + 1) * GH)
                    pool.tensor_tensor(kbe[:, n % 2].rearrange("p f h e -> p (f h) e"), k, bexp[:, u, c].unsqueeze(2).broadcast_to(six), ALU.mult)
                    pool.tensor_tensor(made["key_dec"][:, u, d], k, kexp[:, u, c].unsqueeze(2).broadcast_to(six), ALU.mult)
                    pool.tensor_tensor(vb[:, n % 2].rearrange("p f h e -> p (f h) e"), v, beta[:, u, c].unsqueeze(2).broadcast_to(six),
                                       ALU.mult).then_inc(rhs, 1)

                pool.wait_ge(rhs_step, 1)
                for n, (u, d) in enumerate(groups):
                    sides(n)
                    for v in range(levels + 1):
                        for f in range(2):
                            if v == 0:
                                pool.wait_ge(lower[f], n + 1)
                                if due(n):
                                    pool.wait_ge(start_t[f], n)
                                if due(levels * n):
                                    pool.wait_ge(y_made[f], levels * n)
                            pool.tensor_tensor(cut[f][:, v], work[f]["lt"][:, :, :], lvl[d][:, v].unsqueeze(1).broadcast_to(three),
                                               ALU.mult).then_inc(cuts[f], 1)


def gdn_states(core, layer, need_ctx, heads_t, made):
    nc = core.nc
    tag = f"gs{layer}"
    with ExitStack() as scope:
        sb = core.sbuf(scope, tag)
        ps = core.psum(scope, tag)
        state = [sb(f"state{d}", [HD, GH, HD]) for d in range(2)]
        new = [sb(f"new{d}", [P, GH, HD]) for d in range(2)]
        part = [sb(f"part{d}", [P, GH, HD]) for d in range(2)]
        bank = [ps(f"bank{d}", [P, 4, 512]) for d in range(2)]
        S = core.semaphore
        two = lambda name: [S(f"{name}{d}") for d in range(2)]
        zeroed, read, corrected = two("state_zeroed"), two("state_read"), two("value_corrected")
        added, decayed, stated, outed = two("chunk_added"), two("state_decayed"), two("state_new"), two("out_part")
        out_done = two("out_done")
        steps = 2 * T // HD

        def place(n, d):
            ch = n % 4 if d == 0 else 3 - n % 4
            u = (TT if n < 4 else 0) + ch // 2
            return u, HD * (ch % 2), n >= 4 or need_ctx, 2 * u + ch % 2

        def b6(d, k, a, rows=HD):
            return bank[d][a:a + rows, k, 0:GH * HD].rearrange("p (h e) -> p h e", h=GH)

        with nc.Block() as block:

            @block.tensor
            def _(pe):
                for n in range(steps):
                    for d in range(2):
                        u, a, out, _ = place(n, d)
                        pe.wait_ge(zeroed[d], 1)
                        if due(n):
                            pe.wait_ge(stated[d], n)
                        if n:
                            if due(n):
                                pe.wait_ge(out_done[d], n)
                        for h in range(GH):
                            mm = pe.matmul(b6(d, 0, a)[:, h], made["key_t"][:, u, d, h, a:a + HD], state[d][:, h], start=True, stop=True)
                        if out:
                            for h in range(GH):
                                mm = pe.matmul(b6(d, 1, a)[:, h], heads_t[:, u, h, a:a + HD], state[d][:, h], start=True, stop=True)
                        mm.then_inc(read[d], 1)
                    for d in range(2):
                        u, a, out, _ = place(n, d)
                        pe.wait_ge(corrected[d], n + 1)
                        for h in range(GH):
                            mm = pe.matmul(b6(d, 2, 0)[:, h], made["key_dec"][a:a + HD, u, d, h], new[d][a:a + HD, h], start=True, stop=True)
                        if out:
                            for h in range(GH):
                                mm = pe.matmul(b6(d, 3, a)[:, h], made["attn"][a:a + HD, u, d, h, a:a + HD], new[d][a:a + HD, h],
                                               start=True, stop=True)
                        mm.then_inc(added[d], 1)

            @block.vector
            def _(dve):
                for d in range(2):
                    dve.memset(state[d][:, :, :], 0.0).then_inc(zeroed[d], 1)
                six = [HD, GH, HD]
                for n in range(steps):
                    for d in range(2):
                        u, a, out, c = place(n, d)
                        dve.wait_ge(read[d], n + 1)
                        dve.tensor_tensor(new[d][a:a + HD], made["value"][a:a + HD, u, d], b6(d, 0, a), ALU.subtract).then_inc(corrected[d], 1)
                    for d in range(2):
                        u, a, out, c = place(n, d)
                        dve.wait_ge(zeroed[d], 1)
                        if due(n):
                            dve.wait_ge(stated[d], n)
                        dve.tensor_tensor(state[d][:, :, :], state[d][:, :, :],
                                          made["whole"][:, c, d * GH:(d + 1) * GH].unsqueeze(2).broadcast_to(six),
                                          ALU.mult).then_inc(decayed[d], 1)
                        if out:
                            if due(n):
                                dve.wait_ge(out_done[d], n)
                            dve.tensor_tensor(part[d][a:a + HD], b6(d, 1, a),
                                              made["grow"][a:a + HD, u, d * GH:(d + 1) * GH].unsqueeze(2).broadcast_to(six),
                                              ALU.mult).then_inc(outed[d], 1)
                        else:
                            dve.engine_nop().then_inc(outed[d], 1)
                    for d in range(2):
                        u, a, out, c = place(n, d)
                        dve.wait_ge(added[d], n + 1)
                        dve.wait_ge(decayed[d], n + 1)
                        dve.tensor_tensor(state[d][:, :, :], state[d][:, :, :], b6(d, 2, 0), ALU.add).then_inc(stated[d], 1)
                        dve.wait_ge(outed[d], n + 1)
                        if out:
                            dve.wait_ge(corrected[d], n + 1)
                            dve.tensor_tensor(made["value"][a:a + HD, u, d], part[d][a:a + HD], b6(d, 3, a), ALU.add).then_inc(out_done[d], 1)
                        else:
                            dve.engine_nop().then_inc(out_done[d], 1)


def gdn_finish(core, layer, tiles, dram, tok, made):
    nc = core.nc
    tag = f"gf{layer}"
    with ExitStack() as scope:
        sb = core.sbuf(scope, tag)
        gain = sb("gain", [P, HD])
        sq = sb("sq", [P, tiles, GH, HD])
        n2 = sb("n2", [P, tiles, GH])
        z = sb("z", [P, tiles, GDN_W])
        gain_in, step = core.semaphore("gdn_gain_in"), core.semaphore("finish_step")
        squares, roots, gated = core.semaphore("out_squares"), core.semaphore("out_roots"), core.semaphore("z_silu")
        n_steps = [0]
        full = [P, tiles * GH, HD]
        with nc.Block() as block:

            @block.sync
            def _(sp):
                sp.dma_start(gain[:, :], dram["gdn_norm"][layer].unsqueeze(0).broadcast_to([P, HD])).then_inc(gain_in, 16)

            @block.scalar
            def _(act):
                act.activation(z[:, :, :], tok[:, 0:tiles, Z_AT:Z_AT + GDN_W], ACT.Silu).then_inc(gated, 1)
                act.wait_ge(squares, 1)
                act.activation(n2[:, :, :], n2[:, :, :], ACT.Sqrt).then_inc(roots, 1)

            @block.vector
            def _(dve):
                def link(ins):
                    n_steps[0] += 1
                    ins.then_inc(step, 1)
                    dve.wait_ge(step, n_steps[0])

                o = made["value"][:, 0:tiles, 0]
                link(dve.tensor_tensor(o, o, made["value"][:, 0:tiles, 1], ALU.add))
                link(dve.tensor_tensor(sq[:, :, :, :], o, o, ALU.mult))
                link(dve.tensor_reduce(n2[:, :, :], sq[:, :, :, :], AX.X, ALU.add))
                dve.tensor_scalar(n2[:, :, :], n2[:, :, :], 1.0 / HD, EPS, ALU.mult, ALU.add).then_inc(squares, 1)
                dve.wait_ge(roots, 1)
                link(dve.reciprocal(n2[:, :, :], n2[:, :, :]))
                link(dve.tensor_tensor(o, o, n2[:, :, :].unsqueeze(3).broadcast_to([P, tiles, GH, HD]), ALU.mult))
                dve.wait_ge(gain_in, 16)
                g = gain[:, :].unsqueeze(1).unsqueeze(1).broadcast_to([P, tiles, GH, HD])
                link(dve.tensor_tensor(o, o, g, ALU.mult))
                dve.wait_ge(gated, 1)
                dve.tensor_tensor(tok[:, 0:tiles, Z_AT:Z_AT + GDN_W], o.rearrange("p u h e -> p u (h e)"),
                                  z[:, :, :], ALU.mult)


def pooling(core, layer, streams, dram, tok):
    nc = core.nc
    tag = f"pl{layer}"
    with ExitStack() as scope:
        sb = core.sbuf(scope, tag)
        ps = core.psum(scope, tag)
        w = sb("w", [HD, 4, HD])
        scale = sb("scale", [P, POOL_W])
        pooled = sb("pooled", [HD, streams, 4, T])
        a_ps = ps("a_ps", [HD, 2, 2, T])
        o_ps = ps("o_ps", [P, 2, 512])
        rows_in, summed = core.semaphore("pool_rows_in"), core.semaphore("pool_summed")
        kept, made, done = core.semaphore("pool_kept"), core.semaphore("pool_made"), core.semaphore("pool_scaled")
        band = sb("band", [P, 4, TT, T])
        with nc.Block() as block:

            @block.sync
            def _(sp):
                sp.dma_start(w[:, :, :], dram["w_pool"][layer]).then_inc(rows_in, 16)
                sp.dma_start(band[:, :, :, :], dram["band"]).then_inc(rows_in, 16)
                sp.dma_start(scale[:, :], dram["pool_scale"][layer].unsqueeze(0).broadcast_to([P, POOL_W])).then_inc(rows_in, 16)

            @block.tensor
            def _(pe):
                pe.wait_ge(rows_in, 48)
                for n in range(2 * streams):
                    s, b = divmod(n, 2)
                    if due(n - 1):
                        pe.wait_ge(kept, n - 1)
                    for x in range(2):
                        g = 2 * b + x
                        for k in range(TT):
                            mm = pe.matmul(a_ps[:, b, x], tok[:, s * TT + k, g * HD:(g + 1) * HD], band[:, g, k],
                                           start=(k == 0), stop=(k == TT - 1))
                    mm.then_inc(summed, 1)
                for u in range(streams * TT):
                    pe.wait_ge(kept, 2 * (u // TT) + 2)
                    if due(u - 1):
                        pe.wait_ge(done, u - 1)
                    for g in range(4):
                        mm = pe.matmul(o_ps[:, u % 2, g * HD:(g + 1) * HD], pooled[:, u // TT, g, (u % TT) * P:(u % TT + 1) * P],
                                       w[:, g], start=True, stop=True)
                    mm.then_inc(made, 1)

            @block.scalar
            def _(act):
                for n in range(2 * streams):
                    s, b = divmod(n, 2)
                    act.wait_ge(summed, n + 1)
                    act.activation(pooled[:, s, 2 * b:2 * b + 2], a_ps[:, b], ACT.Copy).then_inc(kept, 1)

            @block.vector
            def _(dve):
                dve.wait_ge(rows_in, 48)
                for u in range(streams * TT):
                    dve.wait_ge(made, u + 1)
                    dve.tensor_tensor(tok[:, u, 0:POOL_W], o_ps[:, u % 2, 0:POOL_W], scale[:, :], ALU.mult).then_inc(done, 1)


def attention(core, layer, need_ctx, dram, tok):
    nc = core.nc
    tag = f"at{layer}"
    with ExitStack() as scope:
        sb = core.sbuf(scope, tag)
        ps = core.psum(scope, tag)
        heads = AH + KV
        sink = sb("sink", [P, AH])
        roped = sb("roped", [P, TT, heads * HD])
        tmp = sb("tmp", [P, 2, TT, heads * 2 * 16])
        q_t, k_t = sb("q_t", [HD, UU, AH, P]), sb("k_t", [HD, KV, 2 * T])
        s_sb, p_sb, p_t = sb("s_sb", [P, 2, 2 * T]), sb("p_sb", [P, 2, 2 * T]), sb("p_t", [P, 2, UU, P])
        units = [(u, h) for u in range(UU if need_ctx else TT) for h in range(AH)]
        small = sb("small", [P, 6, len(units)])
        s_ps, t_ps = ps("s_ps", [P, 2, 512]), ps("t_ps", [P, 2, UU, P])
        o_ps, h_ps = ps("o_ps", [P, 2, 512]), ps("h_ps", [HD, 2, 4, P])
        S = core.semaphore
        sink_in, rope_step, roped_s = S("sink_in"), S("rope_step"), S("roped")
        turned, kept = S("att_turned"), S("att_kept")
        scored, masked, peaked, raised, totals = S("att_scored"), S("att_masked"), S("att_peaked"), S("att_raised"), S("att_totals")
        p_turned, p_kept, summed, done = S("p_turned"), S("p_kept"), S("att_summed"), S("att_done")
        peak_found, added_up, inverted = S("peak_found"), S("totals_added"), S("totals_inverted")
        rope, amask = sb("rope", [P, 2, TT, 2, 16]), sb("amask", [P, TT, 2 * T])
        cos, sin = rope[:, 0], rope[:, 1]
        n_rope = [0]
        turns = [(u, x) for u in range(UU) for x in range(2)]
        peak, minus, total, sunk, inv = (small[:, i] for i in range(5))

        def keys(u):
            return slice(0, 2 * T) if u < TT else slice(T, 2 * T)

        with nc.Block() as block:

            @block.sync
            def _(sp):
                sp.dma_start(rope[:, :, :, :, :], dram["rope"]).then_inc(sink_in, 16)
                sp.dma_start(amask[:, :, :], dram["amask"]).then_inc(sink_in, 16)
                sp.dma_start(sink[:, :], dram["sink"][layer].unsqueeze(0).broadcast_to([P, AH])).then_inc(sink_in, 16)

            @block.vector
            def _(dve):
                def link(ins):
                    n_rope[0] += 1
                    ins.then_inc(rope_step, 1)
                    dve.wait_ge(rope_step, n_rope[0])

                dve.wait_ge(sink_in, 48)
                half = [P, heads, 2, 16]
                for u in range(TT):
                    src = tok[:, u, Q_AT:Q_AT + heads * HD].rearrange("p (h a x i) -> p h a x i", h=heads, a=2, x=2)
                    dst = roped[:, u].rearrange("p (h a x i) -> p h a x i", h=heads, a=2, x=2)
                    ts = [tmp[:, k, u].rearrange("p (h a i) -> p h a i", h=heads, a=2) for k in range(2)]
                    c = cos[:, u].unsqueeze(1).broadcast_to(half)
                    s = sin[:, u].unsqueeze(1).broadcast_to(half)
                    dve.tensor_tensor(ts[0], src[:, :, :, 1], s, ALU.mult)
                    dve.tensor_tensor(ts[1], src[:, :, :, 0], s, ALU.mult)
                    dve.tensor_tensor(dst[:, :, :, 0], src[:, :, :, 0], c, ALU.mult)
                    link(dve.tensor_tensor(dst[:, :, :, 1], src[:, :, :, 1], c, ALU.mult))
                    dve.tensor_tensor(dst[:, :, :, 0], dst[:, :, :, 0], ts[0], ALU.subtract)
                    dve.tensor_tensor(dst[:, :, :, 1], dst[:, :, :, 1], ts[1], ALU.add).then_inc(roped_s, 1)

                def back(n):
                    u, h = units[n]
                    dve.wait_ge(totals, n + 1)
                    dve.tensor_tensor(total[:, n:n + 1], total[:, n:n + 1], sunk[:, n:n + 1], ALU.add).then_inc(added_up, 1)
                    dve.wait_ge(added_up, n + 1)
                    dve.reciprocal(inv[:, n:n + 1], total[:, n:n + 1]).then_inc(inverted, 1)
                    dve.wait_ge(summed, n + 1)
                    dve.wait_ge(inverted, n + 1)
                    dve.tensor_scalar(tok[:, u, Q_AT + h * HD:Q_AT + (h + 1) * HD], o_ps[:, n % 2, 0:HD],
                                      inv[:, n:n + 1], None, ALU.mult).then_inc(done, 1)

                def front(n):
                    u, h = units[n]
                    w = slice(0, 2 * T) if u < TT else slice(0, T)
                    dve.wait_ge(scored, n + 1)
                    if due(n - 1):
                        dve.wait_ge(raised, n - 1)
                    if u < TT:
                        ins = dve.scalar_tensor_tensor(s_sb[:, n % 2, w], s_ps[:, n % 2, w], HD ** -0.5, amask[:, u], ALU.mult, ALU.add)
                    else:
                        ins = dve.tensor_scalar(s_sb[:, n % 2, w], s_ps[:, n % 2, w], HD ** -0.5, None, ALU.mult)
                    ins.then_inc(masked, 1)
                    dve.wait_ge(masked, n + 1)
                    dve.tensor_reduce(peak[:, n:n + 1], s_sb[:, n % 2, w], AX.X, ALU.max).then_inc(peak_found, 1)
                    dve.wait_ge(peak_found, n + 1)
                    dve.tensor_scalar(minus[:, n:n + 1], peak[:, n:n + 1], sink[:, h:h + 1], -1.0, ALU.max, ALU.mult).then_inc(peaked, 1)

                for n in range(len(units) + 2):
                    if n >= 2:
                        back(n - 2)
                    if n < len(units):
                        front(n)

            @block.scalar
            def _(act):
                for n, (u, x) in enumerate(turns):
                    act.wait_ge(turned, n + 1)
                    if x == 0:
                        act.activation(q_t[:, u, 0:4], h_ps[:, x], ACT.Copy).then_inc(kept, 1)
                    else:
                        act.activation(q_t[:, u, 4:6], h_ps[:, x, 0:2], ACT.Copy)
                        act.activation(k_t[:, :, u * P:(u + 1) * P], h_ps[:, x, 2:4], ACT.Copy).then_inc(kept, 1)
                act.wait_ge(sink_in, 48)

                def raise_(n):
                    u, h = units[n]
                    w = slice(0, 2 * T) if u < TT else slice(0, T)
                    act.wait_ge(peaked, n + 1)
                    if due(n - 1):
                        act.wait_ge(p_turned, n - 1)
                    act.activation(p_sb[:, n % 2, w], s_sb[:, n % 2, w], ACT.Exp, bias=minus[:, n:n + 1],
                                   accum_out=total[:, n:n + 1]).then_inc(raised, 1)
                    act.activation(sunk[:, n:n + 1], sink[:, h:h + 1], ACT.Exp, bias=minus[:, n:n + 1]).then_inc(totals, 1)

                def keep(n):
                    u, _ = units[n]
                    w = slice(0, UU) if u < TT else slice(0, TT)
                    act.wait_ge(p_turned, n + 1)
                    if due(n - 1):
                        act.wait_ge(summed, n - 1)
                    act.activation(p_t[:, n % 2, w], t_ps[:, n % 2, w], ACT.Copy).then_inc(p_kept, 1)

                for n in range(len(units) + 1):
                    if n < len(units):
                        raise_(n)
                    if n >= 1:
                        keep(n - 1)

            @block.tensor
            def _(pe):
                for n, (u, x) in enumerate(turns):
                    if u < TT:
                        pe.wait_ge(roped_s, u + 1)
                    if due(n - 1):
                        pe.wait_ge(kept, n - 1)
                    for k in range(4):
                        a = (4 * x + k) * HD
                        src = roped[:, u, a:a + HD] if u < TT else tok[:, u, Q_AT + a:Q_AT + a + HD]
                        mm = pe.transpose(h_ps[:, x, k], src, core.ident)
                    mm.then_inc(turned, 1)
                pe.wait_ge(kept, len(turns))

                def score(n):
                    u, h = units[n]
                    if due(n - 1):
                        pe.wait_ge(masked, n - 1)
                    ks = keys(u)
                    pe.matmul(s_ps[:, n % 2, 0:ks.stop - ks.start], q_t[:, u, h], k_t[:, h // (AH // KV), ks],
                              start=True, stop=True).then_inc(scored, 1)

                def turn(n):
                    u, h = units[n]
                    pe.wait_ge(raised, n + 1)
                    if due(n - 1):
                        pe.wait_ge(p_kept, n - 1)
                    for k in range(UU if u < TT else TT):
                        mm = pe.transpose(t_ps[:, n % 2, k], p_sb[:, n % 2, k * P:(k + 1) * P], core.ident)
                    mm.then_inc(p_turned, 1)

                def weigh(n):
                    u, h = units[n]
                    pe.wait_ge(p_kept, n + 1)
                    if due(n - 1):
                        pe.wait_ge(done, n - 1)
                    tiles = range(UU) if u < TT else range(TT, UU)
                    for k, t in enumerate(tiles):
                        a = V_AT + (h // (AH // KV)) * HD
                        mm = pe.matmul(o_ps[:, n % 2, 0:HD], p_t[:, n % 2, k], tok[:, t, a:a + HD],
                                       start=(k == 0), stop=(k == len(tiles) - 1))
                    mm.then_inc(summed, 1)

                for n in range(len(units) + 2):
                    if n < len(units):
                        score(n)
                    if 1 <= n <= len(units):
                        turn(n - 1)
                    if n >= 2:
                        weigh(n - 2)


def project_out(core, layer, streams, dram, tok):
    nc = core.nc
    tag = f"po{layer}"
    n_tok = streams * T
    with ExitStack() as scope:
        sb = core.sbuf(scope, tag)
        ps = core.psum(scope, tag)
        ring = 3
        w = sb("w", [P, ring, DC, P])
        y_t = sb("y_t", [P, DC, n_tok])
        t_ps, o_ps = ps("t_ps", [P, 2, 512]), ps("o_ps", [P, 2, 512])
        w_in = [core.semaphore(f"wo_in{r}") for r in range(ring)]
        turned, kept, made, added = (core.semaphore(x) for x in ("y_turned_o", "y_kept_o", "out_made", "out_added"))
        with nc.Block() as block:

            @block.sync
            def _(sp):
                for j in range(DC):
                    if due(j - ring + 1):
                        sp.wait_ge(made, j - ring + 1)
                    sp.dma_start(w[:, j % ring], dram["w_out"][layer, j]).then_inc(w_in[j % ring], 16)

            @block.tensor
            def _(pe):
                for c in range(DC):
                    if due(c - 1):
                        pe.wait_ge(kept, c - 1)
                    for u in range(streams * TT):
                        mm = pe.transpose(t_ps[:, c % 2, u * P:(u + 1) * P], tok[:, u, MIXED_AT[c]:MIXED_AT[c] + P], core.ident)
                    mm.then_inc(turned, 1)
                pe.wait_ge(kept, DC)
                for j in range(DC):
                    pe.wait_ge(w_in[j % ring], 16 * (j // ring + 1))
                    if due(streams * (j - 1)):
                        pe.wait_ge(added, streams * (j - 1))
                    for c in range(DC):
                        mm = pe.matmul(o_ps[:, j % 2, 0:n_tok], w[:, j % ring, c], y_t[:, c], start=(c == 0), stop=(c == DC - 1))
                    mm.then_inc(made, 1)

            @block.scalar
            def _(act):
                for c in range(DC):
                    act.wait_ge(turned, c + 1)
                    act.activation(y_t[:, c], t_ps[:, c % 2, 0:n_tok], ACT.Copy).then_inc(kept, 1)

            @block.vector
            def _(dve):
                for j in range(DC):
                    dve.wait_ge(made, j + 1)
                    for s in range(streams):
                        cols = slice(s * T, (s + 1) * T)
                        dve.scalar_tensor_tensor(core.x[:, j, cols], o_ps[:, j % 2, cols], core.mod[:, 2 * DC + j, s:s + 1],
                                                 core.x[:, j, cols], ALU.mult, ALU.add).then_inc(added, 1)


def mixing(core, layer, need_ctx, dram):
    nc = core.nc
    tag = f"mx{layer}"
    streams = 2 if need_ctx else 1
    with ExitStack() as scope:
        sb = core.sbuf(scope, tag)
        tok = sb("tok", [P, UU, TOK_W])
        consts = sb("consts", [P, CONSTS])
        consts_in = core.semaphore("mix_consts_in")
        cst = {}
        at = 0
        for name, shape in MIX_CONSTS:
            n = int(np.prod(shape))
            cst[name] = consts[:, at:at + n]
            at += n
        cst["tri"] = [cst["tri"][:, d * P:(d + 1) * P] for d in range(2)]
        cst["neg"] = [cst["neg"][:, d * P:(d + 1) * P] for d in range(2)]
        cst["lvl"] = [cst["lvl"].rearrange("p (d s n) -> p d s n", d=2, s=6)[:, d] for d in range(2)]
        with ExitStack() as inner:
            heads_sb = core.sbuf(inner, tag)
            qkv = heads_sb("qkv", [P, UU, 3 * GDN_W])
            heads_t = heads_sb("heads_t", [HD, UU, 2 * GH, P])
            beta = heads_sb("beta", [P, UU, 2 * GH])
            decay_g = heads_sb("decay_g", [P, UU, 2 * GH])
            with ExitStack() as first:
                conv_in = core.sbuf(first, tag)("conv_in", [P, QKV_C, 2, T + 2 * PAD])
                with ExitStack() as hs:
                    core.h = core.sbuf(hs, tag)("h", [P, DC, 2 * T])
                    with nc.Block() as block:

                        @block.sync
                        def _(sp):
                            sp.dma_start(consts[:, :], dram["mix_consts"]).then_inc(consts_in, 16)
                            sp.wait_ge(consts_in, 16)

                    parts = [(slice(s * T, (s + 1) * T), [core.mod[:, c, s:s + 1] for c in range(DC)],
                              [core.gain[:, 0, c, s:s + 1] for c in range(DC)]) for s in range(2)]
                    normalize(core, tag + "n", slice(0, 2 * T), parts)
                    project_in(core, layer, dram, conv_in, tok)
                short_conv(core, layer, dram, conv_in, qkv, heads_t)
                core.end_stage()
            gdn_gates(core, layer, dram, tok, beta, decay_g)
            made = {
                "attn": heads_sb("attn", [P, UU, 2, GH, P]),
                "value": heads_sb("value", [P, UU, 2, GH, HD]),
                "key_t": heads_sb("key_t", [HD, UU, 2, GH, P]),
                "key_dec": heads_sb("key_dec", [P, UU, 2, GH, HD]),
                "grow": heads_sb("grow", [P, UU, 2 * GH]),
                "whole": heads_sb("whole", [HD, 2 * UU, 2 * GH]),
            }
            gdn_chunks(core, layer, cst, qkv, heads_t, beta, decay_g, made)
            core.end_stage()
            gdn_states(core, layer, need_ctx, heads_t, made)
            gdn_finish(core, layer, streams * TT, dram, tok, made)
        pooling(core, layer, streams, dram, tok)
        attention(core, layer, need_ctx, dram, tok)
        project_out(core, layer, streams, dram, tok)


def topk(core, tag, dram, layer, top, top_i, best, best_i):
    nc = core.nc
    h = core.h
    with ExitStack() as scope:
        sb = core.sbuf(scope, tag)
        ps = core.psum(scope, tag)
        keys = sb("keys", [P, GROUPS, N_KEYS])
        wq = sb("wq", [P, WQ_RING, DC, P])
        q_sb = sb("q_sb", [P, 2, T])
        s_sb = sb("s_sb", [P, 2, TT, N_KEYS])
        s_cut = sb("s_cut", [P, TT, N_KEYS])
        cand = sb("cand", [P, TT, TOPK, TOPK])
        cand_cut = sb("cand_cut", [P, TT, TOPK * TOPK])
        q_ps = ps("q_ps", [P, 2, 512])
        s_ps = ps("s_ps", [P, 2, 512])
        keys_in = core.semaphore("peer_keys_in")
        wq_in = [core.semaphore(f"wq_in{r}") for r in range(WQ_RING)]
        q_made, q_copied = core.semaphore("q_made"), core.semaphore("q_copied")
        s_made, s_copied = core.semaphore("s_made"), core.semaphore("s_copied")
        picked, step = core.semaphore("picked"), core.semaphore("topk_step")
        n_steps = [0]
        with nc.Block() as block:

            @block.sync
            def _(sp):
                for g in range(GROUPS):
                    if due(g - WQ_RING + 1):
                        sp.wait_ge(q_made, g - WQ_RING + 1)
                    sp.dma_start(wq[:, g % WQ_RING], dram["wq"][layer, g]).then_inc(wq_in[g % WQ_RING], 16)
                    if g == 0:
                        sp.dma_start(keys[:, :, :], dram["keys"][layer]).then_inc(keys_in, 16)

            @block.tensor
            def _(pe):
                def queries(g):
                    pe.wait_ge(wq_in[g % WQ_RING], 16 * (g // WQ_RING + 1))
                    if due(g - 1):
                        pe.wait_ge(q_copied, g - 1)
                    for c in range(DC):
                        mm = pe.matmul(q_ps[:, g % 2, 0:T], wq[:, g % WQ_RING, c], h[:, c, 0:T],
                                       start=(c == 0), stop=(c == DC - 1))
                    mm.then_inc(q_made, 1)

                def scores(g):
                    if g == 0:
                        pe.wait_ge(keys_in, 16)
                    pe.wait_ge(q_copied, g + 1)
                    if due(g - 1):
                        pe.wait_ge(s_copied, g - 1)
                    for u in range(TT):
                        mm = pe.matmul(s_ps[:, g % 2, u * P:(u + 1) * P], q_sb[:, g % 2, u * P:(u + 1) * P],
                                       keys[:, g], start=True, stop=True)
                    mm.then_inc(s_made, 1)

                queries(0)
                for g in range(GROUPS):
                    if g + 1 < GROUPS:
                        queries(g + 1)
                    scores(g)

            @block.scalar
            def _(act):
                for g in range(GROUPS):
                    act.wait_ge(q_made, g + 1)
                    if due(g - 1):
                        act.wait_ge(s_made, g - 1)
                    act.activation(q_sb[:, g % 2, :], q_ps[:, g % 2, 0:T], ACT.Copy).then_inc(q_copied, 1)
                    act.wait_ge(s_made, g + 1)
                    if due(g - 1):
                        act.wait_ge(picked, g - 1)
                    act.activation(s_sb[:, g % 2], s_ps[:, g % 2, 0:T], ACT.Copy).then_inc(s_copied, 1)

            @block.vector
            def _(dve):
                def linked(ins):
                    n_steps[0] += 1
                    ins.then_inc(step, 1)
                    dve.wait_ge(step, n_steps[0])

                def best16(values, indices, scores, cut):
                    for u in range(TT):
                        last = dve.max(values(u)[:, 0:8], scores(u))
                    linked(last)
                    for u in range(TT):
                        last = dve.match_replace(cut(u), values(u)[:, 0:8], scores(u), LOWEST)
                    for u in range(TT):
                        dve.max_index(indices(u)[:, 0:8], values(u)[:, 0:8], scores(u))
                    linked(last)
                    for u in range(TT):
                        last = dve.max(values(u)[:, 8:16], cut(u))
                    linked(last)
                    for u in range(TT):
                        last = dve.max_index(indices(u)[:, 8:16], values(u)[:, 8:16], cut(u))
                    return last

                for g in range(GROUPS):
                    dve.wait_ge(s_copied, g + 1)
                    best16(lambda u: top[:, u, g], lambda u: top_i[:, u, g], lambda u: s_sb[:, g % 2, u],
                           lambda u: s_cut[:, u]).then_inc(picked, 1)
                    if g % 2:
                        hd = g // 2
                        for u in range(TT):
                            a = top[:, u, g - 1].unsqueeze(2).broadcast_to([P, TOPK, TOPK])
                            b = top[:, u, g].unsqueeze(1).broadcast_to([P, TOPK, TOPK])
                            last = dve.tensor_tensor(cand[:, u], a, b, ALU.add)
                        linked(last)
                        flat = cand[:, :, :, :].rearrange("p u a b -> p u (a b)")
                        best16(lambda u: best[:, u, hd], lambda u: best_i[:, u, hd], lambda u: flat[:, u],
                               lambda u: cand_cut[:, u])


def gate_matrix(core, tag, dram, top_i, best, best_i, stage):
    nc = core.nc
    with ExitStack() as scope:
        sb = core.sbuf(scope, tag)
        ps = core.psum(scope, tag)
        key_f = sb("key_f", [P, GROUPS, TOPK])
        rank_u = sb("rank_u", [P, 2, HEADS, TOPK], U32)
        rank = sb("rank", [P, 2, HEADS, TOPK])
        hot = sb("hot", [P, 2, HEADS, TOPK, TOPK])
        gate = sb("gate", [P, HEADS, TOPK])
        slot_key = sb("slot_key", [P, 2, SLOTS])
        sums, inv = sb("sums", [P, HEADS]), sb("inv", [P, HEADS])
        slot_major = sb("slot_major", [P, 3, TT, P])
        first = sb("first", [P, ROUND, N_KEYS])
        second = sb("second", [P, ROUND, N_KEYS])
        t_ps = ps("t_ps", [P, 512])
        w_ps = ps("w_ps", [P, QUADS, 4, P])
        step, shifted = core.semaphore("gate_step"), core.semaphore("gates_shifted")
        expd, ready = core.semaphore("gates_exp"), core.semaphore("slots_ready")
        turned, major = core.semaphore("slots_turned"), core.semaphore("slots_major")
        rows = core.semaphore("one_hot_rows")
        outer, staged, stored = core.semaphore("outer_done"), core.semaphore("w_staged"), core.semaphore("w_stored")
        n_steps = [0]
        rounds = P // ROUND

        def tile_rounds(eng, u, body):
            if u == 0:
                body(0)
            with eng.Fori(1 if u == 0 else 0, rounds) as r:
                body(r)

        with nc.Block() as block:

            @block.vector
            def _(dve):
                def linked(ins):
                    n_steps[0] += 1
                    ins.then_inc(step, 1)
                    dve.wait_ge(step, n_steps[0])

                def decode(u):
                    full = [P, HEADS, TOPK, TOPK]
                    dve.tensor_tensor(gate[:, :, :], best[:, u], best[:, u, :, 0:1].broadcast_to([P, HEADS, TOPK]),
                                      ALU.subtract).then_inc(shifted, 1)
                    dve.tensor_copy(key_f[:, :, :], top_i[:, u])
                    dve.tensor_scalar(rank_u[:, 0], best_i[:, u], 4, None, ALU.logical_shift_right)
                    linked(dve.tensor_scalar(rank_u[:, 1], best_i[:, u], TOPK - 1, None, ALU.bitwise_and))
                    linked(dve.tensor_copy(rank[:, :, :, :], rank_u[:, :, :, :]))
                    iota16 = core.iota[:, 0:TOPK].unsqueeze(1).unsqueeze(1).broadcast_to(full)
                    keys = key_f[:, :, :].rearrange("p (h s) k -> p s h k", s=2)
                    for s in range(2):
                        last = dve.tensor_tensor(hot[:, s], rank[:, s].unsqueeze(3).broadcast_to(full), iota16, ALU.is_equal)
                    linked(last)
                    for s in range(2):
                        last = dve.tensor_tensor(hot[:, s], hot[:, s], keys[:, s].unsqueeze(2).broadcast_to(full), ALU.mult)
                    linked(last)
                    for s in range(2):
                        dve.tensor_reduce(slot_key[:, s], hot[:, s].rearrange("p h k r -> p (h k) r"), AX.X, ALU.add)
                    dve.wait_ge(expd, u + 1)
                    linked(dve.tensor_reduce(sums[:, :], gate[:, :, :], AX.X, ALU.add))
                    linked(dve.reciprocal(inv[:, :], sums[:, :]))
                    dve.tensor_tensor(gate[:, :, :], gate[:, :, :], inv[:, :].unsqueeze(2).broadcast_to([P, HEADS, TOPK]),
                                      ALU.mult).then_inc(ready, 1)
                    dve.wait_ge(turned, u + 1)
                    dve.tensor_copy(slot_major[:, :, u], t_ps[:, 0:3 * P].rearrange("p (k t) -> p k t", k=3)).then_inc(major, 1)
                    dve.wait_ge(major, u + 1)

                for u in range(TT):
                    decode(u)

                    def round_(r):
                        for x in range(QUADS):
                            if due(rounds * u + r):
                                dve.wait_ge(outer, (u * rounds + r) * QUADS + (x + 1 - QUADS))
                            for k in range(4 * x, 4 * x + 4):
                                t = r * ROUND + k
                                dve.tensor_scalar(first[:, k], core.iota, slot_major[:, 0, u, bass.ds(t, 1)],
                                                  slot_major[:, 2, u, bass.ds(t, 1)], ALU.is_equal, ALU.mult)
                            keys = slot_major[:, 1, u, bass.ds(r * ROUND + 4 * x, 4)].unsqueeze(2).broadcast_to([P, 4, N_KEYS])
                            iota4 = core.iota.unsqueeze(1).broadcast_to([P, 4, N_KEYS])
                            dve.tensor_tensor(second[:, 4 * x:4 * x + 4], keys, iota4, ALU.is_equal).then_inc(rows, 1)

                    tile_rounds(dve, u, round_)

            @block.tensor
            def _(pe):
                for u in range(TT):
                    pe.wait_ge(ready, u + 1)
                    pe.transpose(t_ps[:, 0:P], slot_key[:, 0], core.ident)
                    pe.transpose(t_ps[:, P:2 * P], slot_key[:, 1], core.ident)
                    pe.transpose(t_ps[:, 2 * P:3 * P], gate[:, :, :].rearrange("p h k -> p (h k)"), core.ident).then_inc(turned, 1)

                    def round_(r):
                        for x in range(QUADS):
                            n = (u * rounds + r) * QUADS
                            pe.wait_ge(rows, n + (x + 1))
                            if due(rounds * u + r):
                                pe.wait_ge(staged, n + (x + 1 - QUADS))
                            for k in range(4):
                                mm = pe.matmul(w_ps[:, x, k], first[:, 4 * x + k], second[:, 4 * x + k], start=True, stop=True)
                            mm.then_inc(outer, 1)

                    tile_rounds(pe, u, round_)

            @block.scalar
            def _(act):
                for u in range(TT):
                    act.wait_ge(shifted, u + 1)
                    act.activation(gate[:, :, :], gate[:, :, :], ACT.Exp).then_inc(expd, 1)
                    if u:
                        act.wait_ge(stored, 16 * u)
                    with act.Fori(0, rounds) as r:
                        for x in range(QUADS):
                            act.wait_ge(outer, (u * rounds + r) * QUADS + (x + 1))
                            act.activation(stage[:, :, bass.ds(r * ROUND + 4 * x, 4)], w_ps[:, x].rearrange("p t i -> p i t"),
                                           ACT.Copy).then_inc(staged, 1)

            @block.sync
            def _(sp):
                sp.wait_ge(staged, QUADS * rounds)
                sp.dma_start(dram["gates"].rearrange("j i t -> i j t"), stage[:, :, :]).then_inc(stored, 16)
                sp.wait_ge(stored, 16)


def experts(core, layer, stream, dram, stage):
    nc = core.nc
    tag = f"ex{layer}{stream}"
    with ExitStack() as scope:
        sb = core.sbuf(scope, tag)
        ps = core.psum(scope, tag)
        h_hi, h_lo = sb("h_hi", [P, DC, T], F32R), sb("h_lo", [P, DC, T], F32R)
        u_raw, v_raw = sb("u_raw", [P, 2, 2, D]), sb("v_raw", [P, 2, 2, D])
        w_raw = sb("w_raw", [P, 2, 2, P])
        u_hi, u_lo = sb("u_hi", [P, 2, D], F32R), sb("u_lo", [P, 2, D], F32R)
        v_hi, v_lo = sb("v_hi", [P, 2, D], F32R), sb("v_lo", [P, 2, D], F32R)
        gel, prod = sb("gel", [P, 2, T]), sb("prod", [P, 2, T])
        p_hi, p_lo = sb("p_hi", [P, 2, T], F32R), sb("p_lo", [P, 2, T], F32R)
        y_sb = sb("y_sb", [P, TT, D])
        a_ps = ps("a_ps", [P, 2, 512])
        y_ps = ps("y_ps", [P, TT, 2, 512])
        t_ps = ps("t_ps", [P, 2, 512])
        u_in = [core.semaphore(f"u_in{r}") for r in range(2)]
        v_in = [core.semaphore(f"v_in{r}") for r in range(2)]
        w_in = [core.semaphore(f"w_in{r}") for r in range(2)]
        h_hi_done, h_split = core.semaphore("h_hi_done"), core.semaphore("h_split")
        u_hi_done, v_hi_done = core.semaphore("u_hi_done"), core.semaphore("v_hi_done")
        u_split, v_split = core.semaphore("u_split"), core.semaphore("v_split")
        scored, gelud, gated = core.semaphore("scored"), core.semaphore("gelud"), core.semaphore("gated")
        p_hi_done, p_split, summed = core.semaphore("p_hi_done"), core.semaphore("p_split"), core.semaphore("summed")
        y_out, y_turned, added = core.semaphore("y_out"), core.semaphore("y_turned"), core.semaphore("added")
        pairs = N_KEYS // 2
        cols = slice(stream * T, (stream + 1) * T)

        def quads(eng, body):
            for n in range(4):
                body(0, n // 2, n % 2)
            with eng.Fori(1, pairs // 2) as q:
                for n in range(4):
                    body(q, n // 2, n % 2)

        with nc.Block() as block:

            @block.sync
            def _(sp):
                def load(q, r):
                    m = 2 * q + r
                    if due(2 * m - 2):
                        sp.wait_ge(u_split, 2 * m - 2)
                    sp.dma_start(u_raw[:, r], dram["u"][layer, bass.ds(m, 1)].rearrange("o p b n -> p (o b) n")).then_inc(u_in[r], 16)
                    if due(2 * m - 2):
                        sp.wait_ge(v_split, 2 * m - 2)
                    sp.dma_start(v_raw[:, r], dram["v"][layer, bass.ds(m, 1)].rearrange("o p b n -> p (o b) n")).then_inc(v_in[r], 16)
                    if due(2 * m - 2):
                        sp.wait_ge(gated, 2 * m - 2)
                    sp.dma_start(w_raw[:, r], dram["gates"][bass.ds(2 * m, 2)].rearrange("b i t -> i b t")).then_inc(w_in[r], 16)

                load(0, 0)
                load(0, 1)
                with sp.Fori(1, pairs // 2) as q:
                    load(q, 0)
                    load(q, 1)

            @block.scalar
            def _(act):
                act.activation(h_hi[:, :, :], core.h[:, :, 0:T], ACT.Copy).then_inc(h_hi_done, 1)

                def body(q, r, b):
                    i = 4 * q + (2 * r + b)
                    act.wait_ge(u_in[r], 16 * q + 16)
                    if due(i - 1):
                        act.wait_ge(scored, i - 1)
                    act.activation(u_hi[:, b], u_raw[:, r, b], ACT.Copy).then_inc(u_hi_done, 1)
                    if not (isinstance(i, int) and i < 1):
                        gelu_and_high(i - 1, 1 - b)
                    act.wait_ge(v_in[r], 16 * q + 16)
                    if due(i - 1):
                        act.wait_ge(summed, i - 1)
                    act.activation(v_hi[:, b], v_raw[:, r, b], ACT.Copy).then_inc(v_hi_done, 1)

                def gelu_and_high(i, b):
                    act.wait_ge(scored, i + 1)
                    if due(i - 1):
                        act.wait_ge(gated, i - 1)
                    act.activation(gel[:, b], a_ps[:, b, 0:T], ACT.Gelu).then_inc(gelud, 1)
                    act.wait_ge(gated, i + 1)
                    if due(i - 1):
                        act.wait_ge(summed, i - 1)
                    act.activation(p_hi[:, b], prod[:, b], ACT.Copy).then_inc(p_hi_done, 1)

                quads(act, body)
                gelu_and_high(N_KEYS - 1, 1)
                for u in range(TT):
                    for k in range(2):
                        act.wait_ge(summed, N_KEYS)
                        act.activation(y_sb[:, u, k * 512:(k + 1) * 512], y_ps[:, u, k], ACT.Copy).then_inc(y_out, 1)

            @block.vector
            def _(dve):
                dve.wait_ge(h_hi_done, 1)
                dve.tensor_tensor(h_lo[:, :, :], core.h[:, :, 0:T], h_hi[:, :, :].bitcast(F32), ALU.subtract).then_inc(h_split, 1)

                def body(q, r, b):
                    i = 4 * q + (2 * r + b)
                    dve.wait_ge(u_hi_done, i + 1)
                    if due(i - 1):
                        dve.wait_ge(scored, i - 1)
                    dve.tensor_tensor(u_lo[:, b], u_raw[:, r, b], u_hi[:, b].bitcast(F32), ALU.subtract).then_inc(u_split, 1)
                    if not (isinstance(i, int) and i < 1):
                        gate(i - 1, 1 - b, r if b else 1 - r, q if b or r else q - 1)
                    dve.wait_ge(v_hi_done, i + 1)
                    if due(i - 1):
                        dve.wait_ge(summed, i - 1)
                    dve.tensor_tensor(v_lo[:, b], v_raw[:, r, b], v_hi[:, b].bitcast(F32), ALU.subtract).then_inc(v_split, 1)

                def gate(i, b, r, q):
                    dve.wait_ge(gelud, i + 1)
                    dve.wait_ge(w_in[r], 16 * q + 16)
                    if due(i - 1):
                        dve.wait_ge(p_split, i - 1)
                    dve.tensor_tensor(prod[:, b, 0:P], gel[:, b, 0:P], w_raw[:, r, b], ALU.mult)
                    w_late = stage[:, i] if isinstance(i, int) else stage[:, bass.ds(i, 1)].rearrange("p o t -> p (o t)")
                    dve.tensor_tensor(prod[:, b, P:T], gel[:, b, P:T], w_late, ALU.mult).then_inc(gated, 1)
                    dve.wait_ge(p_hi_done, i + 1)
                    if due(i - 1):
                        dve.wait_ge(summed, i - 1)
                    dve.tensor_tensor(p_lo[:, b], prod[:, b], p_hi[:, b].bitcast(F32), ALU.subtract).then_inc(p_split, 1)

                quads(dve, body)
                gate(N_KEYS - 1, 1, 1, pairs // 2 - 1)
                for c in range(DC):
                    dve.wait_ge(y_turned, c + 1)
                    dve.scalar_tensor_tensor(core.x[:, c, cols], t_ps[:, c % 2, 0:T], core.mod[:, 5 * DC + c, stream:stream + 1],
                                             core.x[:, c, cols], ALU.mult, ALU.add).then_inc(added, 1)

            @block.tensor
            def _(pe):
                pe.wait_ge(h_split, 1)

                def score(i, b):
                    pe.wait_ge(u_split, i + 1)
                    if due(i - 1):
                        pe.wait_ge(gelud, i - 1)
                    n = 0
                    for lhs, rhs in ((u_hi, h_hi), (u_hi, h_lo), (u_lo, h_hi)):
                        for c in range(DC):
                            mm = pe.matmul(a_ps[:, b, 0:T], lhs[:, b, c * P:(c + 1) * P], rhs[:, c, :],
                                           start=(n == 0), stop=(n == 3 * DC - 1))
                            n += 1
                    mm.then_inc(scored, 1)

                def project(i, b, first, last):
                    pe.wait_ge(p_split, i + 1)
                    pe.wait_ge(v_split, i + 1)
                    for u in range(TT):
                        for n, (lhs, rhs) in enumerate(((p_hi, v_hi), (p_hi, v_lo), (p_lo, v_hi))):
                            for k in range(2):
                                mm = pe.matmul(y_ps[:, u, k], lhs[:, b, u * P:(u + 1) * P], rhs[:, b, k * 512:(k + 1) * 512],
                                               start=(first and n == 0), stop=(last and n == 2), skip_group_check=True)
                    mm.then_inc(summed, 1)

                def body(q, r, b):
                    i = 4 * q + (2 * r + b)
                    score(i, b)
                    if not (isinstance(i, int) and i < 1):
                        project(i - 1, 1 - b, isinstance(i, int) and i == 1, False)

                quads(pe, body)
                project(N_KEYS - 1, 1, False, True)
                pe.wait_ge(y_out, 2 * TT)
                for c in range(DC):
                    if due(c - 1):
                        pe.wait_ge(added, c - 1)
                    for u in range(TT):
                        mm = pe.transpose(t_ps[:, c % 2, u * P:(u + 1) * P], y_sb[:, u, c * P:(c + 1) * P], core.ident)
                    mm.then_inc(y_turned, 1)
def constants():
    i, j = np.arange(P)[None, :], np.arange(P)[:, None]
    same = i // HD == j // HD
    tri = np.stack([same & (j <= i), same & (j >= i)], 1)
    neg = np.where(tri, 0.0, MASKED)
    lvl = np.zeros((P, 2, 6, P))
    for k in range(6):
        s = 2 ** k
        lvl[:, 0, k] = ((i // s) % 2 == 1) & (j // s == i // s - 1)
        lvl[:, 1, k] = ((i // s) % 2 == 0) & (j // s == i // s + 1)
    mix = np.concatenate([same, tri.reshape(P, -1), neg.reshape(P, -1), lvl.reshape(P, -1)], 1)
    base = np.concatenate([np.eye(P), np.ones((P, P)), np.broadcast_to(np.arange(P), (P, P))], 1)
    t = np.arange(T)
    band = np.zeros((T, 4, T))
    for g, w in enumerate(POOL_WINDOWS):
        lo, hi = np.clip(t - w // 2, 0, T), np.clip(t + w - w // 2, 0, T)
        inside = (t[:, None] >= lo[None]) & (t[:, None] < hi[None])
        band[:, g] = inside / (hi - lo)[None] - np.eye(T)
    band = band.reshape(TT, P, 4, T).transpose(1, 2, 0, 3)
    amask = np.zeros((T, 2 * T))
    amask[:, :T] = np.where(np.abs(t[:, None] - t[None]) <= WINDOW, 0.0, MASKED)
    amask = amask.reshape(TT, P, 2 * T).transpose(1, 0, 2)
    f32 = np.float32
    pos = np.stack([t // GRID_W, t % GRID_W], -1).astype(f32)
    inv = np.power(f32(ROPE_BASE), -np.arange(ROPE_PAIRS, dtype=f32) / f32(ROPE_PAIRS))
    ang = pos[:, :, None] * inv
    rope = np.stack([np.cos(ang), np.sin(ang)]).reshape(2, TT, P, 2, ROPE_PAIRS).transpose(2, 0, 1, 3, 4)
    found = {"base_consts": base, "mix_consts": mix, "band": band, "amask": amask, "rope": rope}
    return {k: np.ascontiguousarray(v, dtype=f32) for k, v in found.items()}


def layout(a):
    n = a["w_in"].shape[0]
    cols = lambda v: v.reshape(*v.shape[:-1], DC, P)
    r = {}
    r["x_t"] = np.concatenate([a["x"][0], a["ctx"][0]], 0).T.reshape(DC, P, 2 * T).transpose(1, 0, 2)
    r["c2"] = np.stack([a["c"][0], a["c_ctx"]], -1).reshape(DC, P, 2).transpose(1, 0, 2)
    r["w_ada"] = a["w_ada"].reshape(n, DC, P, 12, 512).transpose(0, 3, 2, 1, 4)
    r["b_ada"] = a["b_ada"].reshape(n, 6 * DC, P).transpose(0, 2, 1)
    r["norms"] = np.stack([cols(a["norm1"]), cols(a["norm2"])], 1).transpose(0, 3, 1, 2)
    r["norm_f"] = cols(a["norm_f"]).T
    q0, q1 = POOL_W, POOL_W + 3 * GDN_W
    r["w_qkv"] = a["w_in"][:, :, q0:q1].reshape(n, DC, P, QKV_C, P).transpose(0, 3, 2, 1, 4)
    r["w_tok"] = np.concatenate([a["w_in"][:, :, :q0], a["w_in"][:, :, q1:]], 2).reshape(n, DC, P, TOK_W).transpose(0, 2, 1, 3)
    r["conv_w"] = a["conv_w"].reshape(n, CONV_K, QKV_C, P).transpose(0, 3, 2, 1)
    r["a_log"] = a["a_log"].reshape(n, 2 * GH)
    r["dt_bias"] = a["dt_bias"].reshape(n, 2 * GH)
    r["gdn_norm"], r["pool_scale"], r["sink"] = a["gdn_norm"], a["pool_scale"], a["sink"]
    r["w_pool"] = a["w_pool"].transpose(0, 2, 1, 3)
    r["w_out"] = a["w_out"].reshape(n, DC, P, DC, P).transpose(0, 3, 2, 1, 4)
    r["wq"] = a["peer_wq"].reshape(n, DC, P, GROUPS, P).transpose(0, 3, 2, 1, 4)
    r["keys"] = a["peer_keys"].reshape(n, GROUPS, N_KEYS, P).transpose(0, 3, 1, 2)
    u = a["peer_u"].reshape(n, N_KEYS, N_KEYS // 2, 2, DC, P)
    r["u"] = u.transpose(0, 2, 5, 3, 4, 1).reshape(n, N_KEYS // 2, P, 2, D)
    r["v"] = a["peer_v"].reshape(n, N_KEYS, N_KEYS // 2, 2, D).transpose(0, 2, 1, 3, 4)
    return {k: np.ascontiguousarray(v) for k, v in r.items()}


def hybrid_backbone(nc, depth, dram, out):
    dram = dict(dram)
    dram["gates"] = nc.dram_tensor("peer_gates", [N_KEYS, N_KEYS, P], F32, kind="Internal").ap()
    with ExitStack() as scope:
        core = Core(nc)
        sb = core.sbuf(scope, "core")
        core.x = sb("x", [P, DC, 2 * T])
        core.mod = sb("mod", [P, 6 * DC, 2])
        core.gain = sb("gain", [P, 2, DC, 2])
        base = sb("base", [P, 3 * P])
        last_gain = sb("norm_f", [P, DC])
        core.ident, core.ones, core.iota = base[:, 0:P], base[:, P:2 * P], base[:, 2 * P:3 * P]
        loaded = core.semaphore("loaded")
        with nc.Block() as block:

            @block.sync
            def _(sp):
                sp.dma_start(base[:, :], dram["base_consts"]).then_inc(loaded, 16)
                sp.dma_start(last_gain[:, :], dram["norm_f"]).then_inc(loaded, 16)
                sp.dma_start(core.x[:, :, :], dram["x_t"]).then_inc(loaded, 16)
                sp.wait_ge(loaded, 48)

        core.end_stage()
        for layer in range(depth):
            need_ctx = layer < depth - 1
            modulation(core, layer, dram)
            core.end_stage()
            mixing(core, layer, need_ctx, dram)
            core.end_stage()
            for stream in range(2 if need_ctx else 1):
                cols = slice(stream * T, (stream + 1) * T)
                with ExitStack() as hs:
                    core.h = core.sbuf(hs, f"pe{layer}{stream}")("h", [P, DC, T])
                    parts = [(slice(0, T), [core.mod[:, 3 * DC + c, stream:stream + 1] for c in range(DC)],
                              [core.gain[:, 1, c, stream:stream + 1] for c in range(DC)])]
                    normalize(core, f"pn{layer}{stream}", cols, parts)
                    tag = f"pr{layer}{stream}"
                    with ExitStack() as ss:
                        stage = core.sbuf(ss, tag)("stage", [P, N_KEYS, P])
                        with ExitStack() as ts:
                            sb = core.sbuf(ts, tag)
                            top, top_i = sb("top", [P, TT, GROUPS, TOPK]), sb("top_i", [P, TT, GROUPS, TOPK], U32)
                            best, best_i = sb("best", [P, TT, HEADS, TOPK]), sb("best_i", [P, TT, HEADS, TOPK], U32)
                            topk(core, tag, dram, layer, top, top_i, best, best_i)
                            core.end_stage()
                            gate_matrix(core, tag, dram, top_i, best, best_i, stage)
                            core.end_stage()
                        experts(core, layer, stream, dram, stage)
                        core.end_stage()
        with ExitStack() as hs:
            core.h = core.sbuf(hs, "final")("h", [P, DC, T])
            normalize(core, "fn", slice(0, T), [(slice(0, T), None, [last_gain[:, c:c + 1] for c in range(DC)])])
            stored = core.semaphore("stored")
            with nc.Block() as block:

                @block.sync
                def _(sp):
                    sp.dma_start(out, core.h[:, :, :]).then_inc(stored, 16)
                    sp.wait_ge(stored, 16)


def kernel(**inputs):
    import concourse.bacc as bacc
    from concourse.bass_utils import run_bass_kernel_spmd

    arrays = layout({k: np.asarray(v) for k, v in inputs.items()})
    arrays.update(constants())
    nc = bacc.Bacc("TRN2", target_bir_lowering=False, num_devices=1)
    dram = {k: nc.dram_tensor(f"in_{k}", v.shape, mybir.dt.from_np(v.dtype), kind="ExternalInput").ap()
            for k, v in arrays.items()}
    out = nc.dram_tensor("out_t", [P, DC, T], F32, kind="ExternalOutput").ap()
    hybrid_backbone(nc, inputs["w_in"].shape[0], dram, out)
    r = run_bass_kernel_spmd(nc, [{f"in_{k}": v for k, v in arrays.items()}], core_ids=[0])
    y = np.asarray(r.results[0]["out_t"])
    return np.ascontiguousarray(y.transpose(2, 1, 0).reshape(1, T, D))
```

```python
from contextlib import ExitStack

import numpy as np

import concourse.bass as bass
from concourse import mybir

F32, F32R, U32 = mybir.dt.float32, mybir.dt.float32r, mybir.dt.uint32
ALU, ACT, AX = mybir.AluOpType, mybir.ActivationFunctionType, mybir.AxisListType

P = 128
D = 1024
DC = D // P
T = 256
TT = T // P
EPS = 1e-6
HEADS, N_KEYS, TOPK = 8, 128, 16
GROUPS = 2 * HEADS
SLOTS = HEADS * TOPK
ROUND = 16
QUADS = ROUND // 4
WQ_RING, WF_RING = 3, 3
WADA_RING = 3
MOD_FIRST, MOD_GATE, MOD_SECOND = list(range(0, 4)), list(range(4, 6)), list(range(6, 12))
LOWEST = -3.0e38
MASKED = -1.0e30

UU = 2 * TT
HD = 64
POOL_W, GDN_W, ATT_W = 256, 384, 384
POOL_WINDOWS = (2, 4, 8, 16)
GH, AH, KV = GDN_W // HD, ATT_W // HD, 2
QKV_C = 3 * GDN_W // P
CONV_K = 5
MOD_BESIDE = len(MOD_GATE) * DC // (QKV_C - 1)
PAD = CONV_K // 2
Z_AT = POOL_W
BA_AT = Z_AT + GDN_W
Q_AT = BA_AT + 4 * GH
V_AT = Q_AT + ATT_W + KV * HD
TOK_W = V_AT + KV * HD
MIXED_AT = [P * c for c in range(5)] + [Q_AT + P * c for c in range(3)]
MIX_CONSTS = (("chunk_ones", (P,)), ("tri", (2, P)), ("neg", (2, P)), ("cross", (2, P)), ("diagonal", (P,)))
CONSTS = sum(int(np.prod(s)) for _, s in MIX_CONSTS)
BLK = 32
WINDOW = 128
GRID_W, ROPE_BASE, ROPE_PAIRS = 64, 10000.0, 16


def due(count):
    return not isinstance(count, int) or count > 0


class Core:

    def __init__(self, nc):
        self.nc, self.semaphores, self.stage = nc, {}, 0

    def semaphore(self, name):
        assert name not in self.semaphores, name
        self.semaphores[name] = self.nc.alloc_semaphore(name=f"{name}_{self.stage}")
        return self.semaphores[name]

    def end_stage(self):
        self.nc.clear_and_free_semaphores(list(self.semaphores.values()))
        self.nc.all_engine_barrier()
        self.semaphores, self.stage = {}, self.stage + 1

    def sbuf(self, scope, tag):
        return lambda name, shape, dt=F32: scope.enter_context(self.nc.sbuf_tensor(f"{tag}_{name}", shape, dt))

    def psum(self, scope, tag):
        return lambda name, shape, dt=F32: scope.enter_context(self.nc.psum_tensor(f"{tag}_{name}", shape, dt))


def normalize(core, scope, block, tag, cols, parts, ahead=()):
    nc = core.nc
    n = cols.stop - cols.start
    sb = core.sbuf(scope, tag)
    ps = core.psum(scope, tag)
    sq = sb("sq", [P, DC, n])
    rstd = sb("rstd", [P, n])
    s_ps = ps("s_ps", [P, n])
    squared, sums = core.semaphore("squared"), core.semaphore("square_sums")
    mean, root, scaled = core.semaphore("mean_square"), core.semaphore("rms"), core.semaphore("h_scaled")
    inverse, shifted = core.semaphore("rstd_ready"), core.semaphore("h_shifted")

    @block.sync
    def _(sp):
        for to, source, arrived in ahead:
            sp.dma_start(to, source).then_inc(arrived, 16)

    @block.scalar
    def _(act):
        for c in range(DC):
            act.activation(sq[:, c], core.x[:, c, cols], ACT.Square).then_inc(squared, 1)
        act.wait_ge(mean, 1)
        act.activation(rstd[:, :], rstd[:, :], ACT.Sqrt).then_inc(root, 1)
        for c in range(DC):
            for i, (to, shift, _) in enumerate(parts):
                if shift is not None:
                    act.wait_ge(scaled, c * len(parts) + i + 1)
                    act.activation(core.h[:, c, to], core.h[:, c, to], ACT.Identity, bias=shift[c]).then_inc(shifted, 1)

    @block.tensor
    def _(pe):
        for c in range(DC):
            pe.wait_ge(squared, c + 1)
            mm = pe.matmul(s_ps[:, :], core.ones, sq[:, c], start=(c == 0), stop=(c == DC - 1))
        mm.then_inc(sums, 1)

    @block.vector
    def _(dve):
        dve.wait_ge(sums, 1)
        dve.tensor_scalar(rstd[:, :], s_ps[:, :], 1.0 / D, EPS, ALU.mult, ALU.add).then_inc(mean, 1)
        dve.wait_ge(root, 1)
        dve.reciprocal(rstd[:, :], rstd[:, :]).then_inc(inverse, 1)
        dve.wait_ge(inverse, 1)
        for c in range(DC):
            for to, _, g in parts:
                src = slice(cols.start + to.start, cols.start + to.stop)
                dve.scalar_tensor_tensor(core.h[:, c, to], core.x[:, c, src], g[c], rstd[:, to],
                                         ALU.mult, ALU.mult).then_inc(scaled, 1)

    return scaled if parts[0][1] is None else shifted


class Modulation:

    def __init__(self, core, scope, dram, groups, row_ps, m_ps):
        self.core, self.dram, self.groups = core, dram, groups
        self.halves = [(layer, half) for layer, halves, _ in groups for half in halves]
        self.count = len(self.halves)
        sb = core.sbuf(scope, "mod{}_{}".format(*self.halves[0]))
        self.w = sb("w", [P, WADA_RING, DC, 512])
        self.bias, self.gain = sb("bias", [P, 4 * self.count]), sb("gain", [P, len(groups), DC])
        self.rows = sb("rows", [2, 2, 512])
        self.row_ps, self.m_ps = row_ps, m_ps
        self.w_in = [core.semaphore(f"wada_in{r}") for r in range(WADA_RING)]
        self.cols_in, self.used, self.copied = core.semaphore("mod_cols_in"), core.semaphore("wada_used"), core.semaphore("mod_row_copied")
        self.turned, self.step = core.semaphore("mod_turned"), core.semaphore("mod_step")

    def load(self, sp):
        at = 0
        for g, (layer, halves, norm) in enumerate(self.groups):
            bias = self.dram["b_ada"][layer, :, 4 * halves[0]:4 * (halves[-1] + 1)]
            sp.dma_start(self.bias[:, at:at + 4 * len(halves)], bias).then_inc(self.cols_in, 16)
            sp.dma_start(self.gain[:, g], self.dram["norms"][layer, :, norm or 0]).then_inc(self.cols_in, 16)
            at += 4 * len(halves)
        for n, (layer, half) in enumerate(self.halves):
            if due(n - WADA_RING + 1):
                sp.wait_ge(self.used, n - WADA_RING + 1)
            sp.dma_start(self.w[:, n % WADA_RING], self.dram["w_ada"][layer, half]).then_inc(self.w_in[n % WADA_RING], 16)

    def multiply(self, pe, i):
        n, c = divmod(i, DC)
        if c == 0:
            pe.wait_ge(self.w_in[n % WADA_RING], 16 * (n // WADA_RING + 1))
            if due(n - len(self.row_ps) + 1):
                pe.wait_ge(self.copied, n - len(self.row_ps) + 1)
        mm = pe.matmul(self.row_ps[n % len(self.row_ps)], self.core.cc[:, c], self.w[:, n % WADA_RING, c], start=(c == 0), stop=(c == DC - 1))
        if c == DC - 1:
            mm.then_inc(self.used, 1)
            if n:
                self.turn(pe, n - 1)

    def turn(self, pe, n):
        pe.wait_ge(self.copied, n + 1)
        for j in range(4):
            mm = pe.transpose(self.m_ps[:, 4 * n + j], self.rows[:, n % 2, j * P:(j + 1) * P], self.core.ident[0:2, 0:2])
        mm.then_inc(self.turned, 1)

    def keep(self, act, n):
        act.wait_ge(self.used, n + 1)
        if due(n - 1):
            act.wait_ge(self.turned, n - 1)
        act.activation(self.rows[:, n % 2], self.row_ps[n % len(self.row_ps)], ACT.Copy).then_inc(self.copied, 1)

    def finish(self, dve):
        dve.wait_ge(self.cols_in, 32 * len(self.groups))
        dve.wait_ge(self.turned, self.count)
        at = 0
        for _, halves, _ in self.groups:
            n = 4 * len(halves)
            dve.tensor_tensor(self.core.mod[:, 4 * halves[0]:4 * halves[0] + n], self.m_ps[:, at:at + n],
                              self.bias[:, at:at + n].unsqueeze(2).broadcast_to([P, n, 2]), ALU.add).then_inc(self.step, 1)
            at += n
        dve.wait_ge(self.step, len(self.groups))
        for g, (_, _, norm) in enumerate(self.groups):
            if norm is not None:
                scale = self.core.mod[:, (3 * norm + 1) * DC:(3 * norm + 2) * DC]
                dve.scalar_tensor_tensor(self.core.gain[:, norm], scale, 1.0, self.gain[:, g].unsqueeze(2).broadcast_to([P, DC, 2]),
                                         ALU.add, ALU.mult)


def modulation(core, dram, ahead):
    nc = core.nc
    with ExitStack() as scope:
        ps = core.psum(scope, "mod")
        row_ps, m_ps = ps("row_ps", [2, 2, 512]), ps("m_ps", [P, 4 * len(MOD_FIRST), 2])
        mod = Modulation(core, scope, dram, [(0, MOD_FIRST, 0)], [row_ps[:, 0], row_ps[:, 1]], m_ps[:, :, :])
        c_in, activated, ahead_in = core.semaphore("c_in"), core.semaphore("c_activated"), core.semaphore("ahead_in")
        with nc.Block() as block:

            @block.sync
            def _(sp):
                sp.dma_start(core.cc[:, :, :], dram["c2"]).then_inc(c_in, 16)
                mod.load(sp)
                for to, source in ahead:
                    sp.dma_start(to, source).then_inc(ahead_in, 16)
                sp.wait_ge(ahead_in, 16 * len(ahead))

            @block.scalar
            def _(act):
                act.wait_ge(c_in, 16)
                act.activation(core.cc[:, :, :], core.cc[:, :, :], ACT.Silu).then_inc(activated, 1)
                for n in range(mod.count):
                    mod.keep(act, n)

            @block.tensor
            def _(pe):
                pe.wait_ge(activated, 1)
                for i in range(mod.count * DC):
                    if i == 2 * DC - 1:
                        pe.wait_ge(ahead_in, 16 * len(ahead))
                    mod.multiply(pe, i)
                mod.turn(pe, mod.count - 1)

            @block.vector
            def _(dve):
                mod.finish(dve)


def project_in(core, scope, block, layer, dram, conv_in, tok, wf, wf_in, h_done):
    nc = core.nc
    tag = f"pi{layer}"
    sb = core.sbuf(scope, tag)
    ps = core.psum(scope, tag)
    ring = WF_RING
    wt = sb("wt", [P, DC, TOK_W])
    o_ps = ps("o_ps", [P, 4, 512])
    wt_in, made = core.semaphore("wt_in"), core.semaphore("proj_made")
    copied = [core.semaphore("proj_copied_act"), core.semaphore("proj_copied_dve")]
    padded = core.semaphore("conv_padded")
    width = TOK_W // 4
    products = QKV_C + 4 * UU

    def place(n):
        if n < QKV_C:
            return conv_in[:, n, :, PAD:PAD + T], o_ps[:, n % 4].rearrange("p (s t) -> p s t", s=2)
        u, k = divmod(n - QKV_C, 4)
        return tok[:, u, k * width:(k + 1) * width], o_ps[:, n % 4, 0:width]


    @block.gpsimd
    def _(pool):
        pool.memset(conv_in[:, :, :, 0:PAD], 0.0)
        pool.memset(conv_in[:, :, :, PAD + T:2 * PAD + T], 0.0).then_inc(padded, 1)

    @block.sync
    def _(sp):
        for j in range(ring, QKV_C):
            if j == ring + 2:
                sp.dma_start(wt[:, :, :], dram["w_tok"][layer]).then_inc(wt_in, 16)
            if due(j - ring + 1):
                sp.wait_ge(made, j - ring + 1)
            sp.dma_start(wf[:, j % ring], dram["w_qkv"][layer, j]).then_inc(wf_in[j % ring], 16)

    @block.tensor
    def _(pe):
        for n in range(products):
            b = n % 4
            if due((n - 4) // 2 + 1):
                pe.wait_ge(copied[n % 2], (n - 4) // 2 + 1)
            if n < QKV_C:
                pe.wait_ge(wf_in[n % ring], 16 * (n // ring + 1))
                for c in range(DC):
                    if n == 0:
                        pe.wait_ge(h_done, 2 * (c + 1))
                    mm = pe.matmul(o_ps[:, b], wf[:, n % ring, c], core.h[:, c, :], start=(c == 0), stop=(c == DC - 1))
            else:
                if n == QKV_C:
                    pe.wait_ge(wt_in, 16)
                u, k = divmod(n - QKV_C, 4)
                for c in range(DC):
                    mm = pe.matmul(o_ps[:, b, 0:width], core.h[:, c, u * P:(u + 1) * P],
                                   wt[:, c, k * width:(k + 1) * width], start=(c == 0), stop=(c == DC - 1))
            mm.then_inc(made, 1)

    @block.scalar
    def _(act):
        for n in range(0, products, 2):
            act.wait_ge(made, n + 1)
            act.activation(*place(n), ACT.Copy).then_inc(copied[0], 1)

    @block.vector
    def _(dve):
        for n in range(1, products, 2):
            dve.wait_ge(made, n + 1)
            dve.tensor_copy(*place(n)).then_inc(copied[1], 1)


def short_conv(core, layer, dram, conv_in, qkv, heads_t, consts):
    nc = core.nc
    tag = f"sc{layer}"
    with ExitStack() as scope:
        sb = core.sbuf(scope, tag)
        ps = core.psum(scope, tag)
        conv = sb("conv", [P, QKV_C, 2, T])
        taps = sb("taps", [P, QKV_C, CONV_K])
        sq = sb("sq", [P, 2, 2 * GDN_W])
        norm = sb("norm", [P, UU, 2 * GH])
        t_ps = ps("t_ps", [P, 2, UU, P])
        h_ps = ps("h_ps", [HD, 3, 4, P])
        consts_in = core.semaphore("mix_consts_in")
        taps_in, step, convolved = core.semaphore("taps_in"), core.semaphore("conv_step"), core.semaphore("convolved")
        silud, turned, back = core.semaphore("conv_silu"), core.semaphore("conv_turned"), core.semaphore("conv_token_major")
        squares, roots, unit = core.semaphore("norm_squares"), core.semaphore("norm_roots"), core.semaphore("unit_qk")
        turned_h, kept_h = core.semaphore("heads_turned"), core.semaphore("heads_kept")
        n_steps = [0]
        row_ps, m_ps = ps("row_ps", [2, 2, 512]), ps("m_ps", [P, 4 * len(MOD_GATE), 2])
        mod = Modulation(core, scope, dram, [(layer, MOD_GATE, None)], [row_ps[:, 0], row_ps[:, 1]], m_ps[:, :, :])
        with nc.Block() as block:

            @block.sync
            def _(sp):
                sp.dma_start(taps[:, :, :], dram["conv_w"][layer]).then_inc(taps_in, 16)
                mod.load(sp)
                sp.dma_start(consts[:, :], dram["mix_consts"]).then_inc(consts_in, 16)
                sp.wait_ge(consts_in, 16)

            @block.vector
            def _(dve):
                def link(ins):
                    n_steps[0] += 1
                    ins.then_inc(step, 1)
                    dve.wait_ge(step, n_steps[0])

                dve.wait_ge(taps_in, 16)
                for j0 in range(0, QKV_C, 3):
                    for k in range(CONV_K):
                        for j in range(j0, j0 + 3):
                            src = conv_in[:, j, :, k:k + T]
                            if k == 0:
                                ins = dve.tensor_scalar(conv[:, j], src, taps[:, j, 0:1], None, ALU.mult)
                            else:
                                ins = dve.scalar_tensor_tensor(conv[:, j], src, taps[:, j, k:k + 1], conv[:, j], ALU.mult, ALU.add)
                            if k == CONV_K - 1:
                                ins.then_inc(convolved, 1)
                        if k < CONV_K - 1:
                            link(ins)
                dve.wait_ge(back, QKV_C)
                for u in range(UU):
                    link(dve.tensor_tensor(sq[:, u % 2], qkv[:, u, 0:2 * GDN_W], qkv[:, u, 0:2 * GDN_W], ALU.mult))
                    link(dve.tensor_reduce(norm[:, u], sq[:, u % 2].rearrange("p (h d) -> p h d", d=HD), AX.X, ALU.add))
                dve.tensor_scalar(norm[:, :, :], norm[:, :, :], EPS, None, ALU.add).then_inc(squares, 1)
                dve.wait_ge(roots, 1)
                link(dve.reciprocal(norm[:, :, :], norm[:, :, :]))
                link(dve.tensor_scalar(norm[:, :, 0:GH], norm[:, :, 0:GH], HD ** -0.5, None, ALU.mult))
                for u in range(UU):
                    rows = qkv[:, u, 0:2 * GDN_W].rearrange("p (h d) -> p h d", d=HD)
                    dve.tensor_tensor(rows, rows, norm[:, u].unsqueeze(2).broadcast_to([P, 2 * GH, HD]),
                                      ALU.mult).then_inc(unit, 1)
                mod.finish(dve)

            @block.scalar
            def _(act):
                for j in range(QKV_C):
                    if j > 1 and MOD_BESIDE * (j - 1) % DC == 0:
                        mod.keep(act, MOD_BESIDE * (j - 1) // DC - 1)
                    act.wait_ge(convolved, j + 1)
                    act.activation(conv[:, j], conv[:, j], ACT.Silu).then_inc(silud, 1)
                    if j:
                        act.wait_ge(turned, j)
                        act.activation(qkv[:, :, (j - 1) * P:j * P], t_ps[:, (j - 1) % 2], ACT.Copy).then_inc(back, 1)
                act.wait_ge(turned, QKV_C)
                act.activation(qkv[:, :, (QKV_C - 1) * P:QKV_C * P], t_ps[:, (QKV_C - 1) % 2], ACT.Copy).then_inc(back, 1)
                mod.keep(act, mod.count - 1)
                act.wait_ge(squares, 1)
                act.activation(norm[:, :, :], norm[:, :, :], ACT.Sqrt).then_inc(roots, 1)
                for n in range(3 * UU):
                    u, g = divmod(n, 3)
                    act.wait_ge(turned_h, n + 1)
                    act.activation(heads_t[:, u, 4 * g:4 * g + 4], h_ps[:, g], ACT.Copy).then_inc(kept_h, 1)

            @block.tensor
            def _(pe):
                for j in range(QKV_C):
                    if j:
                        for i in range(MOD_BESIDE * (j - 1), MOD_BESIDE * j):
                            mod.multiply(pe, i)
                    pe.wait_ge(silud, j + 1)
                    if due(j - 1):
                        pe.wait_ge(back, j - 1)
                    for u in range(UU):
                        mm = pe.transpose(t_ps[:, j % 2, u], conv[:, j, u // TT, (u % TT) * P:(u % TT + 1) * P], core.ident)
                    mm.then_inc(turned, 1)
                for n in range(3 * UU):
                    u, g = divmod(n, 3)
                    pe.wait_ge(unit, u + 1)
                    if due(n - 2):
                        pe.wait_ge(kept_h, n - 2)
                    for x in range(4):
                        hd = 4 * g + x
                        mm = pe.transpose(h_ps[:, g, x], qkv[:, u, hd * HD:(hd + 1) * HD], core.ident)
                    mm.then_inc(turned_h, 1)
                mod.turn(pe, mod.count - 1)


def gdn_gates(core, layer, dram, tok, beta, decay_g):
    nc = core.nc
    tag = f"gg{layer}"
    with ExitStack() as scope:
        sb = core.sbuf(scope, tag)
        rate, bias = sb("rate", [P, 2 * GH]), sb("bias", [P, 2 * GH])
        a, neg = sb("a", [P, UU, 2 * GH]), sb("neg", [P, UU, 2 * GH])
        rows_in, step = core.semaphore("gate_rows_in"), core.semaphore("gate_step")
        biased, logged, done = core.semaphore("gate_biased"), core.semaphore("gate_logged"), core.semaphore("gate_act")
        full = [P, UU, 2 * GH]
        b0 = BA_AT
        with nc.Block() as block:

            @block.sync
            def _(sp):
                sp.dma_start(rate[:, :], dram["a_log"][layer].unsqueeze(0).broadcast_to([P, 2 * GH])).then_inc(rows_in, 16)
                sp.dma_start(bias[:, :], dram["dt_bias"][layer].unsqueeze(0).broadcast_to([P, 2 * GH])).then_inc(rows_in, 16)

            @block.vector
            def _(dve):
                dve.wait_ge(rows_in, 32)
                dve.tensor_tensor(a[:, :, :], tok[:, :, b0 + 2 * GH:b0 + 4 * GH], bias[:, :].unsqueeze(1).broadcast_to(full),
                                  ALU.add).then_inc(step, 1)
                dve.wait_ge(step, 1)
                dve.scalar_tensor_tensor(neg[:, :, :], a[:, :, :], -1.0, a[:, :, :], ALU.mult, ALU.min).then_inc(biased, 1)
                dve.wait_ge(logged, 1)
                dve.scalar_tensor_tensor(a[:, :, :], a[:, :, :], 0.0, neg[:, :, :], ALU.max, ALU.add).then_inc(step, 1)
                dve.wait_ge(step, 2)
                dve.scalar_tensor_tensor(decay_g[:, :, :], a[:, :, :], -1.0, rate[:, :].unsqueeze(1).broadcast_to(full),
                                         ALU.mult, ALU.mult)

            @block.scalar
            def _(act):
                act.wait_ge(rows_in, 32)
                act.activation(beta[:, :, :], tok[:, :, b0:b0 + 2 * GH], ACT.Sigmoid)
                act.activation(rate[:, :], rate[:, :], ACT.Exp)
                act.wait_ge(biased, 1)
                act.activation(neg[:, :, :], neg[:, :, :], ACT.Exp).then_inc(done, 1)
                act.wait_ge(done, 1)
                act.activation(neg[:, :, :], neg[:, :, :], ACT.Ln, bias=1.0).then_inc(logged, 1)


def gdn_chunks(core, layer, cst, qkv, heads_t, beta, decay_g, made):
    nc = core.nc
    tag = f"gc{layer}"
    groups = [(u, f) for u in range(UU) for f in range(2)]
    n_groups = len(groups)
    with ExitStack() as scope:
        sb = core.sbuf(scope, tag)
        ps = core.psum(scope, tag)
        three = [P, 3, P]
        wide = [P, 3, P // BLK, BLK]
        gcol, gtot = sb("gcol", [P, UU, 2 * GH]), sb("gtot", [P, UU, 2 * GH])
        bexp, kexp = sb("bexp", [P, UU, 2 * GH]), sb("kexp", [P, UU, 2 * GH])
        lt = sb("lt", [P, 2, UU * GH, P])
        x_rows = sb("x_rows", [P, 2, BLK, BLK])
        xt_rows = sb("xt_rows", [P, 2, BLK, BLK])
        x_own = sb("x_own", [P, 2, BLK, BLK])
        lt_rows, l_own = x_rows, xt_rows
        outer = sb("outer", [P, 2, BLK * BLK // 4])
        dif, xt = ([[sb(f"{k}{d}{r}", three) for r in range(2)] for d in range(2)] for k in ("dif", "xt"))
        y = [sb(f"y{d}", three) for d in range(2)]
        x = dif
        kv = sb("kv", [P, 2, 2, 3, 2 * HD])
        bank = [ps(f"bank{d}", [P, 4, 512]) for d in range(2)]
        S = core.semaphore
        sums, sums_out, decays, scaled, rates = S("g_sums"), S("g_sums_out"), S("g_decays"), S("g_scaled"), S("beta_rates")
        two = lambda name: [S(f"{name}{d}") for d in range(2)]
        products, g_rows, beta_rows = S("kk_qk"), two("g_rows"), two("beta_rows")
        dif_step, decayed, weighed, lower = two("dif_step"), two("decayed"), two("weighed"), two("lower")
        blocks, padded, started = two("blocks_cut"), S("blocks_padded"), S("x_started")
        own, outers, reduced, back = two("blocks_own"), two("outer_made"), two("x_reduced"), two("x_back")
        cuts, x_full, xt_full, sides = two("cuts"), two("x_full"), two("xt_full"), two("kv_sides")
        y_made, y_kept, update_made, solved = two("y_made"), two("y_kept"), two("update_made"), two("x_solved")
        kv_made, kv_kept = two("kv_made"), two("kv_kept")
        tri, neg, cross, diagonal, chunk_ones = cst["tri"], cst["neg"], cst["cross"], cst["diagonal"], cst["chunk_ones"]

        def b3(d, k):
            return bank[d][:, k, 0:3 * P].rearrange("p (h n) -> p h n", h=3)

        def kk(n):
            return b3(n % 2, 0)

        def qk(n):
            return b3(n % 2, 1)

        def spread(eng, to, rows, n, d):
            src = rows[:, d, :, 3 * n:3 * n + 3].rearrange("p c k -> p k c").unsqueeze(2).broadcast_to(wide)
            keep = diagonal.rearrange("p (b c) -> p b c", c=BLK).unsqueeze(1).broadcast_to(wide)
            return eng.tensor_tensor(to.rearrange("p k (b c) -> p k b c", c=BLK), src, keep, ALU.mult)

        with nc.Block() as block:

            @block.tensor
            def _(pe):
                g_ps, w_ps = bank[0][:, 0], bank[1][0:HD, 0]
                for u in range(UU):
                    for d in range(2):
                        a = u * 24 + d * GH
                        pe.matmul(g_ps[:, a:a + GH], tri[d], decay_g[:, u, d * GH:(d + 1) * GH], start=True, stop=True)
                    pe.matmul(g_ps[:, u * 24 + 12:u * 24 + 24], chunk_ones, decay_g[:, u], start=True, stop=True)
                    for c in range(2):
                        a = (2 * u + c) * 12
                        mm = pe.matmul(w_ps[:, a:a + 12], chunk_ones[:, c * HD:(c + 1) * HD], decay_g[:, u], start=True, stop=True)
                mm.then_inc(sums, 1)
                pe.wait_ge(sums_out, 2)
                for n, (u, f) in enumerate(groups):
                    heads = range(3 * f, 3 * f + 3)
                    for d in range(2):
                        if due(n):
                            pe.wait_ge(dif_step[d], 2 * n - 1)
                        for k, h in enumerate(heads):
                            c = d * GH + h
                            mm = pe.matmul(b3(d, 2)[:, k], decay_g[:, u, c:c + 1].broadcast_to([P, P]), tri[d], start=True, stop=True)
                        mm.then_inc(g_rows[d], 1)
                    for d in range(2):
                        if due(n - 1):
                            pe.wait_ge(weighed[d], n - 1)
                    for k, h in enumerate(heads):
                        pe.matmul(kk(n)[:, k], heads_t[:, u, GH + h], heads_t[:, u, GH + h], start=True, stop=True)
                        mm = pe.matmul(qk(n)[:, k], heads_t[:, u, GH + h], heads_t[:, u, h], start=True, stop=True)
                    mm.then_inc(products, 1)
                    for d in range(2):
                        if due(n):
                            pe.wait_ge(lower[d], n)
                        for k, h in enumerate(heads):
                            c = d * GH + h
                            mm = pe.matmul(b3(d, 3)[:, k], beta[:, u, c:c + 1].broadcast_to([P, P]), core.ident, start=True, stop=True)
                        mm.then_inc(beta_rows[d], 1)

                def times_x(n, d):
                    pe.wait_ge(cuts[d], n + 1)
                    pe.wait_ge(x_full[d], n + 1)
                    if n == 0:
                        pe.wait_ge(lower[d], n_groups)
                        pe.wait_ge(weighed[d], n_groups)
                    else:
                        if due(n):
                            pe.wait_ge(y_kept[d], n)
                    for k in range(3):
                        mm = pe.matmul(b3(d, 0)[:, k], lt[:, d, 3 * n + k], x[d][n % 2][:, k], start=True, stop=True)
                    mm.then_inc(y_made[d], 1)

                def x_times(n, d):
                    pe.wait_ge(y_kept[d], n + 1)
                    pe.wait_ge(xt_full[d], n + 1)
                    if due(n):
                        pe.wait_ge(solved[d], n)
                    for k in range(3):
                        mm = pe.matmul(b3(d, 1)[:, k], y[d][:, k], xt[d][n % 2][:, k], start=True, stop=True)
                    mm.then_inc(update_made[d], 1)

                def solve(n, d):
                    pe.wait_ge(solved[d], n + 1)
                    pe.wait_ge(sides[d], n + 1)
                    if due(n):
                        pe.wait_ge(kv_kept[d], n)
                    for k in range(3):
                        mm = pe.matmul(b3(d, 2)[:, k], kv[:, n % 2, d, k], xt[d][n % 2][:, k], start=True, stop=True)
                    mm.then_inc(kv_made[d], 1)

                for d in range(2):
                    times_x(0, d)
                for n in range(n_groups):
                    for d in range(2):
                        x_times(n, d)
                    if n + 1 < n_groups:
                        for d in range(2):
                            times_x(n + 1, d)
                    for d in range(2):
                        solve(n, d)

            @block.vector
            def _(dve):
                dve.wait_ge(sums, 1)
                g_ps = bank[0][:, 0, 0:UU * 24].rearrange("p (u n) -> p u n", u=UU)
                dve.tensor_copy(gcol[:, :, :], g_ps[:, :, 0:12])
                dve.tensor_copy(gtot[:, :, :], g_ps[:, :, 12:24]).then_inc(sums_out, 1)
                dve.wait_ge(sums_out, 2)
                dve.tensor_tensor(kexp[:, :, :], gtot[:, :, :], gcol[:, :, :], ALU.subtract).then_inc(decays, 1)
                dve.wait_ge(scaled, 1)
                dve.scalar_tensor_tensor(bexp[:, :, :], beta[:, :, :], -1.0, made["grow"][:, :, :], ALU.mult, ALU.mult).then_inc(rates, 1)

                def decay(n, d):
                    u, f = groups[n]
                    c = d * GH + 3 * f
                    dve.wait_ge(g_rows[d], n + 1)
                    if due(n - 1):
                        dve.wait_ge(weighed[d], n - 1)
                    dve.tensor_tensor(dif[d][n % 2][:, :, :], b3(d, 2), gcol[:, u, c:c + 3].unsqueeze(2).broadcast_to(three),
                                      ALU.subtract).then_inc(dif_step[d], 1)

                def mask(n, d):
                    dve.wait_ge(dif_step[d], 2 * n + 1)
                    at = dif[d][n % 2][:, :, :]
                    dve.scalar_tensor_tensor(at, at, 0.0, neg[d].unsqueeze(1).broadcast_to(three), ALU.min, ALU.add).then_inc(dif_step[d], 1)

                def weigh(n, d):
                    u, f = groups[n]
                    dve.wait_ge(decayed[d], n + 1)
                    dve.wait_ge(products, n + 1)
                    dve.tensor_tensor(lt[:, d, 3 * n:3 * n + 3], kk(n), dif[d][n % 2][:, :, :], ALU.mult)
                    for a in (0, HD):
                        ins = dve.tensor_tensor(made["attn"][a:a + HD, u, d, 3 * f:3 * f + 3], qk(n)[a:a + HD, :, a:a + HD],
                                                dif[d][n % 2][a:a + HD, :, a:a + HD], ALU.mult)
                    ins.then_inc(weighed[d], 1)

                def scale(n, d):
                    dve.wait_ge(weighed[d], n + 1)
                    dve.wait_ge(beta_rows[d], n + 1)
                    dve.tensor_tensor(lt[:, d, 3 * n:3 * n + 3], lt[:, d, 3 * n:3 * n + 3], b3(d, 3), ALU.mult).then_inc(lower[d], 1)

                for n in range(n_groups + 1):
                    for step, lag in ((decay, 0), (mask, 0), (weigh, 1), (scale, 1)):
                        for d in range(2):
                            if 0 <= n - lag < n_groups:
                                step(n - lag, d)
                for d in range(2):
                    dve.wait_ge(blocks[d], n_groups)
                    dve.wait_ge(padded, 1)
                    dve.transpose(l_own[:, d], lt_rows[:, d]).then_inc(own[d], 1)
                dve.wait_ge(started, 1)
                for j in range(BLK - 1):
                    parts = []
                    for d in range(2):
                        r = j if d == 0 else BLK - 1 - j
                        rows = slice(r + 1, BLK) if d == 0 else slice(0, r)
                        cols = slice(0, r + 1) if d == 0 else slice(r, BLK)
                        shape = [P, BLK - 1 - j, j + 1]
                        o = outer[:, d, 0:shape[1] * shape[2]].rearrange("p (a b) -> p a b", b=shape[2])
                        parts.append((x_own[:, d, rows, cols], o))
                        dve.wait_ge(own[d], 1)
                        if due(j):
                            dve.wait_ge(reduced[d], j)
                        dve.tensor_tensor(o, l_own[:, d, rows, r:r + 1].broadcast_to(shape),
                                          x_own[:, d, r:r + 1, cols].broadcast_to(shape), ALU.mult).then_inc(outers[d], 1)
                    for d, (rest, o) in enumerate(parts):
                        dve.wait_ge(outers[d], j + 1)
                        dve.tensor_tensor(rest, rest, o, ALU.subtract).then_inc(reduced[d], 1)
                for d in range(2):
                    dve.wait_ge(reduced[d], BLK - 1)
                    dve.transpose(x_rows[:, d], x_own[:, d].rearrange("p i j -> p j i")).then_inc(back[d], 1)
                    dve.transpose(xt_rows[:, d], x_own[:, d]).then_inc(back[d], 1)

                for d in range(2):
                    dve.wait_ge(back[d], 2)
                for n in range(n_groups + 1):
                    for d in range(2):
                        if n < n_groups:
                            if due(n - 1):
                                dve.wait_ge(y_made[d], n - 1)
                            spread(dve, x[d][n % 2], x_rows, n, d).then_inc(x_full[d], 1)
                    if n < n_groups:
                        if due(n - 1):
                            dve.wait_ge(kv_made[0], n - 1)
                        spread(dve, xt[0][n % 2], xt_rows, n, 0).then_inc(xt_full[0], 1)
                    for d in range(2):
                        if n:
                            dve.wait_ge(xt_full[d], n)
                            dve.wait_ge(update_made[d], n)
                            xt_n = xt[d][(n - 1) % 2][:, :, :]
                            dve.tensor_tensor(xt_n, xt_n, b3(d, 1), ALU.subtract).then_inc(solved[d], 1)

            @block.scalar
            def _(act):
                act.wait_ge(sums, 1)
                act.activation(made["whole"][:, :, :], bank[1][0:HD, 0, 0:2 * UU * 12].rearrange("p (c n) -> p c n", c=2 * UU),
                               ACT.Exp).then_inc(sums_out, 1)
                act.wait_ge(decays, 1)
                act.activation(kexp[:, :, :], kexp[:, :, :], ACT.Exp)
                act.activation(made["grow"][:, :, :], gcol[:, :, :], ACT.Exp).then_inc(scaled, 1)

                def diagonal_blocks(n, d):
                    act.wait_ge(lower[d], n + 1)
                    for a in range(0, P, BLK):
                        ins = act.activation(lt_rows[a:a + BLK, d, :, 3 * n:3 * n + 3],
                                             lt[a:a + BLK, d, 3 * n:3 * n + 3, a:a + BLK].rearrange("p m c -> p c m"), ACT.Copy)
                    ins.then_inc(blocks[d], 1)

                for n in range(n_groups):
                    for d in range(2):
                        act.wait_ge(dif_step[d], 2 * n + 2)
                        act.activation(dif[d][n % 2][:, :, :], dif[d][n % 2][:, :, :], ACT.Exp).then_inc(decayed[d], 1)
                    for d in range(2):
                        if n:
                            diagonal_blocks(n - 1, d)
                for d in range(2):
                    diagonal_blocks(n_groups - 1, d)

                def keep_y(n, d):
                    act.wait_ge(y_made[d], n + 1)
                    if due(n):
                        act.wait_ge(update_made[d], n)
                    act.activation(y[d][:, :, :], b3(d, 0), ACT.Copy).then_inc(y_kept[d], 1)

                def keep_kv(n, d):
                    u, f = groups[n]
                    act.wait_ge(kv_made[d], n + 1)
                    act.activation(made["kv_t"][:, u, d, 3 * f:3 * f + 3], b3(d, 2), ACT.Copy).then_inc(kv_kept[d], 1)

                for n in range(n_groups + 1):
                    for d in range(2):
                        if n < n_groups:
                            keep_y(n, d)
                    for d in range(2):
                        if n:
                            keep_kv(n - 1, d)

            @block.gpsimd
            def _(pool):
                pool.memset(lt_rows[:, :, :, UU * GH:BLK], 0.0).then_inc(padded, 1)
                pool.memset(x_own[:, :, :, :], 0.0).then_inc(rates, 1)
                pool.wait_ge(rates, 2)
                pool.memset(x_own[:, :, :, :].rearrange("p d i j -> p d (i j)")[:, :, 0:BLK * BLK:BLK + 1], 1.0).then_inc(started, 1)
                six = [P, GH, HD]
                for u in range(UU):
                    for d in range(2):
                        k = qkv[:, u, GDN_W:2 * GDN_W].rearrange("p (h e) -> p h e", e=HD)
                        pool.tensor_tensor(made["key_dec"][:, u, d], k, kexp[:, u, d * GH:(d + 1) * GH].unsqueeze(2).broadcast_to(six), ALU.mult)
                for n in range(n_groups):
                    for d in range(2):
                        pool.wait_ge(blocks[d], n + 1)
                        pool.tensor_tensor(lt[:, d, 3 * n:3 * n + 3], lt[:, d, 3 * n:3 * n + 3], cross[d].unsqueeze(1).broadcast_to(three),
                                           ALU.mult).then_inc(cuts[d], 1)
                for n, (u, f) in enumerate(groups):
                    for d in range(2):
                        if due(n - 1):
                            pool.wait_ge(kv_made[d], n - 1)
                        c = d * GH + 3 * f
                        for part, (rate, at) in enumerate(((bexp, GDN_W), (beta, 2 * GDN_W))):
                            src = qkv[:, u, at + 3 * f * HD:at + 3 * (f + 1) * HD].rearrange("p (h e) -> p h e", e=HD)
                            ins = pool.tensor_tensor(kv[:, n % 2, d, :, part * HD:(part + 1) * HD], src,
                                                     rate[:, u, c:c + 3].unsqueeze(2).broadcast_to([P, 3, HD]), ALU.mult)
                        ins.then_inc(sides[d], 1)
                    pool.wait_ge(back[1], 2)
                    spread(pool, xt[1][n % 2], xt_rows, n, 1).then_inc(xt_full[1], 1)


def gdn_states(core, layer, need_ctx, heads_t, made):
    nc = core.nc
    tag = f"gs{layer}"
    with ExitStack() as scope:
        sb = core.sbuf(scope, tag)
        ps = core.psum(scope, tag)
        over = [sb(f"state{d}", [P, GH, HD]) for d in range(2)]
        state = [over[d][0:HD] for d in range(2)]
        new = [sb(f"new{d}", [P, GH, HD]) for d in range(2)]
        part = [sb(f"part{d}", [P, GH, HD]) for d in range(2)]
        bank = [ps(f"bank{d}", [P, 4, 512]) for d in range(2)]
        S = core.semaphore
        two = lambda name: [S(f"{name}{d}") for d in range(2)]
        zeroed, read, corrected = two("state_zeroed"), two("state_read"), two("value_corrected")
        added, decayed, stated, outed = two("chunk_added"), two("state_decayed"), two("state_new"), two("out_part")
        out_done = two("out_done")
        steps = 2 * T // HD

        def place(n, d):
            ch = n % 4 if d == 0 else 3 - n % 4
            u = (TT if n < 4 else 0) + ch // 2
            return u, HD * (ch % 2), n >= 4 or need_ctx, 2 * u + ch % 2

        def b6(d, k, a, rows=HD):
            return bank[d][a:a + rows, k, 0:GH * HD].rearrange("p (h e) -> p h e", h=GH)

        with nc.Block() as block:

            @block.tensor
            def _(pe):
                for n in range(steps):
                    for d in range(2):
                        u, a, out, _ = place(n, d)
                        pe.wait_ge(zeroed[d], 1)
                        if due(n):
                            pe.wait_ge(stated[d], n)
                        if n:
                            if due(n):
                                pe.wait_ge(out_done[d], n)
                        for h in range(GH):
                            mm = pe.matmul(b6(d, 0, a)[:, h], made["kv_t"][:, u, d, h, a:a + HD], over[d][:, h], start=True, stop=True)
                        if out:
                            for h in range(GH):
                                mm = pe.matmul(b6(d, 1, a)[:, h], heads_t[:, u, h, a:a + HD], state[d][:, h], start=True, stop=True)
                        mm.then_inc(read[d], 1)
                    for d in range(2):
                        u, a, out, _ = place(n, d)
                        pe.wait_ge(corrected[d], n + 1)
                        for h in range(GH):
                            mm = pe.matmul(b6(d, 2, 0)[:, h], made["key_dec"][a:a + HD, u, d, h], new[d][a:a + HD, h], start=True, stop=True)
                        if out:
                            for h in range(GH):
                                mm = pe.matmul(b6(d, 3, a)[:, h], made["attn"][a:a + HD, u, d, h], new[d][a:a + HD, h],
                                               start=True, stop=True)
                        mm.then_inc(added[d], 1)

            @block.vector
            def _(dve):
                for d in range(2):
                    dve.tensor_copy(over[d][HD:P], core.ident[HD:P, HD:P].unsqueeze(1).broadcast_to([HD, GH, HD]))
                    dve.memset(state[d], 0.0).then_inc(zeroed[d], 1)
                six = [HD, GH, HD]
                for n in range(steps):
                    for d in range(2):
                        u, a, out, c = place(n, d)
                        dve.wait_ge(read[d], n + 1)
                        dve.tensor_copy(new[d][a:a + HD], b6(d, 0, a)).then_inc(corrected[d], 1)
                    for d in range(2):
                        u, a, out, c = place(n, d)
                        dve.wait_ge(zeroed[d], 1)
                        if due(n):
                            dve.wait_ge(stated[d], n)
                        dve.tensor_tensor(state[d], state[d],
                                          made["whole"][:, c, d * GH:(d + 1) * GH].unsqueeze(2).broadcast_to(six),
                                          ALU.mult).then_inc(decayed[d], 1)
                        if out:
                            if due(n):
                                dve.wait_ge(out_done[d], n)
                            dve.tensor_tensor(part[d][a:a + HD], b6(d, 1, a),
                                              made["grow"][a:a + HD, u, d * GH:(d + 1) * GH].unsqueeze(2).broadcast_to(six),
                                              ALU.mult).then_inc(outed[d], 1)
                        else:
                            dve.engine_nop().then_inc(outed[d], 1)
                    for d in range(2):
                        u, a, out, c = place(n, d)
                        dve.wait_ge(added[d], n + 1)
                        dve.wait_ge(decayed[d], n + 1)
                        dve.tensor_tensor(state[d], state[d], b6(d, 2, 0), ALU.add).then_inc(stated[d], 1)
                        dve.wait_ge(outed[d], n + 1)
                        if out:
                            dve.wait_ge(corrected[d], n + 1)
                            dve.tensor_tensor(made["out"][a:a + HD, u, d], part[d][a:a + HD], b6(d, 3, a), ALU.add).then_inc(out_done[d], 1)
                        else:
                            dve.engine_nop().then_inc(out_done[d], 1)


def gdn_finish(core, scope, block, layer, tiles, dram, tok, made):
    nc = core.nc
    tag = f"gf{layer}"
    sb = core.sbuf(scope, tag)
    gain = sb("gain", [P, HD])
    sq = sb("sq", [P, tiles, GH, HD])
    n2 = sb("n2", [P, tiles, GH])
    z = sb("z", [P, tiles, GDN_W])
    gain_in, step = core.semaphore("gdn_gain_in"), core.semaphore("finish_step")
    squares, roots, gated = core.semaphore("out_squares"), core.semaphore("out_roots"), core.semaphore("z_silu")
    n_steps = [0]
    full = [P, tiles * GH, HD]

    @block.sync
    def _(sp):
        sp.dma_start(gain[:, :], dram["gdn_norm"][layer].unsqueeze(0).broadcast_to([P, HD])).then_inc(gain_in, 16)

    @block.scalar
    def _(act):
        act.activation(z[:, :, :], tok[:, 0:tiles, Z_AT:Z_AT + GDN_W], ACT.Silu).then_inc(gated, 1)
        act.wait_ge(squares, 1)
        act.activation(n2[:, :, :], n2[:, :, :], ACT.Sqrt).then_inc(roots, 1)

    @block.vector
    def _(dve):
        def link(ins):
            n_steps[0] += 1
            ins.then_inc(step, 1)
            dve.wait_ge(step, n_steps[0])

        o = made["out"][:, 0:tiles, 0]
        link(dve.tensor_tensor(o, o, made["out"][:, 0:tiles, 1], ALU.add))
        link(dve.tensor_tensor(sq[:, :, :, :], o, o, ALU.mult))
        link(dve.tensor_reduce(n2[:, :, :], sq[:, :, :, :], AX.X, ALU.add))
        dve.tensor_scalar(n2[:, :, :], n2[:, :, :], 1.0 / HD, EPS, ALU.mult, ALU.add).then_inc(squares, 1)
        dve.wait_ge(roots, 1)
        link(dve.reciprocal(n2[:, :, :], n2[:, :, :]))
        link(dve.tensor_tensor(o, o, n2[:, :, :].unsqueeze(3).broadcast_to([P, tiles, GH, HD]), ALU.mult))
        dve.wait_ge(gain_in, 16)
        g = gain[:, :].unsqueeze(1).unsqueeze(1).broadcast_to([P, tiles, GH, HD])
        link(dve.tensor_tensor(o, o, g, ALU.mult))
        dve.wait_ge(gated, 1)
        dve.tensor_tensor(tok[:, 0:tiles, Z_AT:Z_AT + GDN_W], o.rearrange("p u h e -> p u (h e)"),
                          z[:, :, :], ALU.mult)


def pooling(core, scope, block, layer, streams, dram, tok, a_ps, o_ps):
    nc = core.nc
    tag = f"pl{layer}"
    sb = core.sbuf(scope, tag)
    w = sb("w", [HD, 4, HD])
    scale = sb("scale", [P, POOL_W])
    pooled = sb("pooled", [HD, streams, 4, T])
    rows_in, summed = core.semaphore("pool_rows_in"), core.semaphore("pool_summed")
    kept, made, done = core.semaphore("pool_kept"), core.semaphore("pool_made"), core.semaphore("pool_scaled")
    band = sb("band", [P, 4, TT, T])

    @block.sync
    def _(sp):
        sp.dma_start(w[:, :, :], dram["w_pool"][layer]).then_inc(rows_in, 16)
        sp.dma_start(band[:, :, :, :], dram["band"]).then_inc(rows_in, 16)
        sp.dma_start(scale[:, :], dram["pool_scale"][layer].unsqueeze(0).broadcast_to([P, POOL_W])).then_inc(rows_in, 16)

    @block.tensor
    def _(pe):
        pe.wait_ge(rows_in, 48)
        for n in range(2 * streams):
            s, b = divmod(n, 2)
            if due(n - 1):
                pe.wait_ge(kept, n - 1)
            for x in range(2):
                g = 2 * b + x
                for k in range(TT):
                    mm = pe.matmul(a_ps[0:HD, b, x * T:(x + 1) * T], tok[:, s * TT + k, g * HD:(g + 1) * HD], band[:, g, k],
                                   start=(k == 0), stop=(k == TT - 1))
            mm.then_inc(summed, 1)
        for u in range(streams * TT):
            pe.wait_ge(kept, 2 * (u // TT) + 2)
            if due(u - 1):
                pe.wait_ge(done, u - 1)
            for g in range(4):
                mm = pe.matmul(o_ps[:, u % 2, g * HD:(g + 1) * HD], pooled[:, u // TT, g, (u % TT) * P:(u % TT + 1) * P],
                               w[:, g], start=True, stop=True)
            mm.then_inc(made, 1)

    @block.scalar
    def _(act):
        for n in range(2 * streams):
            s, b = divmod(n, 2)
            act.wait_ge(summed, n + 1)
            act.activation(pooled[:, s, 2 * b:2 * b + 2], a_ps[0:HD, b].rearrange("p (x t) -> p x t", x=2), ACT.Copy).then_inc(kept, 1)

    @block.vector
    def _(dve):
        dve.wait_ge(rows_in, 48)
        for u in range(streams * TT):
            dve.wait_ge(made, u + 1)
            dve.tensor_tensor(tok[:, u, 0:POOL_W], o_ps[:, u % 2, 0:POOL_W], scale[:, :], ALU.mult).then_inc(done, 1)

    return (kept, 2 * streams), (done, streams * TT)


def attention(core, scope, block, layer, need_ctx, dram, tok, s_ps, o_ps, banks_free):
    nc = core.nc
    tag = f"at{layer}"
    sb = core.sbuf(scope, tag)
    ps = core.psum(scope, tag)
    heads = AH + KV
    sink = sb("sink", [P, AH])
    roped = sb("roped", [P, TT, heads * HD])
    tmp = sb("tmp", [P, 2, TT, heads * 2 * 16])
    q_t, k_t = sb("q_t", [HD, UU, AH, P]), sb("k_t", [HD, KV, 2 * T])
    s_sb, p_sb, p_t = sb("s_sb", [P, 2, 2 * T]), sb("p_sb", [P, 2, 2 * T]), sb("p_t", [P, 2, UU, P])
    units = [(u, h) for u in range(UU if need_ctx else TT) for h in range(AH)]
    small = sb("small", [P, 6, len(units)])
    t_ps, h_ps = ps("t_ps", [P, 2, UU, P]), ps("h_ps", [P, 2, 4, P])
    row_ps = [h_ps[0:2, 0].rearrange("p a b -> p (a b)")]
    m_ps = h_ps[:, 1].rearrange("p a b -> p (a b)")[:, 0:8 * len(MOD_SECOND + MOD_FIRST)].rearrange("p (n s) -> p n s", s=2)
    groups = [(layer, MOD_SECOND, 1)] + ([(layer + 1, MOD_FIRST, 0)] if need_ctx else [])
    mod = Modulation(core, scope, dram, groups, row_ps, m_ps)
    beside = -(-mod.count * DC // len(units))
    last_beside = [(DC * (half + 1) - 1) // beside for half in range(mod.count)]
    S = core.semaphore
    sink_in, rope_step, roped_s = S("sink_in"), S("rope_step"), S("roped")
    turned, kept = S("att_turned"), S("att_kept")
    scored, masked, peaked, raised, totals = S("att_scored"), S("att_masked"), S("att_peaked"), S("att_raised"), S("att_totals")
    p_turned, p_kept, summed, done = S("p_turned"), S("p_kept"), S("att_summed"), S("att_done")
    peak_found, added_up, inverted = S("peak_found"), S("totals_added"), S("totals_inverted")
    rope, amask = sb("rope", [P, 2, TT, 2, 16]), sb("amask", [P, TT, 2 * T])
    cos, sin = rope[:, 0], rope[:, 1]
    n_rope = [0]
    turns = [(u, x) for u in range(UU) for x in range(2)]
    peak, minus, total, sunk, inv = (small[:, i] for i in range(5))

    def keys(u):
        return slice(0, 2 * T) if u < TT else slice(T, 2 * T)


    @block.sync
    def _(sp):
        sp.dma_start(rope[:, :, :, :, :], dram["rope"]).then_inc(sink_in, 16)
        sp.dma_start(amask[:, :, :], dram["amask"]).then_inc(sink_in, 16)
        sp.dma_start(sink[:, :], dram["sink"][layer].unsqueeze(0).broadcast_to([P, AH])).then_inc(sink_in, 16)
        mod.load(sp)

    @block.vector
    def _(dve):
        def link(ins):
            n_rope[0] += 1
            ins.then_inc(rope_step, 1)
            dve.wait_ge(rope_step, n_rope[0])

        dve.wait_ge(sink_in, 48)
        half = [P, heads, 2, 16]
        for u in range(TT):
            src = tok[:, u, Q_AT:Q_AT + heads * HD].rearrange("p (h a x i) -> p h a x i", h=heads, a=2, x=2)
            dst = roped[:, u].rearrange("p (h a x i) -> p h a x i", h=heads, a=2, x=2)
            ts = [tmp[:, k, u].rearrange("p (h a i) -> p h a i", h=heads, a=2) for k in range(2)]
            c = cos[:, u].unsqueeze(1).broadcast_to(half)
            s = sin[:, u].unsqueeze(1).broadcast_to(half)
            dve.tensor_tensor(ts[0], src[:, :, :, 1], s, ALU.mult)
            dve.tensor_tensor(ts[1], src[:, :, :, 0], s, ALU.mult)
            dve.tensor_tensor(dst[:, :, :, 0], src[:, :, :, 0], c, ALU.mult)
            link(dve.tensor_tensor(dst[:, :, :, 1], src[:, :, :, 1], c, ALU.mult))
            dve.tensor_tensor(dst[:, :, :, 0], dst[:, :, :, 0], ts[0], ALU.subtract)
            dve.tensor_tensor(dst[:, :, :, 1], dst[:, :, :, 1], ts[1], ALU.add).then_inc(roped_s, 1)

        def back(n):
            u, h = units[n]
            dve.wait_ge(totals, n + 1)
            dve.tensor_tensor(total[:, n:n + 1], total[:, n:n + 1], sunk[:, n:n + 1], ALU.add).then_inc(added_up, 1)
            dve.wait_ge(added_up, n + 1)
            dve.reciprocal(inv[:, n:n + 1], total[:, n:n + 1]).then_inc(inverted, 1)
            dve.wait_ge(summed, n + 1)
            dve.wait_ge(inverted, n + 1)
            dve.tensor_scalar(tok[:, u, Q_AT + h * HD:Q_AT + (h + 1) * HD], o_ps[:, n % 2, 0:HD],
                              inv[:, n:n + 1], None, ALU.mult).then_inc(done, 1)

        def front(n):
            u, h = units[n]
            w = slice(0, 2 * T) if u < TT else slice(0, T)
            dve.wait_ge(scored, n + 1)
            if due(n - 1):
                dve.wait_ge(raised, n - 1)
            if u < TT:
                ins = dve.scalar_tensor_tensor(s_sb[:, n % 2, w], s_ps[:, n % 2, w], HD ** -0.5, amask[:, u], ALU.mult, ALU.add)
            else:
                ins = dve.tensor_scalar(s_sb[:, n % 2, w], s_ps[:, n % 2, w], HD ** -0.5, None, ALU.mult)
            ins.then_inc(masked, 1)
            dve.wait_ge(masked, n + 1)
            dve.tensor_reduce(peak[:, n:n + 1], s_sb[:, n % 2, w], AX.X, ALU.max).then_inc(peak_found, 1)
            dve.wait_ge(peak_found, n + 1)
            dve.tensor_scalar(minus[:, n:n + 1], peak[:, n:n + 1], sink[:, h:h + 1], -1.0, ALU.max, ALU.mult).then_inc(peaked, 1)

        for n in range(len(units) + 3):
            if n < len(units):
                front(n)
            if n >= 3:
                back(n - 3)
        mod.finish(dve)

    @block.scalar
    def _(act):
        for n, (u, x) in enumerate(turns):
            act.wait_ge(turned, n + 1)
            if x == 0:
                act.activation(q_t[:, u, 0:4], h_ps[0:HD, x], ACT.Copy).then_inc(kept, 1)
            else:
                act.activation(q_t[:, u, 4:6], h_ps[0:HD, x, 0:2], ACT.Copy)
                act.activation(k_t[:, :, u * P:(u + 1) * P], h_ps[0:HD, x, 2:4], ACT.Copy).then_inc(kept, 1)
        act.wait_ge(sink_in, 48)

        def raise_(n):
            u, h = units[n]
            w = slice(0, 2 * T) if u < TT else slice(0, T)
            act.wait_ge(peaked, n + 1)
            if due(n - 1):
                act.wait_ge(p_turned, n - 1)
            act.activation(p_sb[:, n % 2, w], s_sb[:, n % 2, w], ACT.Exp, bias=minus[:, n:n + 1],
                           accum_out=total[:, n:n + 1]).then_inc(raised, 1)
            act.activation(sunk[:, n:n + 1], sink[:, h:h + 1], ACT.Exp, bias=minus[:, n:n + 1]).then_inc(totals, 1)

        def keep(n):
            u, _ = units[n]
            w = slice(0, UU) if u < TT else slice(0, TT)
            act.wait_ge(p_turned, n + 1)
            if due(n - 1):
                act.wait_ge(summed, n - 1)
            act.activation(p_t[:, n % 2, w], t_ps[:, n % 2, w], ACT.Copy).then_inc(p_kept, 1)

        for n in range(len(units) + 1):
            if n < len(units):
                raise_(n)
                for half in range(mod.count):
                    if last_beside[half] == n:
                        mod.keep(act, half)
            if n >= 1:
                keep(n - 1)

    @block.tensor
    def _(pe):
        for n, (u, x) in enumerate(turns):
            if u < TT:
                pe.wait_ge(roped_s, u + 1)
            if due(n - 1):
                pe.wait_ge(kept, n - 1)
            for k in range(4):
                a = (4 * x + k) * HD
                src = roped[:, u, a:a + HD] if u < TT else tok[:, u, Q_AT + a:Q_AT + a + HD]
                mm = pe.transpose(h_ps[0:HD, x, k], src, core.ident)
            mm.then_inc(turned, 1)
        for others, count in banks_free:
            pe.wait_ge(others, count)
        pe.wait_ge(kept, len(turns))

        def score(n):
            u, h = units[n]
            if due(n - 1):
                pe.wait_ge(masked, n - 1)
            ks = keys(u)
            pe.matmul(s_ps[:, n % 2, 0:ks.stop - ks.start], q_t[:, u, h], k_t[:, h // (AH // KV), ks],
                      start=True, stop=True).then_inc(scored, 1)

        def turn(n):
            u, h = units[n]
            pe.wait_ge(raised, n + 1)
            if due(n - 1):
                pe.wait_ge(p_kept, n - 1)
            for k in range(UU if u < TT else TT):
                mm = pe.transpose(t_ps[:, n % 2, k], p_sb[:, n % 2, k * P:(k + 1) * P], core.ident)
            mm.then_inc(p_turned, 1)

        def weigh(n):
            u, h = units[n]
            pe.wait_ge(p_kept, n + 1)
            if due(n - 1):
                pe.wait_ge(done, n - 1)
            tiles = range(UU) if u < TT else range(TT, UU)
            for k, t in enumerate(tiles):
                a = V_AT + (h // (AH // KV)) * HD
                mm = pe.matmul(o_ps[:, n % 2, 0:HD], p_t[:, n % 2, k], tok[:, t, a:a + HD],
                               start=(k == 0), stop=(k == len(tiles) - 1))
            mm.then_inc(summed, 1)

        for n in range(len(units) + 2):
            if n < len(units):
                score(n)
                for i in range(beside * n, min(beside * (n + 1), mod.count * DC)):
                    mod.multiply(pe, i)
            if 1 <= n <= len(units):
                turn(n - 1)
            if n >= 2:
                weigh(n - 2)
        mod.turn(pe, mod.count - 1)


def project_out(core, layer, streams, dram, tok):
    nc = core.nc
    tag = f"po{layer}"
    n_tok = streams * T
    with ExitStack() as scope:
        sb = core.sbuf(scope, tag)
        ps = core.psum(scope, tag)
        ring = 3
        w = sb("w", [P, ring, DC, P])
        y_t = sb("y_t", [P, DC, n_tok])
        t_ps, o_ps = ps("t_ps", [P, 2, 512]), ps("o_ps", [P, 2, 512])
        w_in = [core.semaphore(f"wo_in{r}") for r in range(ring)]
        turned, kept, made, added = (core.semaphore(x) for x in ("y_turned_o", "y_kept_o", "out_made", "out_added"))
        with nc.Block() as block:

            @block.sync
            def _(sp):
                for j in range(DC):
                    if due(j - ring + 1):
                        sp.wait_ge(made, j - ring + 1)
                    sp.dma_start(w[:, j % ring], dram["w_out"][layer, j]).then_inc(w_in[j % ring], 16)

            @block.tensor
            def _(pe):
                for c in range(DC):
                    if due(c - 1):
                        pe.wait_ge(kept, c - 1)
                    for u in range(streams * TT):
                        mm = pe.transpose(t_ps[:, c % 2, u * P:(u + 1) * P], tok[:, u, MIXED_AT[c]:MIXED_AT[c] + P], core.ident)
                    mm.then_inc(turned, 1)
                pe.wait_ge(kept, DC)
                for j in range(DC):
                    pe.wait_ge(w_in[j % ring], 16 * (j // ring + 1))
                    if due(streams * (j - 1)):
                        pe.wait_ge(added, streams * (j - 1))
                    for c in range(DC):
                        mm = pe.matmul(o_ps[:, j % 2, 0:n_tok], w[:, j % ring, c], y_t[:, c], start=(c == 0), stop=(c == DC - 1))
                    mm.then_inc(made, 1)

            @block.scalar
            def _(act):
                for c in range(DC):
                    act.wait_ge(turned, c + 1)
                    act.activation(y_t[:, c], t_ps[:, c % 2, 0:n_tok], ACT.Copy).then_inc(kept, 1)

            @block.vector
            def _(dve):
                for j in range(DC):
                    dve.wait_ge(made, j + 1)
                    for s in range(streams):
                        cols = slice(s * T, (s + 1) * T)
                        dve.scalar_tensor_tensor(core.x[:, j, cols], o_ps[:, j % 2, cols], core.mod[:, 2 * DC + j, s:s + 1],
                                                 core.x[:, j, cols], ALU.mult, ALU.add).then_inc(added, 1)


def mixing(core, layer, need_ctx, dram):
    nc = core.nc
    tag = f"mx{layer}"
    streams = 2 if need_ctx else 1
    with ExitStack() as scope:
        sb = core.sbuf(scope, tag)
        tok = sb("tok", [P, UU, TOK_W])
        consts = sb("consts", [P, CONSTS])
        cst = {}
        at = 0
        for name, shape in MIX_CONSTS:
            n = int(np.prod(shape))
            cst[name] = consts[:, at:at + n]
            at += n
        cst["tri"] = [cst["tri"][:, d * P:(d + 1) * P] for d in range(2)]
        cst["neg"] = [cst["neg"][:, d * P:(d + 1) * P] for d in range(2)]
        cst["cross"] = [cst["cross"][:, d * P:(d + 1) * P] for d in range(2)]
        qkv = sb("qkv", [P, UU, 3 * GDN_W])
        with ExitStack() as inner:
            heads_sb = core.sbuf(inner, tag)
            heads_t = heads_sb("heads_t", [HD, UU, 2 * GH, P])
            beta = heads_sb("beta", [P, UU, 2 * GH])
            decay_g = heads_sb("decay_g", [P, UU, 2 * GH])
            with ExitStack() as first:
                conv_in = core.sbuf(first, tag)("conv_in", [P, QKV_C, 2, T + 2 * PAD])
                with ExitStack() as hs:
                    core.h = core.sbuf(hs, tag)("h", [P, DC, 2 * T])
                    parts = [(slice(s * T, (s + 1) * T), [core.mod[:, c, s:s + 1] for c in range(DC)],
                              [core.gain[:, 0, c, s:s + 1] for c in range(DC)]) for s in range(2)]
                    wf = core.sbuf(hs, tag)("wf", [P, WF_RING, DC, P])
                    wf_in = [core.semaphore(f"wf_in{r}") for r in range(WF_RING)]
                    ahead = [(wf[:, r], dram["w_qkv"][layer, r], wf_in[r]) for r in range(WF_RING)]
                    with nc.Block() as block:
                        h_done = normalize(core, hs, block, tag + "n", slice(0, 2 * T), parts, ahead)
                        project_in(core, hs, block, layer, dram, conv_in, tok, wf, wf_in, h_done)
                short_conv(core, layer, dram, conv_in, qkv, heads_t, consts)
                core.end_stage()
            gdn_gates(core, layer, dram, tok, beta, decay_g)
            made = {
                "attn": heads_sb("attn", [P, UU, 2, GH, HD]),
                "kv_t": heads_sb("kv_t", [P, UU, 2, GH, P]),
                "key_dec": heads_sb("key_dec", [P, UU, 2, GH, HD]),
                "grow": heads_sb("grow", [P, UU, 2 * GH]),
                "whole": heads_sb("whole", [HD, 2 * UU, 2 * GH]),
            }
            gdn_chunks(core, layer, cst, qkv, heads_t, beta, decay_g, made)
            core.end_stage()
            made["out"] = qkv[:, :, 0:2 * GDN_W].rearrange("p u (d h e) -> p u d h e", d=2, h=GH)
            gdn_states(core, layer, need_ctx, heads_t, made)
            core.end_stage()
        with ExitStack() as inner:
            s_ps, o_ps = (core.psum(inner, tag)(name, [P, 2, 512]) for name in ("s_ps", "o_ps"))
            with nc.Block() as block:
                banks_free = pooling(core, inner, block, layer, streams, dram, tok, s_ps, o_ps)
                gdn_finish(core, inner, block, layer, streams * TT, dram, tok, made)
                attention(core, inner, block, layer, need_ctx, dram, tok, s_ps, o_ps, banks_free)
        project_out(core, layer, streams, dram, tok)


def topk(core, scope, block, tag, dram, layer, keys, wq, keys_in, wq_in, h_done, top, top_i, best, best_i):
    nc = core.nc
    h = core.h
    sb = core.sbuf(scope, tag)
    ps = core.psum(scope, tag)
    q_sb = sb("q_sb", [P, 2, T])
    s_sb = sb("s_sb", [P, 2, TT, N_KEYS])
    s_cut = sb("s_cut", [P, TT, N_KEYS])
    cand = sb("cand", [P, TT, TOPK, TOPK])
    cand_cut = sb("cand_cut", [P, TT, TOPK * TOPK])
    q_ps = ps("q_ps", [P, 2, 512])
    s_ps = ps("s_ps", [P, 2, 512])
    q_made, q_copied = core.semaphore("q_made"), core.semaphore("q_copied")
    s_made, s_copied = core.semaphore("s_made"), core.semaphore("s_copied")
    picked, step = core.semaphore("picked"), core.semaphore("topk_step")
    n_steps = [0]

    @block.sync
    def _(sp):
        for g in range(WQ_RING, GROUPS):
            sp.wait_ge(q_made, g - WQ_RING + 1)
            sp.dma_start(wq[:, g % WQ_RING], dram["wq"][layer, g]).then_inc(wq_in[g % WQ_RING], 16)

    @block.tensor
    def _(pe):
        def queries(g):
            pe.wait_ge(wq_in[g % WQ_RING], 16 * (g // WQ_RING + 1))
            if due(g - 1):
                pe.wait_ge(q_copied, g - 1)
            for c in range(DC):
                if g == 0:
                    pe.wait_ge(h_done, c + 1)
                mm = pe.matmul(q_ps[:, g % 2, 0:T], wq[:, g % WQ_RING, c], h[:, c, 0:T],
                               start=(c == 0), stop=(c == DC - 1))
            mm.then_inc(q_made, 1)

        def scores(g):
            if g == 0:
                pe.wait_ge(keys_in, 16)
            pe.wait_ge(q_copied, g + 1)
            if due(g - 1):
                pe.wait_ge(s_copied, g - 1)
            for u in range(TT):
                mm = pe.matmul(s_ps[:, g % 2, u * P:(u + 1) * P], q_sb[:, g % 2, u * P:(u + 1) * P],
                               keys[:, g], start=True, stop=True)
            mm.then_inc(s_made, 1)

        queries(0)
        for g in range(GROUPS):
            if g + 1 < GROUPS:
                queries(g + 1)
            scores(g)

    @block.scalar
    def _(act):
        for g in range(GROUPS):
            act.wait_ge(q_made, g + 1)
            if due(g - 1):
                act.wait_ge(s_made, g - 1)
            act.activation(q_sb[:, g % 2, :], q_ps[:, g % 2, 0:T], ACT.Copy).then_inc(q_copied, 1)
            act.wait_ge(s_made, g + 1)
            if due(g - 1):
                act.wait_ge(picked, g - 1)
            act.activation(s_sb[:, g % 2], s_ps[:, g % 2, 0:T], ACT.Copy).then_inc(s_copied, 1)

    @block.vector
    def _(dve):
        def linked(ins):
            n_steps[0] += 1
            ins.then_inc(step, 1)
            dve.wait_ge(step, n_steps[0])

        def best16(values, indices, scores, cut):
            for u in range(TT):
                last = dve.max(values(u)[:, 0:8], scores(u))
            linked(last)
            for u in range(TT):
                last = dve.match_replace(cut(u), values(u)[:, 0:8], scores(u), LOWEST)
            for u in range(TT):
                dve.max_index(indices(u)[:, 0:8], values(u)[:, 0:8], scores(u))
            linked(last)
            for u in range(TT):
                last = dve.max(values(u)[:, 8:16], cut(u))
            linked(last)
            for u in range(TT):
                last = dve.max_index(indices(u)[:, 8:16], values(u)[:, 8:16], cut(u))
            return last

        for g in range(GROUPS):
            dve.wait_ge(s_copied, g + 1)
            best16(lambda u: top[:, u, g], lambda u: top_i[:, u, g], lambda u: s_sb[:, g % 2, u],
                   lambda u: s_cut[:, u]).then_inc(picked, 1)
            if g % 2:
                hd = g // 2
                for u in range(TT):
                    a = top[:, u, g - 1].unsqueeze(2).broadcast_to([P, TOPK, TOPK])
                    b = top[:, u, g].unsqueeze(1).broadcast_to([P, TOPK, TOPK])
                    last = dve.tensor_tensor(cand[:, u], a, b, ALU.add)
                linked(last)
                flat = cand[:, :, :, :].rearrange("p u a b -> p u (a b)")
                best16(lambda u: best[:, u, hd], lambda u: best_i[:, u, hd], lambda u: flat[:, u],
                       lambda u: cand_cut[:, u])


def gate_matrix(core, tag, dram, top_i, best, best_i, stage, ahead):
    nc = core.nc
    with ExitStack() as scope:
        sb = core.sbuf(scope, tag)
        ps = core.psum(scope, tag)
        key_f = sb("key_f", [P, GROUPS, TOPK])
        rank_u = sb("rank_u", [P, 2, HEADS, TOPK], U32)
        rank = sb("rank", [P, 2, HEADS, TOPK])
        hot = sb("hot", [P, 2, HEADS, TOPK, TOPK])
        gate = sb("gate", [P, HEADS, TOPK])
        slot_key = sb("slot_key", [P, 2, SLOTS])
        sums, inv = sb("sums", [P, HEADS]), sb("inv", [P, HEADS])
        slot_major = sb("slot_major", [P, 3, TT, P])
        first = sb("first", [P, ROUND, N_KEYS])
        second = sb("second", [P, ROUND, N_KEYS])
        t_ps = ps("t_ps", [P, 512])
        w_ps = ps("w_ps", [P, QUADS, 4, P])
        step, shifted = core.semaphore("gate_step"), core.semaphore("gates_shifted")
        expd, ready = core.semaphore("gates_exp"), core.semaphore("slots_ready")
        turned, major = core.semaphore("slots_turned"), core.semaphore("slots_major")
        rows = core.semaphore("one_hot_rows")
        outer, staged, stored = core.semaphore("outer_done"), core.semaphore("w_staged"), core.semaphore("w_stored")
        n_steps = [0]
        rounds = P // ROUND

        def tile_rounds(eng, u, body):
            if u == 0:
                body(0)
            with eng.Fori(1 if u == 0 else 0, rounds) as r:
                body(r)

        with nc.Block() as block:

            @block.vector
            def _(dve):
                def linked(ins):
                    n_steps[0] += 1
                    ins.then_inc(step, 1)
                    dve.wait_ge(step, n_steps[0])

                def decode(u):
                    full = [P, HEADS, TOPK, TOPK]
                    dve.tensor_tensor(gate[:, :, :], best[:, u], best[:, u, :, 0:1].broadcast_to([P, HEADS, TOPK]),
                                      ALU.subtract).then_inc(shifted, 1)
                    dve.tensor_copy(key_f[:, :, :], top_i[:, u])
                    dve.tensor_scalar(rank_u[:, 0], best_i[:, u], 4, None, ALU.logical_shift_right)
                    linked(dve.tensor_scalar(rank_u[:, 1], best_i[:, u], TOPK - 1, None, ALU.bitwise_and))
                    linked(dve.tensor_copy(rank[:, :, :, :], rank_u[:, :, :, :]))
                    iota16 = core.iota[:, 0:TOPK].unsqueeze(1).unsqueeze(1).broadcast_to(full)
                    keys = key_f[:, :, :].rearrange("p (h s) k -> p s h k", s=2)
                    for s in range(2):
                        last = dve.tensor_tensor(hot[:, s], rank[:, s].unsqueeze(3).broadcast_to(full), iota16, ALU.is_equal)
                    linked(last)
                    for s in range(2):
                        last = dve.tensor_tensor(hot[:, s], hot[:, s], keys[:, s].unsqueeze(2).broadcast_to(full), ALU.mult)
                    linked(last)
                    for s in range(2):
                        dve.tensor_reduce(slot_key[:, s], hot[:, s].rearrange("p h k r -> p (h k) r"), AX.X, ALU.add)
                    dve.wait_ge(expd, u + 1)
                    linked(dve.tensor_reduce(sums[:, :], gate[:, :, :], AX.X, ALU.add))
                    linked(dve.reciprocal(inv[:, :], sums[:, :]))
                    dve.tensor_tensor(gate[:, :, :], gate[:, :, :], inv[:, :].unsqueeze(2).broadcast_to([P, HEADS, TOPK]),
                                      ALU.mult).then_inc(ready, 1)
                    dve.wait_ge(turned, u + 1)
                    dve.tensor_copy(slot_major[:, :, u], t_ps[:, 0:3 * P].rearrange("p (k t) -> p k t", k=3)).then_inc(major, 1)
                    dve.wait_ge(major, u + 1)

                for u in range(TT):
                    decode(u)

                    def round_(r):
                        for x in range(QUADS):
                            if due(rounds * u + r):
                                dve.wait_ge(outer, (u * rounds + r) * QUADS + (x + 1 - QUADS))
                            for k in range(4 * x, 4 * x + 4):
                                t = r * ROUND + k
                                dve.tensor_scalar(first[:, k], core.iota, slot_major[:, 0, u, bass.ds(t, 1)],
                                                  slot_major[:, 2, u, bass.ds(t, 1)], ALU.is_equal, ALU.mult)
                            keys = slot_major[:, 1, u, bass.ds(r * ROUND + 4 * x, 4)].unsqueeze(2).broadcast_to([P, 4, N_KEYS])
                            iota4 = core.iota.unsqueeze(1).broadcast_to([P, 4, N_KEYS])
                            dve.tensor_tensor(second[:, 4 * x:4 * x + 4], keys, iota4, ALU.is_equal).then_inc(rows, 1)

                    tile_rounds(dve, u, round_)

            @block.tensor
            def _(pe):
                for u in range(TT):
                    pe.wait_ge(ready, u + 1)
                    pe.transpose(t_ps[:, 0:P], slot_key[:, 0], core.ident)
                    pe.transpose(t_ps[:, P:2 * P], slot_key[:, 1], core.ident)
                    pe.transpose(t_ps[:, 2 * P:3 * P], gate[:, :, :].rearrange("p h k -> p (h k)"), core.ident).then_inc(turned, 1)

                    def round_(r):
                        for x in range(QUADS):
                            n = (u * rounds + r) * QUADS
                            pe.wait_ge(rows, n + (x + 1))
                            if due(rounds * u + r):
                                pe.wait_ge(staged, n + (x + 1 - QUADS))
                            for k in range(4):
                                mm = pe.matmul(w_ps[:, x, k], first[:, 4 * x + k], second[:, 4 * x + k], start=True, stop=True)
                            mm.then_inc(outer, 1)

                    tile_rounds(pe, u, round_)

            @block.scalar
            def _(act):
                for u in range(TT):
                    act.wait_ge(shifted, u + 1)
                    act.activation(gate[:, :, :], gate[:, :, :], ACT.Exp).then_inc(expd, 1)
                    if u:
                        act.wait_ge(stored, 16 * u)
                    with act.Fori(0, rounds) as r:
                        for x in range(QUADS):
                            act.wait_ge(outer, (u * rounds + r) * QUADS + (x + 1))
                            act.activation(stage[:, :, bass.ds(r * ROUND + 4 * x, 4)], w_ps[:, x].rearrange("p t i -> p i t"),
                                           ACT.Copy).then_inc(staged, 1)

            @block.sync
            def _(sp):
                for to, source, arrived in ahead:
                    sp.dma_start(to, source).then_inc(arrived, 16)
                sp.wait_ge(staged, QUADS * rounds)
                sp.dma_start(dram["gates"].rearrange("j i t -> i j t"), stage[:, :, :]).then_inc(stored, 16)
                sp.wait_ge(stored, 16)


def experts(core, layer, stream, dram, stage, u_raw, v_raw, u_in, v_in):
    nc = core.nc
    tag = f"ex{layer}{stream}"
    with ExitStack() as scope:
        sb = core.sbuf(scope, tag)
        ps = core.psum(scope, tag)
        h_hi, h_lo = sb("h_hi", [P, DC, T], F32R), sb("h_lo", [P, DC, T], F32R)
        w_raw = sb("w_raw", [P, 2, 2, P])
        u_hi, u_lo = sb("u_hi", [P, 2, D], F32R), sb("u_lo", [P, 2, D], F32R)
        v_hi, v_lo = sb("v_hi", [P, 2, D], F32R), sb("v_lo", [P, 2, D], F32R)
        gel, prod = sb("gel", [P, 2, T]), sb("prod", [P, 2, T])
        p_hi, p_lo = sb("p_hi", [P, 2, T], F32R), sb("p_lo", [P, 2, T], F32R)
        y_sb = sb("y_sb", [P, TT, D])
        a_ps = ps("a_ps", [P, 2, 512])
        y_ps = ps("y_ps", [P, TT, 2, 512])
        t_ps = ps("t_ps", [P, 2, 512])
        w_in = [core.semaphore(f"w_in{r}") for r in range(2)]
        h_hi_done, h_split = core.semaphore("h_hi_done"), core.semaphore("h_split")
        u_hi_done, v_hi_done = core.semaphore("u_hi_done"), core.semaphore("v_hi_done")
        u_split, v_split = core.semaphore("u_split"), core.semaphore("v_split")
        scored, gelud, gated = core.semaphore("scored"), core.semaphore("gelud"), core.semaphore("gated")
        p_hi_done, p_split, summed = core.semaphore("p_hi_done"), core.semaphore("p_split"), core.semaphore("summed")
        y_out, y_turned, added = core.semaphore("y_out"), core.semaphore("y_turned"), core.semaphore("added")
        pairs = N_KEYS // 2
        cols = slice(stream * T, (stream + 1) * T)

        def quads(eng, body):
            for n in range(4):
                body(0, n // 2, n % 2)
            with eng.Fori(1, pairs // 2) as q:
                for n in range(4):
                    body(q, n // 2, n % 2)

        with nc.Block() as block:

            @block.sync
            def _(sp):
                def load(q, r):
                    m = 2 * q + r
                    sp.wait_ge(u_split, 2 * m - 2)
                    sp.dma_start(u_raw[:, r], dram["u"][layer, bass.ds(m, 1)].rearrange("o p b n -> p (o b) n")).then_inc(u_in[r], 16)
                    sp.wait_ge(v_split, 2 * m - 2)
                    sp.dma_start(v_raw[:, r], dram["v"][layer, bass.ds(m, 1)].rearrange("o p b n -> p (o b) n")).then_inc(v_in[r], 16)
                    sp.wait_ge(gated, 2 * m - 2)
                    sp.dma_start(w_raw[:, r], dram["gates"][bass.ds(2 * m, 2)].rearrange("b i t -> i b t")).then_inc(w_in[r], 16)

                for r in range(2):
                    sp.dma_start(w_raw[:, r], dram["gates"][2 * r:2 * r + 2].rearrange("b i t -> i b t")).then_inc(w_in[r], 16)
                with sp.Fori(1, pairs // 2) as q:
                    load(q, 0)
                    load(q, 1)

            @block.scalar
            def _(act):
                act.activation(h_hi[:, :, :], core.h[:, :, 0:T], ACT.Copy).then_inc(h_hi_done, 1)

                def body(q, r, b):
                    i = 4 * q + (2 * r + b)
                    act.wait_ge(u_in[r], 16 * q + 16)
                    if due(i - 1):
                        act.wait_ge(scored, i - 1)
                    act.activation(u_hi[:, b], u_raw[:, r, b], ACT.Copy).then_inc(u_hi_done, 1)
                    if not (isinstance(i, int) and i < 1):
                        gelu_and_high(i - 1, 1 - b)
                    act.wait_ge(v_in[r], 16 * q + 16)
                    if due(i - 1):
                        act.wait_ge(summed, i - 1)
                    act.activation(v_hi[:, b], v_raw[:, r, b], ACT.Copy).then_inc(v_hi_done, 1)

                def gelu_and_high(i, b):
                    act.wait_ge(scored, i + 1)
                    if due(i - 1):
                        act.wait_ge(gated, i - 1)
                    act.activation(gel[:, b], a_ps[:, b, 0:T], ACT.Gelu).then_inc(gelud, 1)
                    act.wait_ge(gated, i + 1)
                    if due(i - 1):
                        act.wait_ge(summed, i - 1)
                    act.activation(p_hi[:, b], prod[:, b], ACT.Copy).then_inc(p_hi_done, 1)

                quads(act, body)
                gelu_and_high(N_KEYS - 1, 1)
                for u in range(TT):
                    for k in range(2):
                        act.wait_ge(summed, N_KEYS)
                        act.activation(y_sb[:, u, k * 512:(k + 1) * 512], y_ps[:, u, k], ACT.Copy).then_inc(y_out, 1)

            @block.vector
            def _(dve):
                dve.wait_ge(h_hi_done, 1)
                dve.tensor_tensor(h_lo[:, :, :], core.h[:, :, 0:T], h_hi[:, :, :].bitcast(F32), ALU.subtract).then_inc(h_split, 1)

                def body(q, r, b):
                    i = 4 * q + (2 * r + b)
                    dve.wait_ge(u_hi_done, i + 1)
                    if due(i - 1):
                        dve.wait_ge(scored, i - 1)
                    dve.tensor_tensor(u_lo[:, b], u_raw[:, r, b], u_hi[:, b].bitcast(F32), ALU.subtract).then_inc(u_split, 1)
                    if not (isinstance(i, int) and i < 1):
                        gate(i - 1, 1 - b, r if b else 1 - r, q if b or r else q - 1)
                    dve.wait_ge(v_hi_done, i + 1)
                    if due(i - 1):
                        dve.wait_ge(summed, i - 1)
                    dve.tensor_tensor(v_lo[:, b], v_raw[:, r, b], v_hi[:, b].bitcast(F32), ALU.subtract).then_inc(v_split, 1)

                def gate(i, b, r, q):
                    dve.wait_ge(gelud, i + 1)
                    dve.wait_ge(w_in[r], 16 * q + 16)
                    if due(i - 1):
                        dve.wait_ge(p_split, i - 1)
                    dve.tensor_tensor(prod[:, b, 0:P], gel[:, b, 0:P], w_raw[:, r, b], ALU.mult)
                    w_late = stage[:, i] if isinstance(i, int) else stage[:, bass.ds(i, 1)].rearrange("p o t -> p (o t)")
                    dve.tensor_tensor(prod[:, b, P:T], gel[:, b, P:T], w_late, ALU.mult).then_inc(gated, 1)
                    dve.wait_ge(p_hi_done, i + 1)
                    if due(i - 1):
                        dve.wait_ge(summed, i - 1)
                    dve.tensor_tensor(p_lo[:, b], prod[:, b], p_hi[:, b].bitcast(F32), ALU.subtract).then_inc(p_split, 1)

                quads(dve, body)
                gate(N_KEYS - 1, 1, 1, pairs // 2 - 1)
                for c in range(DC):
                    dve.wait_ge(y_turned, c + 1)
                    dve.scalar_tensor_tensor(core.x[:, c, cols], t_ps[:, c % 2, 0:T], core.mod[:, 5 * DC + c, stream:stream + 1],
                                             core.x[:, c, cols], ALU.mult, ALU.add).then_inc(added, 1)

            @block.tensor
            def _(pe):
                pe.wait_ge(h_split, 1)

                def score(i, b):
                    pe.wait_ge(u_split, i + 1)
                    if due(i - 1):
                        pe.wait_ge(gelud, i - 1)
                    n = 0
                    for lhs, rhs in ((u_hi, h_hi), (u_hi, h_lo), (u_lo, h_hi)):
                        for c in range(DC):
                            mm = pe.matmul(a_ps[:, b, 0:T], lhs[:, b, c * P:(c + 1) * P], rhs[:, c, :],
                                           start=(n == 0), stop=(n == 3 * DC - 1))
                            n += 1
                    mm.then_inc(scored, 1)

                def project(i, b, first, last):
                    pe.wait_ge(p_split, i + 1)
                    pe.wait_ge(v_split, i + 1)
                    for u in range(TT):
                        for n, (lhs, rhs) in enumerate(((p_hi, v_hi), (p_hi, v_lo), (p_lo, v_hi))):
                            for k in range(2):
                                mm = pe.matmul(y_ps[:, u, k], lhs[:, b, u * P:(u + 1) * P], rhs[:, b, k * 512:(k + 1) * 512],
                                               start=(first and n == 0), stop=(last and n == 2), skip_group_check=True)
                    mm.then_inc(summed, 1)

                def body(q, r, b):
                    i = 4 * q + (2 * r + b)
                    score(i, b)
                    if not (isinstance(i, int) and i < 1):
                        project(i - 1, 1 - b, isinstance(i, int) and i == 1, False)

                quads(pe, body)
                project(N_KEYS - 1, 1, False, True)
                pe.wait_ge(y_out, 2 * TT)
                for c in range(DC):
                    if due(c - 1):
                        pe.wait_ge(added, c - 1)
                    for u in range(TT):
                        mm = pe.transpose(t_ps[:, c % 2, u * P:(u + 1) * P], y_sb[:, u, c * P:(c + 1) * P], core.ident)
                    mm.then_inc(y_turned, 1)
def constants():
    i, j = np.arange(P)[None, :], np.arange(P)[:, None]
    same = i // HD == j // HD
    tri = np.stack([same & (j <= i), same & (j >= i)], 1)
    neg = np.where(tri, 0.0, MASKED)
    cross = np.stack([same & (j // BLK == i // BLK - 1), same & (j // BLK == i // BLK + 1)], 1)
    mix = np.concatenate([same, tri.reshape(P, -1), neg.reshape(P, -1), cross.reshape(P, -1), i // BLK == j // BLK], 1)
    base = np.concatenate([np.eye(P), np.ones((P, P)), np.broadcast_to(np.arange(P), (P, P))], 1)
    t = np.arange(T)
    band = np.zeros((T, 4, T))
    for g, w in enumerate(POOL_WINDOWS):
        lo, hi = np.clip(t - w // 2, 0, T), np.clip(t + w - w // 2, 0, T)
        inside = (t[:, None] >= lo[None]) & (t[:, None] < hi[None])
        band[:, g] = inside / (hi - lo)[None] - np.eye(T)
    band = band.reshape(TT, P, 4, T).transpose(1, 2, 0, 3)
    amask = np.zeros((T, 2 * T))
    amask[:, :T] = np.where(np.abs(t[:, None] - t[None]) <= WINDOW, 0.0, MASKED)
    amask = amask.reshape(TT, P, 2 * T).transpose(1, 0, 2)
    f32 = np.float32
    pos = np.stack([t // GRID_W, t % GRID_W], -1).astype(f32)
    inv = np.power(f32(ROPE_BASE), -np.arange(ROPE_PAIRS, dtype=f32) / f32(ROPE_PAIRS))
    ang = pos[:, :, None] * inv
    rope = np.stack([np.cos(ang), np.sin(ang)]).reshape(2, TT, P, 2, ROPE_PAIRS).transpose(2, 0, 1, 3, 4)
    found = {"base_consts": base, "mix_consts": mix, "band": band, "amask": amask, "rope": rope}
    return {k: np.ascontiguousarray(v, dtype=f32) for k, v in found.items()}


def layout(a):
    n = a["w_in"].shape[0]
    cols = lambda v: v.reshape(*v.shape[:-1], DC, P)
    r = {}
    r["x_t"] = np.concatenate([a["x"][0], a["ctx"][0]], 0).T.reshape(DC, P, 2 * T).transpose(1, 0, 2)
    r["c2"] = np.stack([a["c"][0], a["c_ctx"]], -1).reshape(DC, P, 2).transpose(1, 0, 2)
    r["w_ada"] = a["w_ada"].reshape(n, DC, P, 12, 512).transpose(0, 3, 2, 1, 4)
    r["b_ada"] = a["b_ada"].reshape(n, 6 * DC, P).transpose(0, 2, 1)
    r["norms"] = np.stack([cols(a["norm1"]), cols(a["norm2"])], 1).transpose(0, 3, 1, 2)
    r["norm_f"] = cols(a["norm_f"]).T
    q0, q1 = POOL_W, POOL_W + 3 * GDN_W
    r["w_qkv"] = a["w_in"][:, :, q0:q1].reshape(n, DC, P, QKV_C, P).transpose(0, 3, 2, 1, 4)
    r["w_tok"] = np.concatenate([a["w_in"][:, :, :q0], a["w_in"][:, :, q1:]], 2).reshape(n, DC, P, TOK_W).transpose(0, 2, 1, 3)
    r["conv_w"] = a["conv_w"].reshape(n, CONV_K, QKV_C, P).transpose(0, 3, 2, 1)
    r["a_log"] = a["a_log"].reshape(n, 2 * GH)
    r["dt_bias"] = a["dt_bias"].reshape(n, 2 * GH)
    r["gdn_norm"], r["pool_scale"], r["sink"] = a["gdn_norm"], a["pool_scale"], a["sink"]
    r["w_pool"] = a["w_pool"].transpose(0, 2, 1, 3)
    r["w_out"] = a["w_out"].reshape(n, DC, P, DC, P).transpose(0, 3, 2, 1, 4)
    r["wq"] = a["peer_wq"].reshape(n, DC, P, GROUPS, P).transpose(0, 3, 2, 1, 4)
    r["keys"] = a["peer_keys"].reshape(n, GROUPS, N_KEYS, P).transpose(0, 3, 1, 2)
    u = a["peer_u"].reshape(n, N_KEYS, N_KEYS // 2, 2, DC, P)
    r["u"] = u.transpose(0, 2, 5, 3, 4, 1).reshape(n, N_KEYS // 2, P, 2, D)
    r["v"] = a["peer_v"].reshape(n, N_KEYS, N_KEYS // 2, 2, D).transpose(0, 2, 1, 3, 4)
    return {k: np.ascontiguousarray(v) for k, v in r.items()}


def hybrid_backbone(nc, depth, dram, out):
    dram = dict(dram)
    dram["gates"] = nc.dram_tensor("peer_gates", [N_KEYS, N_KEYS, P], F32, kind="Internal").ap()
    with ExitStack() as scope:
        core = Core(nc)
        sb = core.sbuf(scope, "core")
        core.x = sb("x", [P, DC, 2 * T])
        core.cc = sb("cc", [P, DC, 2])
        core.mod = sb("mod", [P, 6 * DC, 2])
        core.gain = sb("gain", [P, 2, DC, 2])
        base = sb("base", [P, 3 * P])
        last_gain = sb("norm_f", [P, DC])
        core.ident, core.ones, core.iota = base[:, 0:P], base[:, P:2 * P], base[:, 2 * P:3 * P]
        ahead = [(base[:, :], dram["base_consts"]), (last_gain[:, :], dram["norm_f"]), (core.x[:, :, :], dram["x_t"])]
        modulation(core, dram, ahead)
        core.end_stage()
        for layer in range(depth):
            need_ctx = layer < depth - 1
            mixing(core, layer, need_ctx, dram)
            core.end_stage()
            for stream in range(2 if need_ctx else 1):
                cols = slice(stream * T, (stream + 1) * T)
                with ExitStack() as hs:
                    core.h = core.sbuf(hs, f"pe{layer}{stream}")("h", [P, DC, T])
                    parts = [(slice(0, T), [core.mod[:, 3 * DC + c, stream:stream + 1] for c in range(DC)],
                              [core.gain[:, 1, c, stream:stream + 1] for c in range(DC)])]
                    tag = f"pr{layer}{stream}"
                    with ExitStack() as ss:
                        stage = core.sbuf(ss, tag)("stage", [P, N_KEYS, P])
                        raw = core.sbuf(ss, tag)
                        u_raw, v_raw = raw("u_raw", [P, 2, 2, D]), raw("v_raw", [P, 2, 2, D])
                        with ExitStack() as ts:
                            sb = core.sbuf(ts, tag)
                            top, top_i = sb("top", [P, TT, GROUPS, TOPK]), sb("top_i", [P, TT, GROUPS, TOPK], U32)
                            best, best_i = sb("best", [P, TT, HEADS, TOPK]), sb("best_i", [P, TT, HEADS, TOPK], U32)
                            with ExitStack() as ws:
                                sb = core.sbuf(ws, tag)
                                keys, wq = sb("keys", [P, GROUPS, N_KEYS]), sb("wq", [P, WQ_RING, DC, P])
                                keys_in = core.semaphore("peer_keys_in")
                                wq_in = [core.semaphore(f"wq_in{r}") for r in range(WQ_RING)]
                                ahead = [(wq[:, r], dram["wq"][layer, r], wq_in[r]) for r in range(WQ_RING)]
                                ahead.append((keys[:, :, :], dram["keys"][layer], keys_in))
                                with nc.Block() as block:
                                    h_done = normalize(core, ws, block, f"pn{layer}{stream}", cols, parts, ahead)
                                    topk(core, ws, block, tag, dram, layer, keys, wq, keys_in, wq_in, h_done, top, top_i, best, best_i)
                            core.end_stage()
                            u_in = [core.semaphore(f"u_in{r}") for r in range(2)]
                            v_in = [core.semaphore(f"v_in{r}") for r in range(2)]
                            ahead = [(to[:, r], dram[name][layer, r], arrived[r]) for r in range(2)
                                     for to, name, arrived in ((u_raw, "u", u_in), (v_raw, "v", v_in))]
                            gate_matrix(core, tag, dram, top_i, best, best_i, stage, ahead)
                        experts(core, layer, stream, dram, stage, u_raw, v_raw, u_in, v_in)
                        core.end_stage()
        with ExitStack() as hs:
            core.h = core.sbuf(hs, "final")("h", [P, DC, T])
            stored = core.semaphore("stored")
            with nc.Block() as block:
                parts = [(slice(0, T), None, [last_gain[:, c:c + 1] for c in range(DC)])]
                h_done = normalize(core, hs, block, "fn", slice(0, T), parts)

                @block.sync
                def _(sp):
                    sp.wait_ge(h_done, DC)
                    sp.dma_start(out, core.h[:, :, :]).then_inc(stored, 16)
                    sp.wait_ge(stored, 16)


def kernel(**inputs):
    import concourse.bacc as bacc
    from concourse.bass_utils import run_bass_kernel_spmd

    arrays = layout({k: np.asarray(v) for k, v in inputs.items()})
    arrays.update(constants())
    nc = bacc.Bacc("TRN2", target_bir_lowering=False, num_devices=1)
    dram = {k: nc.dram_tensor(f"in_{k}", v.shape, mybir.dt.from_np(v.dtype), kind="ExternalInput").ap()
            for k, v in arrays.items()}
    out = nc.dram_tensor("out_t", [P, DC, T], F32, kind="ExternalOutput").ap()
    hybrid_backbone(nc, inputs["w_in"].shape[0], dram, out)
    r = run_bass_kernel_spmd(nc, [{f"in_{k}": v for k, v in arrays.items()}], core_ids=[0])
    y = np.asarray(r.results[0]["out_t"])
    return np.ascontiguousarray(y.transpose(2, 1, 0).reshape(1, T, D))
```
